# Optimizing a Trainium2 kernel written in Bass

```python
import jax, jax.numpy as jnp
from jax import lax
import numpy as np
import math

D_MODEL = 1024
BATCH = 1
SEQ = 1024
DEPTH = 2

N_META = 16
N_MIXERS = 2
N_CONV_LAYERS = (DEPTH + 1) // 2
N_GLA_LAYERS = DEPTH // 2
DN_ALPHA = (2 * DEPTH) ** 0.25
DN_BETA = (8 * DEPTH) ** -0.25
LN_EPS = 1e-5
RMS_EPS = 1e-6
CONV_CH = D_MODEL
CONV_TAPS = 31
CONV_IN = 3 * CONV_CH
GLA_HEADS = 4
GLA_DK = D_MODEL // 2
GLA_DV = D_MODEL
GLA_HK = GLA_DK // GLA_HEADS
GLA_HV = GLA_DV // GLA_HEADS
GLA_GATE_RANK = 16
GLA_TAU = 16.0
GLA_CHUNK = 64
GLA_IN = 2 * GLA_DK + 2 * GLA_DV + GLA_GATE_RANK


def layer_norm(x, g, b):
    xf = x.astype(jnp.float32)
    mu = jnp.mean(xf, axis=-1, keepdims=True)
    xc = xf - mu
    var = jnp.mean(xc * xc, axis=-1, keepdims=True)
    y = xc * lax.rsqrt(var + LN_EPS) * g.astype(jnp.float32) + b.astype(jnp.float32)
    return y.astype(x.dtype)

def conformer_mixer(h, w_in, b_in, w_dw, b_dw, norm_g, norm_b, w_out, b_out):
    u = h @ w_in + b_in
    a, ga, z = jnp.split(u, 3, axis=-1)
    glu = a * jax.nn.sigmoid(ga)
    c = lax.conv_general_dilated(
        glu, w_dw[:, None, :].astype(glu.dtype), window_strides=(1,),
        padding=[(CONV_TAPS - 1, 0)], dimension_numbers=('NWC', 'WIO', 'NWC'),
        feature_group_count=CONV_CH) + b_dw
    c = jax.nn.silu(layer_norm(c, norm_g, norm_b))
    return (c * jax.nn.silu(z)) @ w_out + b_out

def _gla_chunk_step(S, inp):
    qc, kc, vc, gc = inp
    bc = jnp.cumsum(gc, axis=1)
    o_inter = jnp.einsum('bthd,bhde->bthe', qc * jnp.exp(bc), S)
    causal = jnp.tril(jnp.ones((GLA_CHUNK, GLA_CHUNK), dtype=bool))
    diff = bc[:, :, None] - bc[:, None, :]
    decay = jnp.exp(jnp.where(causal[None, :, :, None, None], diff, -jnp.inf))
    att = jnp.einsum('bthd,bshd,btshd->bhts', qc, kc, decay)
    o_intra = jnp.einsum('bhts,bshe->bthe', att, vc)
    b_last = bc[:, -1]
    S_new = jnp.exp(b_last)[..., None] * S + jnp.einsum(
        'bshd,bshe->bhde', kc * jnp.exp(b_last[:, None] - bc), vc)
    return S_new, o_inter + o_intra

def gla_mixer(h, w_in, w_a2, b_a, norm_g, w_out):
    B, L, _ = h.shape
    u = h @ w_in
    q, k, v, r, a1 = jnp.split(
        u, [GLA_DK, 2 * GLA_DK, 2 * GLA_DK + GLA_DV, 2 * GLA_DK + 2 * GLA_DV], axis=-1)
    glog = jax.nn.log_sigmoid((a1 @ w_a2 + b_a).astype(jnp.float32)) / GLA_TAU
    pad = GLA_CHUNK - N_META
    n_chunks = (L + pad) // GLA_CHUNK

    def prep(t, hd):
        t = jnp.pad(t.astype(jnp.float32), ((0, 0), (pad, 0), (0, 0)))
        return t.reshape(B, n_chunks, GLA_CHUNK, GLA_HEADS, hd).transpose(1, 0, 2, 3, 4)

    qs = prep(q, GLA_HK) * (GLA_HK ** -0.5)
    ks = prep(k, GLA_HK)
    vs = prep(v, GLA_HV)
    gs = prep(glog, GLA_HK)
    S0 = jnp.zeros((B, GLA_HEADS, GLA_HK, GLA_HV), jnp.float32)
    _, o = lax.scan(_gla_chunk_step, S0, (qs, ks, vs, gs))
    o = o.transpose(1, 0, 2, 3, 4).reshape(B, n_chunks * GLA_CHUNK, GLA_HEADS, GLA_HV)[:, pad:]
    o = o * lax.rsqrt(jnp.mean(o * o, axis=-1, keepdims=True) + RMS_EPS) * norm_g.astype(jnp.float32)
    o = o.reshape(B, L, GLA_DV).astype(h.dtype)
    return (o * jax.nn.silu(r)) @ w_out

def first_inputs(seed: int = 0) -> dict:
    key = jax.random.key(seed)
    ks = jax.random.split(key, 20)
    nrm = jax.random.normal
    f32 = jnp.float32
    Lc, Lg = N_CONV_LAYERS, N_GLA_LAYERS
    return {
        "x": nrm(ks[0], (BATCH, SEQ, D_MODEL), f32),
        "meta": nrm(ks[1], (N_META, D_MODEL), f32),
        "conv_w_in": nrm(ks[2], (Lc, D_MODEL, CONV_IN), f32) * D_MODEL ** -0.5,
        "conv_b_in": nrm(ks[3], (Lc, CONV_IN), f32) * 0.02,
        "conv_w_dw": nrm(ks[4], (Lc, CONV_TAPS, CONV_CH), f32) * CONV_TAPS ** -0.5,
        "conv_b_dw": nrm(ks[5], (Lc, CONV_CH), f32) * 0.02,
        "conv_norm_g": 1.0 + 0.02 * nrm(ks[6], (Lc, CONV_CH), f32),
        "conv_norm_b": nrm(ks[7], (Lc, CONV_CH), f32) * 0.02,
        "conv_w_out": nrm(ks[8], (Lc, CONV_CH, D_MODEL), f32) * (CONV_CH ** -0.5 * DN_BETA),
        "conv_b_out": nrm(ks[9], (Lc, D_MODEL), f32) * 0.02,
        "gla_w_in": nrm(ks[10], (Lg, D_MODEL, GLA_IN), f32) * D_MODEL ** -0.5,
        "gla_w_a2": nrm(ks[11], (Lg, GLA_GATE_RANK, GLA_DK), f32) * GLA_GATE_RANK ** -0.5,
        "gla_b_a": nrm(ks[12], (Lg, GLA_DK), f32) * 0.02,
        "gla_norm_g": 1.0 + 0.02 * nrm(ks[13], (Lg, GLA_HV), f32),
        "gla_w_out": nrm(ks[14], (Lg, GLA_DV, D_MODEL), f32) * (GLA_DV ** -0.5 * DN_BETA),
        "post_ln_g": 1.0 + 0.02 * nrm(ks[15], (DEPTH, D_MODEL), f32),
        "post_ln_b": nrm(ks[16], (DEPTH, D_MODEL), f32) * 0.02,
    }

def first_block(x, meta, conv_w_in, conv_b_in, conv_w_dw, conv_b_dw, conv_norm_g, conv_norm_b,
              conv_w_out, conv_b_out, gla_w_in, gla_w_a2, gla_b_a, gla_norm_g, gla_w_out,
              post_ln_g, post_ln_b):
    B = x.shape[0]
    h = jnp.concatenate(
        [jnp.broadcast_to(meta[None].astype(x.dtype), (B, N_META, D_MODEL)), x], axis=1)
    for i in range(DEPTH):
        j = i // N_MIXERS
        if i % N_MIXERS == 0:
            y = conformer_mixer(h, conv_w_in[j], conv_b_in[j], conv_w_dw[j], conv_b_dw[j],
                                conv_norm_g[j], conv_norm_b[j], conv_w_out[j], conv_b_out[j])
        else:
            y = gla_mixer(h, gla_w_in[j], gla_w_a2[j], gla_b_a[j], gla_norm_g[j], gla_w_out[j])
        h = layer_norm(DN_ALPHA * h + y, post_ln_g[i], post_ln_b[i])
    return h[:, N_META:]


DEPTH_2 = 1

D_PLE = 256
D_MIX = D_MODEL
ATTN_HEADS = 8
HEAD_DIM = 64
D_ATTN = ATTN_HEADS * HEAD_DIM
POOL_WINDOWS = (2, 4, 8, 16)
POOL_GROUPS = len(POOL_WINDOWS)
D_POOL = D_MIX - D_ATTN
POOL_CH = D_POOL // POOL_GROUPS
D_IN = 3 * D_ATTN + ATTN_HEADS + D_POOL
D_FF = int(math.ceil(8 * D_MODEL / 3 / 256) * 256)
Q_BLOCK = 128


def rms_norm(x, g):
    xf = x.astype(jnp.float32)
    y = xf * lax.rsqrt(jnp.mean(xf * xf, axis=-1, keepdims=True) + RMS_EPS)
    return (y * g.astype(jnp.float32)).astype(x.dtype)

def forgetting_attention(q, k, v, log_f):
    b, s, h, dh = q.shape
    scale = 1.0 / math.sqrt(dh)
    c = jnp.cumsum(log_f, axis=1).transpose(0, 2, 1)
    nb = s // Q_BLOCK
    qb = q.reshape(b, nb, Q_BLOCK, h, dh).transpose(1, 0, 2, 3, 4)
    cb = c.reshape(b, h, nb, Q_BLOCK).transpose(2, 0, 1, 3)
    starts = jnp.arange(nb, dtype=jnp.int32) * Q_BLOCK
    kpos = jnp.arange(s, dtype=jnp.int32)

    def one_block(args):
        q_i, c_i, s0 = args
        scores = jnp.einsum('bqhd,bkhd->bhqk', q_i, k).astype(jnp.float32) * scale
        scores = scores + c_i[:, :, :, None] - c[:, :, None, :]
        qpos = s0 + jnp.arange(Q_BLOCK, dtype=jnp.int32)
        causal = kpos[None, :] <= qpos[:, None]
        scores = jnp.where(causal, scores, -jnp.inf)
        probs = jax.nn.softmax(scores, axis=-1).astype(v.dtype)
        return jnp.einsum('bhqk,bkhd->bqhd', probs, v)

    out = lax.map(one_block, (qb, cb, starts))
    return out.transpose(1, 0, 2, 3, 4).reshape(b, s, h * dh)

def multiscale_pool(u, w_pool, pool_scale):
    b, s, _ = u.shape
    uf = u.astype(jnp.float32)
    cs = jnp.cumsum(uf, axis=1)
    pos = jnp.arange(s, dtype=jnp.int32)
    outs = []
    for g, w in enumerate(POOL_WINDOWS):
        lo, hi = g * POOL_CH, (g + 1) * POOL_CH
        cs_g = cs[:, :, lo:hi]
        cs_shift = jnp.pad(cs_g, ((0, 0), (w, 0), (0, 0)))[:, :s]
        count = jnp.minimum(pos + 1, w).astype(jnp.float32)[None, :, None]
        outs.append((cs_g - cs_shift) / count - uf[:, :, lo:hi])
    y = jnp.stack(outs, axis=2).astype(u.dtype)
    y = jnp.einsum('bsgc,gcd->bsgd', y, w_pool).reshape(b, s, D_POOL)
    return y * pool_scale

def second_inputs(seed: int = 0) -> dict:
    key = jax.random.key(seed)
    ks = jax.random.split(key, 24)
    f32 = jnp.float32

    def nrm(k, shape, fan_in):
        return jax.random.normal(k, shape, f32) * (fan_in ** -0.5)

    def gain(k, shape):
        return 1.0 + 0.05 * jax.random.normal(k, shape, f32)

    return {
        "x": jax.random.normal(ks[0], (BATCH, SEQ, D_MODEL), f32),
        "p": jax.random.normal(ks[1], (DEPTH_2, BATCH, SEQ, D_PLE), f32),
        "g_mix_pre": gain(ks[2], (DEPTH_2, D_MODEL)),
        "w_in": nrm(ks[3], (DEPTH_2, D_MODEL, D_IN), D_MODEL),
        "b_forget": jax.random.uniform(ks[4], (DEPTH_2, ATTN_HEADS), f32, 1.0, 4.0),
        "g_attn_grp": gain(ks[5], (DEPTH_2, D_ATTN)),
        "g_pool_grp": gain(ks[6], (DEPTH_2, D_POOL)),
        "w_pool": nrm(ks[7], (DEPTH_2, POOL_GROUPS, POOL_CH, POOL_CH), POOL_CH),
        "pool_scale": 1.0 + 0.1 * jax.random.normal(ks[8], (DEPTH_2, D_POOL), f32),
        "w_out": nrm(ks[9], (DEPTH_2, D_MIX, D_MODEL), D_MIX),
        "g_mix_post": gain(ks[10], (DEPTH_2, D_MODEL)),
        "g_ffn_pre": gain(ks[11], (DEPTH_2, D_MODEL)),
        "w_ffn_gate": nrm(ks[12], (DEPTH_2, D_MODEL, D_FF), D_MODEL),
        "w_ffn_up": nrm(ks[13], (DEPTH_2, D_MODEL, D_FF), D_MODEL),
        "w_ffn_down": nrm(ks[14], (DEPTH_2, D_FF, D_MODEL), D_FF),
        "g_ffn_post": gain(ks[15], (DEPTH_2, D_MODEL)),
        "w_ple_proj": nrm(ks[16], (DEPTH_2, D_PLE, D_MODEL), D_PLE),
        "g_ple": gain(ks[17], (DEPTH_2, D_MODEL)),
        "w_ple_gate": nrm(ks[18], (DEPTH_2, D_MODEL, D_MODEL), D_MODEL),
    }

def second_block(x, p, g_mix_pre, w_in, b_forget, g_attn_grp, g_pool_grp, w_pool, pool_scale,
              w_out, g_mix_post, g_ffn_pre, w_ffn_gate, w_ffn_up, w_ffn_down, g_ffn_post,
              w_ple_proj, g_ple, w_ple_gate):
    b, s, _ = x.shape
    h = x
    for i in range(DEPTH_2):
        hn = rms_norm(h, g_mix_pre[i])
        z = hn @ w_in[i]
        o = 0
        q = z[..., o:o + D_ATTN].reshape(b, s, ATTN_HEADS, HEAD_DIM); o += D_ATTN
        k = z[..., o:o + D_ATTN].reshape(b, s, ATTN_HEADS, HEAD_DIM); o += D_ATTN
        v = z[..., o:o + D_ATTN].reshape(b, s, ATTN_HEADS, HEAD_DIM); o += D_ATTN
        f_logit = z[..., o:o + ATTN_HEADS]; o += ATTN_HEADS
        u = z[..., o:o + D_POOL]
        log_f = jax.nn.log_sigmoid(f_logit.astype(jnp.float32) + b_forget[i].astype(jnp.float32))
        a = forgetting_attention(q, k, v, log_f)
        m = multiscale_pool(u, w_pool[i], pool_scale[i])
        mix = jnp.concatenate([rms_norm(a, g_attn_grp[i]), rms_norm(m, g_pool_grp[i])], axis=-1)
        h = h + rms_norm(mix @ w_out[i], g_mix_post[i])
        hn = rms_norm(h, g_ffn_pre[i])
        ff = (jax.nn.silu(hn @ w_ffn_gate[i]) * (hn @ w_ffn_up[i])) @ w_ffn_down[i]
        h = h + rms_norm(ff, g_ffn_post[i])
        e = rms_norm(p[i] @ w_ple_proj[i], g_ple[i])
        h = h + jax.nn.sigmoid(h @ w_ple_gate[i]) * e
    return h


def setup_inputs(seed=0):
    out = dict(first_inputs(seed))
    for name, value in second_inputs(seed + 1).items():
        if name != "x":
            out[name + "_2"] = value
    return out


def reference(
    x, meta, conv_w_in, conv_b_in, conv_w_dw, conv_b_dw, conv_norm_g, conv_norm_b, conv_w_out,
    conv_b_out, gla_w_in, gla_w_a2, gla_b_a, gla_norm_g, gla_w_out, post_ln_g, post_ln_b, p_2,
    g_mix_pre_2, w_in_2, b_forget_2, g_attn_grp_2, g_pool_grp_2, w_pool_2, pool_scale_2,
    w_out_2, g_mix_post_2, g_ffn_pre_2, w_ffn_gate_2, w_ffn_up_2, w_ffn_down_2, g_ffn_post_2,
    w_ple_proj_2, g_ple_2, w_ple_gate_2,
):
    x = first_block(
        x, meta, conv_w_in, conv_b_in, conv_w_dw, conv_b_dw, conv_norm_g, conv_norm_b,
        conv_w_out, conv_b_out, gla_w_in, gla_w_a2, gla_b_a, gla_norm_g, gla_w_out, post_ln_g,
        post_ln_b,
    )
    return second_block(
        x, p_2, g_mix_pre_2, w_in_2, b_forget_2, g_attn_grp_2, g_pool_grp_2, w_pool_2,
        pool_scale_2, w_out_2, g_mix_post_2, g_ffn_pre_2, w_ffn_gate_2, w_ffn_up_2,
        w_ffn_down_2, g_ffn_post_2, w_ple_proj_2, g_ple_2, w_ple_gate_2,
    )


_drawn_inputs = setup_inputs


def setup_inputs(seed=0):
    import zlib

    import numpy as np

    out = dict(_drawn_inputs(seed))
    spreads = {}
    factors = {'conv_b_in': 8.0,
     'conv_b_dw': 8.0,
     'conv_norm_g': 8.0,
     'conv_norm_b': 8.0,
     'gla_b_a': 8.0,
     'gla_norm_g': 25.161,
     'g_ple_2': 3.591,
     'conv_b_out': 2.79}
    for name, (base, spread) in spreads.items():
        noise = np.random.default_rng([zlib.crc32(name.encode()), seed]).standard_normal(out[name].shape)
        drawn = base * np.exp(spread * noise) if base else spread * noise
        out[name] = __import__('jax').numpy.asarray(drawn.astype(out[name].dtype))
    for name, factor in factors.items():
        out[name] = (out[name] * factor).astype(out[name].dtype)
    return out
```

```python
from contextlib import ExitStack

import concourse.bass as bass
from concourse import mybir

ALU = mybir.AluOpType
ACT = mybir.ActivationFunctionType
F32 = mybir.dt.float32
F32R = mybir.dt.float32r
I32 = mybir.dt.int32

P = 128
D = 1024
SEQ = 1024
META = 16
T = META + SEQ
KT = D // P
NX = SEQ // P
HALF = 512
TAPS = 31
PAD = TAPS - 1
ALPHA = 4 ** 0.25
LN_EPS = 1e-5
RMS_EPS = 1e-6
UNIT = 256
GH, GK, GV = 4, 128, 256
TAU = 16.0
RANK = 16
LEVELS = 7
AH, AD = 8, 64
FGROUPS = 11
MASKED = 1e30
BIG = 3e38

TILES = [(0, META)] + [(META + P * j, P) for j in range(NX)]
CHUNKS3 = [(0, 352), (352, 352), (704, 336)]
CHUNKS2 = [(0, 512), (512, 512)]

U_CONV, U_GQK, U_GV, U_GR, U_AQK, U_AV, U_AU, U_FFN, U_END = 0, 12, 16, 20, 24, 28, 30, 32, 65


def u_gate(g):
    return U_FFN if g == 0 else U_FFN + 2 + 3 * (g - 1)


def u_down(g):
    return U_FFN + 4 + 3 * g if g < FGROUPS - 1 else U_END - 1


class Chain:

    def __init__(self, sem):
        self.sem, self.n = sem, 0

    def step(self, eng, ins):
        self.n += 1
        ins.then_inc(self.sem, 1)
        eng.wait_ge(self.sem, self.n)


def after(eng, sem, value, base=0):
    if value > 0:
        eng.wait_ge(sem, base + value)


def hybrid_block(nc, I, out):
    ctx = ExitStack()
    with ctx:
        base = (nc.sbuf_base + 31) // 32 * 32

        def at(name, shape, off, dt=F32):
            return nc.alloc_sbuf_tensor_at(name, shape, dt, offset=base + off)

        def sem(name):
            return ctx.enter_context(nc.semaphore(name))

        C0 = 0
        A0 = 3200
        A1 = A0 + KT * T * 4
        S0 = A0 + 2 * KT * T * 4
        SLOT = 2 * KT * UNIT * 4
        W0 = S0 + 3 * SLOT
        O0 = W0 + 16384
        Z0 = O0 + KT * T * 4

        ident = at("ident", [P, P], C0)
        ones_mean = at("ones_mean", [P, P], C0 + 512)
        NV = TAPS + 6
        conv_vec = at("conv_vec", [P, KT, NV], C0 + 1024)
        causal = at("causal", [P, P], C0 + 1024)
        inv_count = at("inv_count", [P, 16], C0 + 2208)
        stat = at("stat", [P, 96], C0 + 2272)
        a1_raw = at("a1_raw", [P, KT, RANK], C0 + 2656)
        f_raw = at("f_raw", [P, KT, AH], C0 + 2656)

        xh = at("xh", [P, KT, T], A0, F32R)
        xl = at("xl", [P, KT, T], A0 + KT * T * 4, F32R)
        raw = at("raw", [P, KT, UNIT], W0)
        raw_down = raw[:].rearrange("p k n -> p (k n)").rearrange("p (f n) -> p f n", f=2)
        wh = [at(f"wh{s}", [P, KT, UNIT], S0 + s * SLOT, F32R) for s in range(3)]
        wl = [at(f"wl{s}", [P, KT, UNIT], S0 + s * SLOT + SLOT // 2, F32R) for s in range(3)]
        wh_down = wh[2][:].rearrange("p k n -> p (k n)").rearrange("p (f n) -> p f n", f=2)
        wl_down = wl[2][:].rearrange("p k n -> p (k n)").rearrange("p (f n) -> p f n", f=2)

        x_stage = at("x_stage", [P, 4, D], O0)
        vec_rows = at("vec_rows", [NV, D], Z0 + KT * (T + PAD) * 4)
        silu_z = at("silu_z", [P, KT, T], O0)
        glu = at("glu", [P, KT, T + PAD], Z0)
        a_part = at("a_part", [P, T], Z0 + KT * (T + PAD) * 4)
        gate_part = at("gate_part", [P, T], Z0 + KT * (T + PAD) * 4 + T * 4)
        tap_sum = [at(f"tap_sum{e}", [P, T], S0 + 2 * SLOT + e * T * 4) for e in range(2)]
        conv_sq = at("conv_sq", [P, KT, 352], S0 + 2 * SLOT)
        conv_std = at("conv_std", [P, T], Z0 + KT * (T + PAD) * 4)
        w_conv_out = at("w_conv_out", [P, KT, D], S0)
        rows3 = [at(f"rows3_{s}", [P, D], W0 + 8192 + s * 4096) for s in range(2)]
        gain3 = [at(f"gain3_{s}", [P, D], O0 + s * 4096) for s in range(3)]

        qk = at("qk", [P, 2 * GH, T], Z0)
        arg = at("arg", [P, 4, GH, P], Z0 + 33280)
        v_meta = at("v_meta", [META, D], Z0 + 33280)
        a1h = at("a1h", [P, KT, P], O0, F32R)
        a1l = at("a1l", [P, KT, P], O0 + 4096, F32R)
        a1_pad = at("a1_pad", [P, KT, P], O0 + 8192)
        decay = at("decay", [P, GH, P], Z0 + 41472)
        v_rows = at("v_rows", [P, NX, D], O0)
        k_decayed = at("k_decayed", [P, GH, P], S0 + 2 * SLOT)
        k_rows = at("k_rows", [P, GH, P], S0 + 2 * SLOT + 2048)
        att = at("att", [P, GH, P], S0 + 2 * SLOT + 4096)
        state = at("state", [P, GH, GV], S0 + 2 * SLOT + 6144)
        a1 = at("a1", [33, T], S0 + 2 * SLOT + 10240)
        pair_mask = at("pair_mask", [P, LEVELS, 64], S0 + 2 * SLOT + 14400, I32)
        pair_mask_f = at("pair_mask_f", [P, LEVELS, 64], Z0 + 33280)
        w_a2 = at("w_a2", [33, GH * GK], W0 + 8192)
        q_decayed = at("q_decayed", [P, GH, P], W0 + 8192 + 2048)
        soft = at("soft", [P, GH, P], W0 + 8192 + 4096)
        norm_bc = at("norm_bc", [P, GV], W0 + 8192 + 6144)
        o_junk = at("o_junk", [P, GV], W0 + 8192 + 7168)
        r_silu = [at(f"r_silu{s}", [P, GV], Z0 + 33280 + s * 1024) for s in range(2)]
        w_gla_out = at("w_gla_out", [P, KT, D], Z0)
        act5 = [at(f"act5_{s}", [P, KT, P], Z0 + 33280 + s * 4096) for s in range(2)]
        rows5 = [at(f"rows5_{s}", [P, D], S0 + 2 * SLOT + s * 4096) for s in range(2)]
        normed5 = at("normed5", [P, D], S0 + 2 * SLOT + 8192)
        gain5 = [at("gain5_0", [P, D], W0 + 8192), at("gain5_1", [P, D], W0 + 12288),
                 at("gain5_2", [P, D], S0 + 2 * SLOT + 12288)]

        aqk = at("aqk", [P, KT, SEQ], Z0)
        fh = at("fh", [P, KT, P], Z0 + 32768, F32R)
        fl = at("fl", [P, KT, P], Z0 + 32768 + 4096, F32R)
        f_pad = at("f_pad", [P, KT, P], O0 + 12288)
        f_logit = at("f_logit", [AH, SEQ], O0)
        f_soft = at("f_soft", [AH, SEQ], O0 + 4096)
        f_cum = at("f_cum", [AH, SEQ], O0 + 8192)
        v6 = at("v6", [P, NX, HALF], S0 + 2 * SLOT)
        pool_u = at("pool_u", [P, 4, SEQ], W0)
        cum_bc = at("cum_bc", [P, AH, SEQ], O0)
        score = [at(f"score{s}", [P, SEQ], A0 + 32768 + s * 4096) for s in range(2)]
        prob_t = [at(f"prob_t{s}", [P, SEQ], A0 + 40960 + s * 4096) for s in range(2)]
        mix_row = [at(f"mix_row{s}", [P, D], A0 + 49152 + s * 4096) for s in range(2)]
        pool_tmp = [at(f"pool_tmp{s}", [P, SEQ], A0 + 57344 + s * 4096) for s in range(2)]
        mix_gain = at("mix_gain", [P, D], Z0 + 32768)
        pool_gain = at("pool_gain", [P, HALF], Z0 + 32768 + 4096)
        w_pool = at("w_pool", [P, 4, P], Z0 + 32768 + 6144)
        mix_t = at("mix_t", [P, KT, SEQ], A0)
        mix_sq = at("mix_sq", [P, HALF], Z0 + 40960)
        w_mix_out = at("w_mix_out", [P, KT, D], S0)
        rows7 = [at(f"rows7_{s}", [P, D], Z0 + s * 4096) for s in range(2)]
        scaled7 = [at(f"scaled7_{s}", [P, D], Z0 + 8192 + s * 4096) for s in range(2)]
        gain7 = [at(f"gain7_{s}", [P, D], Z0 + 16384 + s * 4096) for s in range(2)]
        normed7 = [at(f"normed7_{s}", [P, D], Z0 + 24576 + s * 4096) for s in range(2)]
        xh7 = at("xh7", [P, KT, T], O0, F32R)
        xl7 = at("xl7", [P, KT, T], A0 + KT * T * 4, F32R)

        ffh = [at(f"ffh{b}", [P, 2, SEQ], A0 + b * 16384, F32R) for b in range(2)]
        ffl = [at(f"ffl{b}", [P, 2, SEQ], A0 + b * 16384 + 8192, F32R) for b in range(2)]
        ff_acc = at("ff_acc", [P, NX, D], Z0)
        ff_silu = at("ff_silu", [P, 2, SEQ], Z0 + 32768)
        ff_prod = [at(f"ff_prod{t}", [P, SEQ], W0 + 8192 + t * 4096) for t in range(2)]

        rows9 = [at(f"rows9_{s}", [P, D], A1 + s * 4096) for s in range(2)]
        w_ple_gate = at("w_ple_gate", [P, KT, D], O0)
        w_ple_proj = at("w_ple_proj", [P, 2, D], A1 + 8192)
        p_t = at("p_t", [P, 2, SEQ], A1 + 16384)
        out_row = [at(f"out_row{s}", [P, D], A1 + 24576 + s * 4096) for s in range(2)]
        act9 = [at(f"act9_{s}", [P, KT, P], S0 + s * 4096) for s in range(2)]
        p_stage = at("p_stage", [P, NX, 2 * P], S0 + 8192)
        gain9 = [at(f"gain9_{s}", [P, D], S0 + SLOT + s * 4096) for s in range(2)]
        e_row = at("e_row", [P, D], S0 + SLOT + 8192)
        sq9 = at("sq9", [P, D], S0 + SLOT + 12288)
        sq9e = at("sq9e", [P, D], W0 + 8192)

        PS = ctx.enter_context(nc.psum_tensor("PS", [P, 8, 512], F32))

        def banks(b, n, cols=None):
            return PS[:, b:b + n, :].rearrange("p b n -> p (b n)")[:, 0:cols or n * 512]

        def blocks(b):
            return PS[:, b:b + 2, :].rearrange("p b (q n) -> p (b q) n", n=P)

        h1_rows = nc.dram_tensor("h1_rows", (SEQ, D), F32, kind="Internal").ap()
        h2_rows = nc.dram_tensor("h2_rows", (SEQ, D), F32, kind="Internal").ap()
        h3_rows = nc.dram_tensor("h3_rows", (SEQ, D), F32, kind="Internal").ap()
        cum_rows = nc.dram_tensor("cum_rows", (AH, SEQ), F32, kind="Internal").ap()
        x_rows = I["x"][0]
        meta_rows = I["meta"]

        def row_tile(dram, j):
            return dram[j * P:(j + 1) * P, :]

        def bcast_row(vec, n):
            return vec.rearrange("(o n) -> o n", o=1).broadcast_to([P, n])

        def unit_src(w, col):
            return w[:, col:col + UNIT].rearrange("(k p) n -> p k n", p=P)

        raw_ready, unit_hi, unit_ready = sem("raw_ready"), sem("unit_hi"), sem("unit_ready")

        turned, part_hi, part_lo = sem("turned"), sem("part_hi"), sem("part_lo")
        H1, N5, N7 = 9, 18, 26
        dense_done, dense_left = sem("dense_done"), sem("dense_left")
        row_var, row_std = sem("row_var"), sem("row_std")
        Y5, Y7, Y9 = 9, 17, 25
        matrix_in, gain_in = sem("matrix_in"), sem("gain_in")
        W5, W7, W9 = 16, 32, 48
        G5, G6, G7, G9 = 48, 96, 160, 192
        rows_in, rows_out = [sem("rows_in0"), sem("rows_in1")], [sem("rows_out0"), sem("rows_out1")]
        ROWS5, ROWS7, ROWS9 = [80, 64], [144, 128], [208, 192]
        H2_OUT, H3_OUT, OUT = 64, 128, 192
        dve_own, act_own, pool_own = Chain(sem("dve_own")), Chain(sem("act_own")), Chain(sem("pool_own"))

        def load_unit(sp, u):
            after(sp, unit_ready, u)
            if u < 8:
                for s in range(2):
                    sp.dma_start(raw[:, :, s * P:(s + 1) * P], I["conv_w_in"][0][:, u * P + s * D:u * P + s * D + P]
                                       .rearrange("(k p) n -> p k n", p=P)).then_inc(raw_ready, 16)
                return
            if u < U_GQK:
                src = unit_src(I["conv_w_in"][0], 2 * D + (u - 8) * UNIT)
            elif u < U_AQK:
                src = unit_src(I["gla_w_in"][0], (u - U_GQK) * UNIT)
            elif u < U_AU:
                src = unit_src(I["w_in_2"][0], (u - U_AQK) * UNIT)
            elif u < U_FFN:
                src = unit_src(I["w_in_2"][0], 3 * HALF + AH + (u - U_AU) * UNIT)
            else:
                n = u - U_FFN - 2
                if u == U_END - 1 or (n >= 0 and n % 3 == 2):
                    g = FGROUPS - 1 if u == U_END - 1 else n // 3
                    sp.dma_start(raw_down, I["w_ffn_down_2"][0][g * UNIT:(g + 1) * UNIT, :]
                                 .rearrange("(f p) n -> p f n", p=P)).then_inc(raw_ready, 16)
                    return
                g, up = (0, u - U_FFN) if n < 0 else (1 + n // 3, n % 3)
                src = unit_src(I["w_ffn_up_2" if up else "w_ffn_gate_2"][0], g * UNIT)
            sp.dma_start(raw[:], src).then_inc(raw_ready, 16)

        def raw_count(u):
            return 16 * (u + 1 + min(u + 1, 8))

        def split_unit(pool, u, slot):
            pool.wait_ge(raw_ready, raw_count(u))
            nc.gpsimd.tensor_copy(wh[slot][:], raw[:]).then_inc(unit_hi, 1)
            pool.wait_ge(unit_hi, u + 1)
            nc.gpsimd.tensor_tensor(wl[slot][:], raw[:], wh[slot][:].bitcast(F32), ALU.subtract).then_inc(unit_ready, 1)

        def products(terms, chunks, out_of):
            for n, (sh, sl, mh, ml) in enumerate(terms):
                for m, (s, x) in enumerate(((sh, mh), (sh, ml), (sl, mh))):
                    for c, (c0, cn) in enumerate(chunks):
                        last = nc.tensor.matmul(out_of(c, cn), s, x[:, c0:c0 + cn], start=n == 0 and m == 0,
                                                stop=n == len(terms) - 1 and m == 2)
            return last

        def channel_tile(h, l, t, chunks, bank, x=(xh, xl)):
            return products([(h[:, k, t * P:(t + 1) * P], l[:, k, t * P:(t + 1) * P], x[0][:, k, :], x[1][:, k, :])
                             for k in range(KT)], chunks, lambda c, cn: PS[:, bank + c, 0:cn])

        def token_tile(slot, c0, bank):
            return products([(xh[:, k, c0:c0 + P], xl[:, k, c0:c0 + P], wh[slot][:, k, :], wl[slot][:, k, :])
                             for k in range(KT)], [(0, UNIT)], lambda c, cn: PS[:, bank, 0:cn])

        def dense_rows(act_of, w, rows, bank):
            for k in range(KT):
                for half in range(2):
                    last = nc.tensor.matmul(PS[0:rows, bank + half, :], act_of(k), w[:, k, half * HALF:(half + 1) * HALF],
                                            start=k == 0, stop=k == KT - 1)
            return last

        def turn_row(src, rows, bank):
            for k in range(KT):
                last = nc.tensor.transpose(blocks(bank)[:, k, 0:rows], src[0:rows, k * P:(k + 1) * P], ident[0:rows, 0:rows])
            return last

        const_ready, vec_in, vec_turned, vec_ready = sem("const_ready"), sem("vec_in"), sem("vec_turned"), sem("vec_ready")
        x_in = [sem(f"x_in{s}") for s in range(4)]

        def consts_pool(pool):
            own = Chain(const_ready)
            own.step(pool, nc.gpsimd.memset(ident[:], 0.0))
            own.step(pool, nc.gpsimd.affine_select(out=ident[:], in_=ident[:], compare_op=ALU.not_equal, fill=1.0, base=0,
                                             pattern=[[-1, P]], channel_multiplier=1))
            own.step(pool, nc.gpsimd.memset(ones_mean[:], 1.0 / D))

        def inputs_sync(sp):
            rows = [(0, TAPS, I["conv_w_dw"][0]), (TAPS, 1, I["conv_b_dw"]), (TAPS + 1, 1, I["conv_norm_g"]),
                    (TAPS + 2, 1, I["conv_norm_b"]), (TAPS + 3, 3, I["conv_b_in"][0].rearrange("(r n) -> r n", r=3))]
            for r0, n, src in rows:
                sp.dma_start(vec_rows[r0:r0 + n, :], src).then_inc(vec_in, 16)
            for t, (c0, n) in enumerate(TILES):
                after(sp, turned, t - 3)
                src = meta_rows if t == 0 else row_tile(x_rows, t - 1)
                sp.dma_start(x_stage[0:n, t % 4, :], src).then_inc(x_in[t % 4], 16)
                if t == 3:
                    load_unit(sp, 0)

        def inputs_tensor(pe):
            pe.wait_ge(const_ready, 3)
            pe.wait_ge(vec_in, 80)
            for k in range(KT):
                last = nc.tensor.transpose(PS[:, 0, k * NV:(k + 1) * NV], vec_rows[:, k * P:(k + 1) * P], ident[0:NV, 0:NV])
            last.then_inc(vec_turned, 1)
            for t, (c0, n) in enumerate(TILES):
                pe.wait_ge(x_in[t % 4], 16 * (t // 4 + 1))
                after(pe, part_lo, t - 1)
                turn_row(x_stage[:, t % 4, :], n, 4 + 2 * (t % 2)).then_inc(turned, 1)

        def inputs_scalar(act):
            for t, (c0, n) in enumerate(TILES):
                act.wait_ge(turned, t + 1)
                nc.scalar.copy(xh[:, :, c0:c0 + n], blocks(4 + 2 * (t % 2))[:, :, 0:n]).then_inc(part_hi, 1)

        def inputs_vector(dve):
            dve.wait_ge(vec_turned, 1)
            nc.vector.tensor_copy(conv_vec[:].rearrange("p k r -> p (k r)"), PS[:, 0, 0:KT * NV]).then_inc(vec_ready, 1)
            for t, (c0, n) in enumerate(TILES):
                dve.wait_ge(part_hi, t + 1)
                nc.vector.tensor_tensor(xl[:, :, c0:c0 + n], blocks(4 + 2 * (t % 2))[:, :, 0:n],
                                        xh[:, :, c0:c0 + n].bitcast(F32), ALU.subtract).then_inc(part_lo, 1)

        conv_tile, conv_left = sem("conv_tile"), sem("conv_left")
        pads_ready, glu_ready, tap_done, conv_ready = sem("pads_ready"), sem("glu_ready"), sem("tap_done"), sem("conv_ready")

        def conv_in_sync(sp):
            for u in range(1, U_GQK):
                load_unit(sp, u)

        def conv_in_tensor(pe):
            pe.wait_ge(part_lo, len(TILES))
            pe.wait_ge(vec_ready, 1)
            with pe.Fori(0, U_GQK // 2) as i:
                for slot in range(2):
                    pe.wait_ge(unit_ready, i * 2 + slot + 1)
                    for t in range(2):
                        pe.wait_ge(conv_left, i * 4 + 2 * slot + t + 1)
                        channel_tile(wh[slot], wl[slot], t, CHUNKS3, 3 * t).then_inc(conv_tile, 1)

        def out_of_banks(eng_op, dst, bank, width=352, cols=T):
            eng_op(dst[:, 0:2 * width].rearrange("p (c n) -> p c n", c=2), PS[:, bank:bank + 2, 0:width])
            return eng_op(dst[:, 2 * width:cols], PS[:, bank + 2, 0:cols - 2 * width])

        def conv_in_scalar(act):
            act.wait_ge(vec_ready, 1)
            bias = lambda r, k: conv_vec[:, k, TAPS + 3 + r:TAPS + 4 + r]
            for u in range(8):
                act.wait_ge(conv_tile, 2 * u + 1)
                after(act, glu_ready, u)
                out_of_banks(lambda o, i: nc.scalar.activation(o, i, ACT.Identity, bias=bias(0, u)), a_part, 0)\
                    .then_inc(conv_left, 1)
                act.wait_ge(conv_tile, 2 * u + 2)
                out_of_banks(lambda o, i: nc.scalar.activation(o, i, ACT.Sigmoid, bias=bias(1, u)), gate_part, 3)\
                    .then_inc(conv_left, 1)
            for k in range(KT):
                act.wait_ge(conv_tile, 16 + k + 1)
                out_of_banks(lambda o, i: nc.scalar.activation(o, i, ACT.Silu, bias=bias(2, k)), silu_z[:, k, :], 3 * (k % 2))\
                    .then_inc(conv_left, 1)

        def conv_in_pool(pool):
            nc.gpsimd.memset(glu[:, :, 0:PAD], 0.0).then_inc(pads_ready, 1)
            split_unit(pool, 0, 0)
            split_unit(pool, 1, 1)
            for u in range(U_GQK):
                if u < 8:
                    pool.wait_ge(conv_left, 2 + 2 * u + 2)
                    nc.gpsimd.tensor_tensor(glu[:, u, PAD:], a_part[:], gate_part[:], ALU.mult).then_inc(glu_ready, 1)
                if u + 2 < U_GQK:
                    pool.wait_ge(conv_tile, 2 * (u + 1))
                    split_unit(pool, u + 2, u % 2)

        def conv_vector(dve):
            nc.vector.memset(stat[:, 95:96], 0.0).then_inc(conv_left, 2)
            dve.wait_ge(pads_ready, 1)
            with dve.Fori(0, KT) as k:
                g = glu[:, bass.ds(k, 1), :].rearrange("p o t -> p (o t)")
                vec = conv_vec[:, bass.ds(k, 1), :].rearrange("p o r -> p (o r)")
                dve.wait_ge(glu_ready, k + 1)
                for j in range(TAPS):
                    if j >= 2:
                        dve.wait_ge(tap_done, k * TAPS + j - 1)
                    acc = tap_sum[j % 2]
                    if j == 0:
                        ins = nc.vector.tensor_scalar(acc[:], g[:, 0:T], vec[:, 0:1], vec[:, TAPS:TAPS + 1], ALU.mult, ALU.add)
                    elif j == 1:
                        ins = nc.vector.tensor_scalar(acc[:], g[:, 1:1 + T], vec[:, 1:2], None, ALU.mult)
                    else:
                        ins = nc.vector.scalar_tensor_tensor(out=acc[:], in0=g[:, j:j + T], scalar=vec[:, j:j + 1], in1=acc[:],
                                                             op0=ALU.mult, op1=ALU.add)
                    ins.then_inc(tap_done, 1)
                dve.wait_ge(tap_done, (k + 1) * TAPS)
                nc.vector.tensor_tensor(g[:, PAD:], tap_sum[0][:], tap_sum[1][:], ALU.add).then_inc(conv_ready, 1)
                dve.wait_ge(conv_ready, k + 1)

        (mean_ready, centered, squared, var_ready, std_ready, conv_normed, conv_silu, conv_gated) = (
            sem(s) for s in ("mean_ready", "centered", "squared", "var_ready", "std_ready", "conv_normed", "conv_silu", "conv_gated"))

        def conv_chunk(c):
            c0, cn = CHUNKS3[c]
            return glu[:, :, PAD + c0:PAD + c0 + cn]

        def over_channels(ap, n):
            return ap.rearrange("p (o n) -> p o n", o=1).broadcast_to([P, KT, n])

        def conv_norm_tensor(pe):
            pe.wait_ge(conv_ready, KT)
            pe.wait_ge(conv_left, 2 + 24)
            for c, (c0, cn) in enumerate(CHUNKS3):
                for k in range(KT):
                    last = nc.tensor.matmul(PS[:, c, 0:cn], ones_mean[:], conv_chunk(c)[:, k, :], start=k == 0, stop=k == KT - 1)
                last.then_inc(mean_ready, 1)
            for c, (c0, cn) in enumerate(CHUNKS3):
                pe.wait_ge(squared, c + 1)
                for k in range(KT):
                    last = nc.tensor.matmul(PS[:, 3 + c, 0:cn], ones_mean[:], conv_sq[:, k, 0:cn], start=k == 0, stop=k == KT - 1)
                last.then_inc(var_ready, 1)

        def conv_norm_vector(dve):
            for c, (c0, cn) in enumerate(CHUNKS3):
                dve.wait_ge(mean_ready, c + 1)
                nc.vector.tensor_tensor(conv_chunk(c), conv_chunk(c), over_channels(PS[:, c, 0:cn], cn), ALU.subtract)\
                    .then_inc(centered, 1)
            for c, (c0, cn) in enumerate(CHUNKS3):
                dve.wait_ge(std_ready, c + 1)
                rstd = conv_std[:, c0:c0 + cn]
                dve_own.step(dve, nc.vector.reciprocal(rstd, rstd))
                nc.vector.tensor_tensor(conv_chunk(c), conv_chunk(c), over_channels(rstd, cn), ALU.mult).then_inc(conv_normed, 1)
            for c, (c0, cn) in enumerate(CHUNKS3):
                dve.wait_ge(conv_silu, KT * (c + 1))
                nc.vector.tensor_tensor(conv_chunk(c), conv_chunk(c), silu_z[:, :, c0:c0 + cn], ALU.mult).then_inc(conv_gated, 1)

        def conv_norm_scalar(act):
            for c, (c0, cn) in enumerate(CHUNKS3):
                act.wait_ge(centered, c + 1)
                after(act, var_ready, c)
                nc.scalar.activation(conv_sq[:, :, 0:cn], conv_chunk(c), ACT.Square).then_inc(squared, 1)
            for c, (c0, cn) in enumerate(CHUNKS3):
                act.wait_ge(var_ready, c + 1)
                nc.scalar.activation(conv_std[:, c0:c0 + cn], PS[:, 3 + c, 0:cn], ACT.Sqrt, bias=LN_EPS).then_inc(std_ready, 1)
            for c, (c0, cn) in enumerate(CHUNKS3):
                act.wait_ge(conv_normed, c + 1)
                for k in range(KT):
                    x = conv_chunk(c)[:, k, :]
                    nc.scalar.activation(x, x, ACT.Silu, bias=conv_vec[:, k, TAPS + 2:TAPS + 3],
                                         scale=conv_vec[:, k, TAPS + 1:TAPS + 2]).then_inc(conv_silu, 1)

        a1_in = sem("a1_in")
        (xn3, h1_done) = (
            sem(s) for s in ("xn3", "h1_done"))
        STATS, MEAN, VAR, STD, RSTD = stat[:, 0:12], stat[:, 12:13], stat[:, 13:14], stat[:, 14:15], stat[:, 15:16]

        def conv_out_sync(sp):
            sp.wait_ge(conv_tile, 24)
            sp.dma_start(w_conv_out[:], I["conv_w_out"][0].rearrange("(k p) n -> p k n", p=P)).then_inc(matrix_in, 16)
            for t in range(2):
                src = meta_rows if t == 0 else row_tile(x_rows, t - 1)
                sp.dma_start(rows3[t][0:TILES[t][1], :], src).then_inc(rows_in[t], 16)
            load_unit(sp, U_GQK)
            sp.wait_ge(conv_gated, 3)
            for s, vec in enumerate((I["conv_b_out"][0], I["post_ln_g"][0], I["post_ln_b"][0])):
                sp.dma_start(gain3[s][:], bcast_row(vec, D)).then_inc(gain_in, 16)
            sp.dma_start(a1_raw[:], I["gla_w_in"][0][:, 3 * D:3 * D + RANK].rearrange("(k p) n -> p k n", p=P)).then_inc(a1_in, 16)
            for t, (c0, n) in enumerate(TILES):
                sp.wait_ge(h1_done, t + 1)
                if t > 0:
                    sp.dma_start(row_tile(h1_rows, t - 1), rows3[t % 2][:]).then_inc(rows_out[t % 2], 16)
                if t + 2 < len(TILES):
                    after(sp, rows_out[t % 2], 16 * (t // 2 + t % 2))
                    sp.wait_ge(turned, H1 + t + 1)
                    sp.dma_start(rows3[t % 2][:], row_tile(x_rows, t + 1)).then_inc(rows_in[t % 2], 16)

        def conv_out_tensor(pe):
            pe.wait_ge(matrix_in, 16)
            pe.wait_ge(conv_gated, 3)

            def turn(t):
                pe.wait_ge(h1_done, t + 1)
                after(pe, part_lo, t - 1, H1)
                turn_row(rows3[t % 2], TILES[t][1], 4 + 2 * (t % 2)).then_inc(turned, 1)

            for t, (c0, n) in enumerate(TILES):
                after(pe, dense_left, t - 1)
                dense_rows(lambda k: glu[:, k, PAD + c0:PAD + c0 + n], w_conv_out, n, 2 * (t % 2)).then_inc(dense_done, 1)
                if t >= 1:
                    turn(t - 1)
            turn(len(TILES) - 1)

        def layer_norm_rows(dve, x, n, count):
            for h in range(2):
                last = nc.vector.bn_stats(STATS[0:n, h * 6:(h + 1) * 6], x[0:n, h * HALF:(h + 1) * HALF])
            dve_own.step(dve, last)
            nc.vector.bn_aggr(stat[0:n, 12:14], STATS[0:n, :]).then_inc(row_var, 1)
            dve.wait_ge(row_std, count)
            dve_own.step(dve, nc.vector.reciprocal(RSTD[0:n, :], STD[0:n, :]))
            return nc.vector.tensor_scalar(x[0:n, :], x[0:n, :], MEAN[0:n, :], RSTD[0:n, :], ALU.subtract, ALU.mult)

        def conv_out_vector(dve):
            dve.wait_ge(gain_in, 48)

            def low(t):
                c0, n = TILES[t]
                dve.wait_ge(part_hi, H1 + t + 1)
                nc.vector.tensor_tensor(xl[:, :, c0:c0 + n], blocks(4 + 2 * (t % 2))[:, :, 0:n],
                                        xh[:, :, c0:c0 + n].bitcast(F32), ALU.subtract).then_inc(part_lo, 1)

            for t, (c0, n) in enumerate(TILES):
                x = rows3[t % 2]
                dve.wait_ge(rows_in[t % 2], 16 * (t // 2 + 1))
                dve.wait_ge(dense_done, t + 1)
                nc.vector.scalar_tensor_tensor(out=x[0:n, :], in0=x[0:n, :], scalar=ALPHA, in1=banks(2 * (t % 2), 2, D)[0:n, :],
                                               op0=ALU.mult, op1=ALU.add).then_inc(dense_left, 1)
                dve.wait_ge(dense_left, t + 1)
                dve_own.step(dve, nc.vector.tensor_tensor(x[0:n, :], x[0:n, :], gain3[0][0:n, :], ALU.add))
                layer_norm_rows(dve, x, n, t + 1).then_inc(xn3, 1)
                if t >= 1:
                    low(t - 1)
            low(len(TILES) - 1)

        def conv_out_scalar(act):
            def high(t):
                c0, n = TILES[t]
                act.wait_ge(turned, H1 + t + 1)
                nc.scalar.copy(xh[:, :, c0:c0 + n], blocks(4 + 2 * (t % 2))[:, :, 0:n]).then_inc(part_hi, 1)

            for t, (c0, n) in enumerate(TILES):
                act.wait_ge(row_var, t + 1)
                nc.scalar.activation(STD[0:n, :], VAR[0:n, :], ACT.Sqrt, bias=LN_EPS).then_inc(row_std, 1)
                if t >= 1:
                    high(t - 1)
            high(len(TILES) - 1)

        def conv_out_pool(pool):
            for t, (c0, n) in enumerate(TILES):
                x = rows3[t % 2]
                pool.wait_ge(xn3, t + 1)
                pool_own.step(pool, nc.gpsimd.tensor_tensor(x[0:n, :], x[0:n, :], gain3[1][0:n, :], ALU.mult))
                nc.gpsimd.tensor_tensor(x[0:n, :], x[0:n, :], gain3[2][0:n, :], ALU.add).then_inc(h1_done, 1)

        (a1_split, a2_zero, a2_in, mask_ready) = (
            sem(s) for s in ("a1_split", "a2_zero", "a2_in", "mask_ready"))
        (gqk_tile, gqk_left, gv_tile, gv_left, a1_ready) = (
            sem(s) for s in ("gqk_tile", "gqk_left", "gv_tile", "gv_left", "a1_ready"))
        NV_TILES = len(TILES)

        def gla_in_sync(sp):
            load_unit(sp, U_GQK + 1)
            sp.wait_ge(a2_zero, 1)
            sp.dma_start(w_a2[0:RANK, :], I["gla_w_a2"][0]).then_inc(a2_in, 16)
            sp.dma_start(w_a2[32:33, :], I["gla_b_a"]).then_inc(a2_in, 16)
            sp.dma_start(norm_bc[:], bcast_row(I["gla_norm_g"][0], GV)).then_inc(a2_in, 16)
            for u in range(U_GQK + 2, U_GR + 4):
                load_unit(sp, u)

        def gla_in_pool(pool):
            own = Chain(a1_split)
            pool.wait_ge(dense_done, 9)
            split_unit(pool, U_GQK, 0)
            split_unit(pool, U_GQK + 1, 1)
            pool.wait_ge(h1_done, 9)
            own.step(pool, nc.gpsimd.memset(a1_pad[:], 0.0))
            pool.wait_ge(a1_in, 16)
            own.step(pool, nc.gpsimd.tensor_copy(a1_pad[:, :, 0:RANK], a1_raw[:]))
            own.step(pool, nc.gpsimd.tensor_copy(a1h[:], a1_pad[:]))
            own.step(pool, nc.gpsimd.tensor_tensor(a1l[:], a1_pad[:], a1h[:].bitcast(F32), ALU.subtract))
            for s in range(2):
                pool.wait_ge(rows_out[s], 64)
            pool.wait_ge(turned, H1 + 9)
            nc.gpsimd.memset(w_a2[:], 0.0).then_inc(a2_zero, 1)
            pool.wait_ge(a2_zero, 1)
            nc.gpsimd.memset(a1[32:33, :], 1.0).then_inc(a1_ready, 1)
            pool.wait_ge(a1_ready, 1)
            own = Chain(mask_ready)
            own.step(pool, nc.gpsimd.memset(pair_mask_f[:], 1.0))
            for l in range(LEVELS):
                b = 64 >> l
                view = pair_mask_f[:, l, :].rearrange("p (n b) -> p n b", b=b)
                own.step(pool, nc.gpsimd.affine_select(out=view, in_=view, compare_op=ALU.is_ge, fill=0.0, base=0,
                                                 pattern=[[-2 * b, 64 // b], [0, b]], channel_multiplier=1))
                own.step(pool, nc.gpsimd.affine_select(out=view, in_=view, compare_op=ALU.is_ge, fill=0.0, base=b - 1,
                                                 pattern=[[2 * b, 64 // b], [0, b]], channel_multiplier=-1))
            own.step(pool, nc.gpsimd.tensor_copy(pair_mask[:], pair_mask_f[:]))
            for u in range(U_GQK + 2, U_GR + 2):
                before = u - 2
                if before < U_GV:
                    pool.wait_ge(gqk_tile, 2 * (before - U_GQK + 1))
                else:
                    pool.wait_ge(gv_tile, NV_TILES * (before - U_GV + 1))
                split_unit(pool, u, u % 2)

        def gla_in_tensor(pe):
            pe.wait_ge(part_lo, H1 + 9)
            pe.wait_ge(dense_left, 9)
            with pe.Fori(0, 2) as i:
                for slot in range(2):
                    pe.wait_ge(unit_ready, i * 2 + U_GQK + slot + 1)
                    for t in range(2):
                        pe.wait_ge(gqk_left, i * 4 + 2 * slot + t + 1)
                        channel_tile(wh[slot], wl[slot], t, CHUNKS3, 3 * t).then_inc(gqk_tile, 1)
            pe.wait_ge(a1_split, 4)
            pe.wait_ge(gqk_left, 9)
            channel_tile(a1h, a1l, 0, CHUNKS3, 0).then_inc(gqk_tile, 1)
            pe.wait_ge(gqk_left, 10)
            with pe.Fori(0, 2) as i:
                for slot in range(2):
                    pe.wait_ge(unit_ready, i * 2 + U_GV + slot + 1)
                    for t, (c0, n) in enumerate(TILES):
                        q = slot * NV_TILES + t
                        pe.wait_ge(gv_left, i * (2 * NV_TILES) + q + 1)
                        token_tile(slot, c0, 3 + q % 3).then_inc(gv_tile, 1)

        def gla_in_vector(dve):
            nc.vector.memset(stat[:, 92:93], 0.0).then_inc(gqk_left, 2)
            nc.vector.memset(stat[:, 93:94], 0.0).then_inc(gv_left, 3)

        def gla_in_scalar(act):
            act.wait_ge(conv_gated, 3)
            act.wait_ge(dense_done, 9)
            for i in range(8):
                act.wait_ge(gqk_tile, i + 1)
                scale = GK ** -0.5 if i < GH else 1.0
                out_of_banks(lambda o, x: nc.scalar.activation(o, x, ACT.Copy, scale=scale), qk[:, i, :], 3 * (i % 2))\
                    .then_inc(gqk_left, 1)
            act.wait_ge(gqk_tile, 9)
            out_of_banks(lambda o, x: nc.scalar.copy(o, x[0:32]), a1[0:32, :], 0).then_inc(gqk_left, 1)
            act.wait_ge(mask_ready, 2 + 2 * LEVELS)
            for h in range(GH):
                for t, (c0, n) in enumerate(TILES):
                    q = h * NV_TILES + t
                    act.wait_ge(gv_tile, q + 1)
                    dst = v_meta[:, h * GV:(h + 1) * GV] if t == 0 else v_rows[:, t - 1, h * GV:(h + 1) * GV]
                    nc.scalar.copy(dst, PS[0:n, 3 + q % 3, 0:GV]).then_inc(gv_left, 1)

        (z_ready, z_abs, z_min, soft_ready, cum_done, arg_ready, arg_exp, arg_mul, pair_done, diag_done, att_ready,
         bl_ready, ebl_ready, dec_exp, dec_ready, kt_done, k_rows_done, o_done, s_done, state_ready, o_kept) = (
            sem(s) for s in ("z_ready", "z_abs", "z_min", "soft_ready", "cum_done", "arg_ready", "arg_exp", "arg_mul", "pair_done",
                                     "diag_done", "att_ready", "bl_ready", "ebl_ready", "dec_exp", "dec_ready", "kt_done", "k_rows_done",
                                     "o_done", "s_done", "state_ready", "o_kept"))
        BL16, EBL = stat[:, 84:88], stat[:, 52:56]
        SS_O = stat[:, 20:52]
        GROUPS = [range(0, 4), range(4, LEVELS)]
        PAIR_BANK = [1, 4]

        def pair_scores(l):
            g = 0 if l < 4 else 1
            return banks(PAIR_BANK[g], 2, 1024).rearrange("p (l h t) -> p l h t", l=4, h=GH)[:, l % 4, :, :]

        def halves(ap, l):
            return ap.rearrange("p h t -> p (h t)").rearrange("p (m e b) -> p m e b", e=2, b=64 >> l)

        def gla_tensor(pe):
            pe.wait_ge(a2_in, 48)
            pe.wait_ge(a1_ready, 1)
            pe.wait_ge(gqk_left, 2 + 9)
            pe.wait_ge(gv_left, 3 + 4 * NV_TILES)
            for c, (c0, n) in enumerate(TILES):
                after(pe, k_rows_done, c)
                for h in range(GH):
                    last = nc.tensor.matmul(PS[:, 0, h * P:h * P + n], w_a2[:, h * GK:(h + 1) * GK], a1[:, c0:c0 + n],
                                            start=True, stop=True)
                last.then_inc(z_ready, 1)
                if c > 0:
                    after(pe, att_ready, c - 1)
                    for h in range(GH):
                        last = nc.tensor.matmul(PS[:, 3, h * P:(h + 1) * P], qk[:, GH + h, c0:c0 + n], qk[:, h, c0:c0 + n],
                                                start=True, stop=True)
                    last.then_inc(diag_done, 1)
                    for g, group in enumerate(GROUPS):
                        if g == 1:
                            after(pe, o_kept, c - 1)
                        pe.wait_ge(arg_mul, 2 * (c - 1) + g + 1)
                        for l in group:
                            for h in range(GH):
                                odd = halves(arg[:, l % 4, h:h + 1, :], l)[:, :, 1, :]
                                last = nc.tensor.matmul(pair_scores(l)[:, h, :], arg[:, l % 4, h, :], odd, start=True, stop=True)
                        last.then_inc(pair_done, 1)
                pe.wait_ge(dec_ready, 2 * c + 1)
                pe.wait_ge(z_min, c + 1)
                if c < NX:
                    for h in range(GH):
                        last = nc.tensor.transpose(PS[0:n, 0, h * P:(h + 1) * P], k_decayed[:, h, 0:n], ident[:])
                    last.then_inc(kt_done, 1)
                if c > 0:
                    pe.wait_ge(dec_ready, 2 * c + 2)
                    pe.wait_ge(att_ready, c)
                    pe.wait_ge(state_ready, c)
                    for h in range(GH):
                        o = PS[:, 4 + h // 2, (h % 2) * GV:(h % 2 + 1) * GV]
                        nc.tensor.matmul(o, att[:, h, :], v_rows[:, c - 1, h * GV:(h + 1) * GV], start=True, stop=False)
                        last = nc.tensor.matmul(o, q_decayed[:, h, :], state[:, h, :], start=False, stop=True)
                    last.then_inc(o_done, 1)
                if c < NX:
                    pe.wait_ge(k_rows_done, c + 1)
                    after(pe, state_ready, c)
                    v = v_meta if c == 0 else v_rows[:, c - 1, :]
                    for h in range(GH):
                        last = nc.tensor.matmul(PS[:, 6 + h // 2, (h % 2) * GV:(h % 2 + 1) * GV], k_rows[0:n, h, :],
                                                v[:, h * GV:(h + 1) * GV], start=True, stop=True)
                    last.then_inc(s_done, 1)

        def gla_scalar(act):
            for c, (c0, n) in enumerate(TILES):
                act.wait_ge(z_ready, c + 1)
                after(act, cum_done, GH * c)
                z = PS[:, 0, :].rearrange("p (h t) -> p h t", h=GH)[:, :, 0:n]
                x = soft[:, :, 0:n]
                nc.scalar.activation(x, z, ACT.Abs).then_inc(z_abs, 1)
                act.wait_ge(z_abs, c + 1)
                act_own.step(act, nc.scalar.activation(x, x, ACT.Exp, scale=-1.0))
                nc.scalar.activation(x, x, ACT.Ln, bias=1.0).then_inc(soft_ready, 1)
                act.wait_ge(bl_ready, c + 1)
                after(act, kt_done, c)
                for h in range(GH):
                    last = nc.scalar.activation(k_decayed[:, h, 0:n], decay[:, h, 0:n], ACT.Exp, bias=BL16[:, h:h + 1],
                                                scale=-1 / TAU)
                last.then_inc(dec_exp, 1)
                after(act, state_ready, c)
                nc.scalar.activation(EBL, BL16, ACT.Exp).then_inc(ebl_ready, 1)
                after(act, o_done, c - 1)
                if c > 0:
                    nc.scalar.activation(q_decayed[:], decay[:], ACT.Exp, scale=1 / TAU).then_inc(dec_exp, 1)
                    for g, group in enumerate(GROUPS):
                        act.wait_ge(arg_ready, 2 * (c - 1) + g + 1)
                        x = arg[:, 0:len(group), :, :]
                        nc.scalar.activation(x, x, ACT.Exp, scale=1 / TAU).then_inc(arg_exp, 1)
                if c < NX:
                    act.wait_ge(kt_done, c + 1)
                    after(act, s_done, c)
                    nc.scalar.copy(k_rows[0:n].rearrange("p h t -> p (h t)"), PS[0:n, 0, :]).then_inc(k_rows_done, 1)
                if c > 0:
                    act.wait_ge(o_done, c)
                    for h in range(GH):
                        o = PS[:, 4 + h // 2, (h % 2) * GV:(h % 2 + 1) * GV]
                        col = 4 * (c - 1) + h
                        act_own.step(act, nc.scalar.activation(o_junk[:], o, ACT.Square,
                                             accum_out=SS_O[:, col:col + 1]))
                    if c < NX:
                        act.wait_ge(s_done, c + 1)
                    nc.scalar.copy(v_rows[:, c - 1, :], banks(4, 2, D)).then_inc(o_kept, 1)

        def gla_vector(dve):
            dve.wait_ge(mask_ready, 2 + 2 * LEVELS)
            for c, (c0, n) in enumerate(TILES):
                dve.wait_ge(z_abs, c + 1)
                after(dve, dec_ready, 2 * c)
                z = PS[:, 0, :].rearrange("p (h t) -> p h t", h=GH)[:, :, 0:n]
                nc.vector.tensor_scalar(decay[:, :, 0:n], z, 0.0, None, ALU.min).then_inc(z_min, 1)
                dve.wait_ge(z_min, c + 1)
                dve.wait_ge(soft_ready, c + 1)
                for h in range(GH):
                    x = decay[:, h, 0:n]
                    nc.vector.tensor_tensor_scan(x, x, soft[:, h, 0:n], 0.0, ALU.add, ALU.subtract).then_inc(cum_done, 1)
                dve.wait_ge(cum_done, GH * (c + 1))
                after(dve, ebl_ready, c)
                nc.vector.tensor_scalar(BL16, decay[:, :, n - 1:n].rearrange("p h o -> p (h o)"), 1 / TAU, None, ALU.mult)\
                    .then_inc(bl_ready, 1)
                if c > 0:
                    if c == 1:
                        dve.wait_ge(s_done, 1)
                    for g, group in enumerate(GROUPS):
                        after(dve, pair_done, 2 * (c - 1) + g)
                        for l in group:
                            x, e = halves(decay[:], l), halves(arg[:, l % 4, :, :], l)
                            b = 64 >> l
                            ref = x[:, :, 0, b - 1:b].broadcast_to([P, 4 * 64 // b, b])
                            nc.vector.tensor_tensor(e[:, :, 0, :], ref, x[:, :, 0, :], ALU.subtract)
                            last = nc.vector.tensor_tensor(e[:, :, 1, :], x[:, :, 1, :], ref, ALU.subtract)
                        last.then_inc(arg_ready, 1)
                    dve.wait_ge(diag_done, c)
                    after(dve, o_done, c - 1)
                    dve_own.step(dve, nc.vector.tensor_tensor(att[:], PS[:, 3, :].rearrange("p (h t) -> p h t", h=GH),
                                                     ident[:].rearrange("p (o t) -> p o t", o=1).broadcast_to([P, GH, P]), ALU.mult))
                    for g, group in enumerate(GROUPS):
                        dve.wait_ge(pair_done, 2 * (c - 1) + g + 1)
                        for l in group:
                            b = 64 >> l
                            odd = att[:].rearrange("p h (m e b) -> p h m e b", e=2, b=b)[:, :, :, 1, :]
                            mask = pair_mask[:, l:l + 1, :].rearrange("p o (m b) -> p o m b", b=b).broadcast_to([P, GH, 64 // b, b])
                            last = nc.vector.copy_predicated(odd, mask, pair_scores(l).rearrange("p h (m b) -> p h m b", b=b))
                            if l < LEVELS - 1:
                                dve_own.step(dve, last)
                    last.then_inc(att_ready, 1)
                if c < NX:
                    dve.wait_ge(s_done, c + 1)
                    dve.wait_ge(ebl_ready, c + 1)
                    if c == 0:
                        nc.vector.tensor_copy(state[:].rearrange("p h e -> p (h e)"), banks(6, 2, D)).then_inc(state_ready, 1)
                    else:
                        dve.wait_ge(o_done, c)
                        for h in range(GH):
                            last = nc.vector.scalar_tensor_tensor(
                                out=state[:, h, :], in0=state[:, h, :], scalar=EBL[:, h:h + 1],
                                in1=PS[:, 6 + h // 2, (h % 2) * GV:(h % 2 + 1) * GV], op0=ALU.mult, op1=ALU.add)
                        last.then_inc(state_ready, 1)

        def gla_pool(pool):
            pool.wait_ge(gqk_left, 2 + 9)
            for c, (c0, n) in enumerate(TILES):
                pool.wait_ge(dec_exp, max(2 * c, 1))
                nc.gpsimd.tensor_tensor(k_decayed[:, :, 0:n], k_decayed[:, :, 0:n], qk[:, GH:, c0:c0 + n], ALU.mult)\
                    .then_inc(dec_ready, 1 if c else 2)
                if c == 0:
                    continue
                pool.wait_ge(dec_exp, 2 * c + 1)
                nc.gpsimd.tensor_tensor(q_decayed[:], q_decayed[:], qk[:, 0:GH, c0:c0 + n], ALU.mult).then_inc(dec_ready, 1)
                for g, group in enumerate(GROUPS):
                    pool.wait_ge(arg_exp, 2 * (c - 1) + g + 1)
                    for l in group:
                        b = 64 >> l
                        e = arg[:, l % 4, :, :].rearrange("p h (m e b) -> p h m e b", e=2, b=b)
                        q = qk[:, 0:GH, c0:c0 + n].rearrange("p h (m e b) -> p h m e b", e=2, b=b)
                        k = qk[:, GH:, c0:c0 + n].rearrange("p h (m e b) -> p h m e b", e=2, b=b)
                        nc.gpsimd.tensor_tensor(e[:, :, :, 0, :], e[:, :, :, 0, :], k[:, :, :, 0, :], ALU.mult)
                        last = nc.gpsimd.tensor_tensor(e[:, :, :, 1, :], e[:, :, :, 1, :], q[:, :, :, 1, :], ALU.mult)
                    last.then_inc(arg_mul, 1)

        (r_tile, r_left, rstd_own, r_used, gla_ready) = (
            sem(s) for s in ("r_tile", "r_left", "rstd_own", "r_used", "gla_ready"))

        def gla_gate_tensor(pe):
            pe.wait_ge(att_ready, NX)
            pe.wait_ge(k_rows_done, NX)
            with pe.Fori(0, 2) as i:
                for slot in range(2):
                    pe.wait_ge(unit_ready, i * 2 + U_GR + slot + 1)
                    for j in range(NX):
                        pe.wait_ge(r_left, i * (2 * NX) + slot * NX + j + 1)
                        token_tile(slot, META + j * P, j % 4).then_inc(r_tile, 1)

        def gla_gate_scalar(act):
            act.wait_ge(o_kept, NX)
            nc.scalar.activation(SS_O, SS_O, ACT.Sqrt, scale=1 / GV, bias=RMS_EPS).then_inc(rstd_own, 1)
            act.wait_ge(pair_done, 2 * NX)
            for q in range(GH * NX):
                act.wait_ge(r_tile, q + 1)
                after(act, r_used, q - 1)
                nc.scalar.activation(r_silu[q % 2][:], PS[:, q % 4, 0:GV], ACT.Silu).then_inc(r_left, 1)

        def gla_gate_vector(dve):
            nc.vector.memset(stat[:, 94:95], 0.0).then_inc(r_left, 4)
            dve.wait_ge(rstd_own, 1)
            dve_own.step(dve, nc.vector.reciprocal(SS_O, SS_O))
            dve.wait_ge(o_kept, NX)
            for q in range(GH * NX):
                h, j = divmod(q, NX)
                col = 4 * j + h
                dve.wait_ge(r_left, 4 + q + 1)
                x = v_rows[:, j, h * GV:(h + 1) * GV]
                nc.vector.scalar_tensor_tensor(out=x, in0=x, scalar=SS_O[:, col:col + 1], in1=r_silu[q % 2][:],
                                               op0=ALU.mult, op1=ALU.mult).then_inc(r_used, 1)

        def gla_gate_pool(pool):
            pool.wait_ge(a2_in, 48)
            for q in range(GH * NX):
                h, j = divmod(q, NX)
                if j == 0 and h < 2:
                    pool.wait_ge(r_tile, NX * (h + 1))
                    split_unit(pool, U_GR + 2 + h, h)
            for q in range(GH * NX):
                h, j = divmod(q, NX)
                pool.wait_ge(r_used, q + 1)
                x = v_rows[:, j, h * GV:(h + 1) * GV]
                nc.gpsimd.tensor_tensor(x, x, norm_bc[:], ALU.mult).then_inc(gla_ready, 1)

        (gla_turned, act5_ready, xn5, h2_done, h2_std, h2_n, n5_done) = (
            sem(s) for s in ("gla_turned", "act5_ready", "xn5", "h2_done", "h2_std", "h2_n", "n5_done"))

        def gla_out_sync(sp):
            sp.wait_ge(dec_ready, 2 * NX + 2)
            sp.wait_ge(arg_mul, 2 * NX)
            sp.wait_ge(diag_done, NX)
            sp.dma_start(w_gla_out[:], I["gla_w_out"][0].rearrange("(k p) n -> p k n", p=P)).then_inc(matrix_in, 16)
            sp.wait_ge(state_ready, NX)
            sp.wait_ge(o_done, NX)
            for j in range(2):
                sp.dma_start(rows5[j][:], row_tile(h1_rows, j)).then_inc(rows_in[j], 16)
            sp.dma_start(gain5[2][:], bcast_row(I["g_mix_pre_2"][0], D)).then_inc(gain_in, 16)
            sp.wait_ge(gla_ready, GH * NX)
            for s, vec in enumerate((I["post_ln_g"][1], I["post_ln_b"][1])):
                sp.dma_start(gain5[s][:], bcast_row(vec, D)).then_inc(gain_in, 16)
            load_unit(sp, U_AQK)
            load_unit(sp, U_AQK + 1)
            for j in range(NX):
                s = j % 2
                sp.wait_ge(h2_done, j + 1)
                sp.dma_start(row_tile(h2_rows, j), rows5[s][:]).then_inc(rows_out[s], 16)
                if j + 2 < NX:
                    sp.wait_ge(rows_out[s], H2_OUT + 16 * (j // 2 + 1))
                    sp.wait_ge(h2_n, j + 1)
                    sp.dma_start(rows5[s][:], row_tile(h1_rows, j + 2)).then_inc(rows_in[s], 16)
            for s in range(2):
                sp.wait_ge(rows_out[s], H2_OUT + 64)

        def gla_out_tensor(pe):
            pe.wait_ge(matrix_in, W5 + 16)
            pe.wait_ge(r_left, 4 + GH * NX)

            def turn(j):
                pe.wait_ge(n5_done, j + 1)
                after(pe, part_lo, j, N5)
                turn_row(normed5, P, 6).then_inc(turned, 1)

            for j in range(NX):
                pe.wait_ge(gla_ready, (GH - 1) * NX + j + 1)
                after(pe, act5_ready, j)
                turn_row(v_rows[:, j, :], P, 4).then_inc(gla_turned, 1)
                pe.wait_ge(act5_ready, j + 1)
                after(pe, dense_left, j - 1, Y5)
                dense_rows(lambda k: act5[j % 2][:, k, :], w_gla_out, P, 2 * (j % 2)).then_inc(dense_done, 1)
                if j >= 1:
                    turn(j - 1)
            turn(NX - 1)

        def gla_out_scalar(act):
            def high(j):
                act.wait_ge(turned, N5 + j + 1)
                nc.scalar.copy(xh[:, :, j * P:(j + 1) * P], blocks(6)).then_inc(part_hi, 1)

            def gla_act(j):
                act.wait_ge(gla_turned, j + 1)
                after(act, dense_done, j - 1, Y5)
                nc.scalar.copy(act5[j % 2][:], blocks(4)).then_inc(act5_ready, 1)

            act.wait_ge(r_used, GH * NX)
            gla_act(0)
            for j in range(NX):
                if j + 1 < NX:
                    gla_act(j + 1)
                act.wait_ge(row_var, Y5 + j + 1)
                nc.scalar.activation(STD, VAR, ACT.Sqrt, bias=LN_EPS).then_inc(row_std, 1)
                act.wait_ge(h2_done, j + 1)
                after(act, turned, j, N5)
                act_own.step(act, nc.scalar.activation(normed5[:], rows5[j % 2][:], ACT.Square, accum_out=stat[:, 16:17]))
                nc.scalar.activation(stat[:, 17:18], stat[:, 16:17], ACT.Sqrt, scale=1 / D, bias=RMS_EPS).then_inc(h2_std, 1)
                if j >= 1:
                    high(j - 1)
            high(NX - 1)

        def gla_out_vector(dve):
            for j in range(NX):
                x = rows5[j % 2]
                dve.wait_ge(rows_in[j % 2], ROWS5[j % 2] + 16 * (j // 2 + 1))
                dve.wait_ge(dense_done, Y5 + j + 1)
                nc.vector.scalar_tensor_tensor(out=x[:], in0=x[:], scalar=ALPHA, in1=banks(2 * (j % 2), 2, D),
                                               op0=ALU.mult, op1=ALU.add).then_inc(dense_left, 1)
                dve.wait_ge(dense_left, Y5 + j + 1)
                layer_norm_rows(dve, x, P, Y5 + j + 1).then_inc(xn5, 1)
                if j >= 1:
                    low5(dve, j - 1)
                dve.wait_ge(h2_std, j + 1)
                dve_own.step(dve, nc.vector.reciprocal(stat[:, 18:19], stat[:, 17:18]))
                nc.vector.tensor_scalar(normed5[:], x[:], stat[:, 18:19], None, ALU.mult).then_inc(h2_n, 1)
            low5(dve, NX - 1)

        def low5(dve, j):
            cols = slice(j * P, (j + 1) * P)
            dve.wait_ge(part_hi, N5 + j + 1)
            nc.vector.tensor_tensor(xl[:, :, cols], blocks(6), xh[:, :, cols].bitcast(F32), ALU.subtract).then_inc(part_lo, 1)

        def gla_out_pool(pool):
            pool.wait_ge(r_tile, GH * NX)
            split_unit(pool, U_AQK, 0)
            split_unit(pool, U_AQK + 1, 1)
            pool.wait_ge(gain_in, G5 + 48)
            for j in range(NX):
                x = rows5[j % 2]
                pool.wait_ge(xn5, j + 1)
                pool_own.step(pool, nc.gpsimd.tensor_tensor(x[:], x[:], gain5[0][:], ALU.mult))
                nc.gpsimd.tensor_tensor(x[:], x[:], gain5[1][:], ALU.add).then_inc(h2_done, 1)
                pool.wait_ge(h2_n, j + 1)
                nc.gpsimd.tensor_tensor(normed5[:], normed5[:], gain5[2][:], ALU.mult).then_inc(n5_done, 1)

        (in6_tile, in6_left, v6_tile, v6_left) = (
            sem(s) for s in ("in6_tile", "in6_left", "v6_tile", "v6_left"))
        (f_in, f_split, f_abs, f_soft_ready, f_cum_ready, cum_out, cum_in, causal_ready) = (
            sem(s) for s in ("f_in", "f_split", "f_abs", "f_soft_ready", "f_cum_ready", "cum_out", "cum_in", "causal_ready"))
        count_ready = sem("count_ready")
        B_F = stat[0:AH, 76:77]
        N_QK = 8

        def attn_in_sync(sp):
            sp.dma_start(f_raw[:], I["w_in_2"][0][:, 3 * HALF:3 * HALF + AH].rearrange("(k p) n -> p k n", p=P)).then_inc(f_in, 16)
            sp.dma_start(B_F, I["b_forget_2"].rearrange("o h -> h o")).then_inc(f_in, 16)
            for u in range(U_AQK + 2, U_FFN):
                load_unit(sp, u)
                if u == U_AV:
                    sp.wait_ge(f_cum_ready, 1)
                    sp.dma_start(cum_rows, f_cum[:]).then_inc(cum_out, 16)
                    sp.wait_ge(cum_out, 16)
                    sp.dma_start(cum_bc[:].rearrange("p h t -> p (h t)"), bcast_row(cum_rows.rearrange("h t -> (h t)"), AH * SEQ))\
                        .then_inc(cum_in, 16)
                    sp.wait_ge(in6_tile, N_QK + 1)
                    for half, name in enumerate(("g_attn_grp_2", "g_pool_grp_2")):
                        sp.dma_start(mix_gain[:, half * HALF:(half + 1) * HALF], bcast_row(I[name][0], HALF)).then_inc(gain_in, 16)
                    sp.dma_start(pool_gain[:], bcast_row(I["pool_scale_2"][0], HALF)).then_inc(gain_in, 16)
                    sp.dma_start(w_pool[:], I["w_pool_2"][0].rearrange("g c d -> c g d")).then_inc(gain_in, 16)

        def attn_in_pool(pool):
            own = Chain(f_split)
            pool.wait_ge(dense_done, Y5 + NX)
            own.step(pool, nc.gpsimd.memset(f_pad[:], 0.0))
            pool.wait_ge(f_in, 32)
            own.step(pool, nc.gpsimd.tensor_copy(f_pad[:, :, 0:AH], f_raw[:]))
            own.step(pool, nc.gpsimd.tensor_copy(fh[:], f_pad[:]))
            own.step(pool, nc.gpsimd.tensor_tensor(fl[:], f_pad[:], fh[:].bitcast(F32), ALU.subtract))
            own = Chain(causal_ready)
            own.step(pool, nc.gpsimd.memset(causal[:], 0.0))
            own.step(pool, nc.gpsimd.affine_select(out=causal[:], in_=causal[:], compare_op=ALU.is_ge, fill=MASKED, base=0,
                                             pattern=[[-1, P]], channel_multiplier=1))
            for u in range(U_AQK + 2, U_FFN):
                before = u - 2
                if before < U_AV:
                    pool.wait_ge(in6_tile, 2 * (before - U_AQK + 1))
                else:
                    pool.wait_ge(v6_tile, NX * (before - U_AV + 1))
                split_unit(pool, u, u % 2)

        def attn_in_tensor(pe):
            pe.wait_ge(part_lo, N5 + NX)
            pe.wait_ge(dense_left, Y5 + NX)
            with pe.Fori(0, 2) as i:
                for slot in range(2):
                    pe.wait_ge(unit_ready, i * 2 + U_AQK + slot + 1)
                    for t in range(2):
                        pe.wait_ge(in6_left, i * 4 + 2 * slot + t + 1)
                        channel_tile(wh[slot], wl[slot], t, CHUNKS2, 2 * t).then_inc(in6_tile, 1)
            pe.wait_ge(f_split, 4)
            pe.wait_ge(in6_left, N_QK + 1)
            channel_tile(fh, fl, 0, CHUNKS2, 0).then_inc(in6_tile, 1)
            for slot in range(2):
                pe.wait_ge(unit_ready, U_AV + slot + 1)
                for j in range(NX):
                    q = slot * NX + j
                    pe.wait_ge(v6_left, q + 1)
                    token_tile(slot, j * P, 4 + j % 4).then_inc(v6_tile, 1)
            for slot in range(2):
                pe.wait_ge(unit_ready, U_AU + slot + 1)
                for t in range(2):
                    q = N_QK + 1 + 2 * slot + t
                    pe.wait_ge(in6_left, q + 1)
                    channel_tile(wh[slot], wl[slot], t, CHUNKS2, 2 * (q % 2)).then_inc(in6_tile, 1)

        def attn_in_scalar(act):
            act.wait_ge(dense_done, Y5 + NX)
            for i in range(N_QK):
                act.wait_ge(in6_tile, i + 1)
                nc.scalar.activation(aqk[:, i, :], banks(2 * (i % 2), 2), ACT.Copy, scale=-AD ** -0.5 if i < 4 else 1.0)\
                    .then_inc(in6_left, 1)
            act.wait_ge(f_in, 32)
            act.wait_ge(in6_tile, N_QK + 1)
            nc.scalar.activation(f_soft[:], banks(0, 2)[0:AH, :], ACT.Abs, bias=B_F).then_inc(f_abs, 1)
            act.wait_ge(f_abs, 1)
            act_own.step(act, nc.scalar.activation(f_soft[:], f_soft[:], ACT.Exp, scale=-1.0))
            nc.scalar.activation(f_soft[:], f_soft[:], ACT.Ln, bias=1.0).then_inc(f_soft_ready, 1)
            for q in range(2 * NX):
                half, j = divmod(q, NX)
                act.wait_ge(v6_tile, q + 1)
                nc.scalar.copy(v6[:, j, half * UNIT:(half + 1) * UNIT], PS[:, 4 + j % 4, 0:UNIT]).then_inc(v6_left, 1)
            act.wait_ge(unit_ready, U_FFN)
            for g in range(4):
                q = N_QK + 1 + g
                act.wait_ge(in6_tile, q + 1)
                nc.scalar.copy(pool_u[:, g, :], banks(2 * (q % 2), 2)).then_inc(in6_left, 1)

        def attn_in_vector(dve):
            nc.vector.memset(stat[:, 90:91], 0.0).then_inc(in6_left, 2)
            nc.vector.memset(stat[:, 91:92], 0.0).then_inc(v6_left, 4)
            for t in range(16):
                nc.vector.memset(inv_count[:, t:t + 1], 1.0 / (t + 1)).then_inc(count_ready, 1)
            dve.wait_ge(f_abs, 1)
            dve_own.step(dve, nc.vector.tensor_scalar(f_logit[:], banks(0, 2)[0:AH, :], B_F, 0.0, ALU.add, ALU.min))
            nc.vector.memset(stat[:, 89:90], 0.0).then_inc(in6_left, 1)
            dve.wait_ge(f_soft_ready, 1)
            nc.vector.tensor_tensor_scan(f_cum[:], f_logit[:], f_soft[:], 0.0, ALU.add, ALU.subtract).then_inc(f_cum_ready, 1)

        pool_ready = sem("pool_ready")
        (score_done, score_ready, prob_ready, prob_turned, prob_left, pv_done) = (
            sem(s) for s in ("score_done", "score_ready", "prob_ready", "prob_turned", "prob_left", "pv_done"))
        (attn_left, pool_done, pool_left, mix_std, mix_n, mix_done, mix_turned, mix_ready) = (
            sem(s) for s in ("attn_left", "pool_done", "pool_left", "mix_std", "mix_n", "mix_done", "mix_turned", "mix_ready"))
        STEPS = NX * AH
        TAIL_LAG = 4

        def low_score(s):
            return stat[:, 56 + s % 2:57 + s % 2]

        def row_sums(i):
            return stat[:, 60 + 8 * (i % 2):68 + 8 * (i % 2)]

        def tails(s, lag, work):
            i, h = divmod(s - lag, AH)
            if h == AH - 1 and i >= 0:
                work(i)

        def attn_tensor(pe):
            pe.wait_ge(causal_ready, 2)
            pe.wait_ge(in6_left, N_QK + 7)
            pe.wait_ge(v6_left, 4 + 2 * NX)

            def scores(s):
                i, h = divmod(s, AH)
                after(pe, score_ready, s - 1)
                rows = slice((h % 2) * AD, (h % 2 + 1) * AD)
                n, bank = (i + 1) * P, 2 * (s % 2)
                for c0 in range(0, n, 512):
                    cn = min(512, n - c0)
                    diag = c0 + cn == n
                    nc.tensor.matmul(PS[:, bank + c0 // 512, 0:cn], aqk[rows, h // 2, i * P:(i + 1) * P],
                                     aqk[rows, 4 + h // 2, c0:c0 + cn], start=True, stop=not diag)
                    if diag:
                        last = nc.tensor.matmul(PS[:, bank + c0 // 512, cn - P:cn], ident[:], causal[:], start=False, stop=True)
                last.then_inc(score_done, 1)

            def turn(s):
                i, h = divmod(s, AH)
                pe.wait_ge(prob_ready, s + 1)
                after(pe, prob_left, s)
                if TAIL_LAG < s:
                    after(pe, mix_ready, (s - 1 - TAIL_LAG + 1) // AH)
                for kb in range(i + 1):
                    last = nc.tensor.transpose(blocks(4)[:, kb, :], score[s % 2][:, kb * P:(kb + 1) * P], ident[:])
                last.then_inc(prob_turned, 1)

            def values(s):
                i, h = divmod(s, AH)
                pe.wait_ge(prob_left, s + 1)
                if h == 0:
                    after(pe, attn_left, i)
                for kb in range(i + 1):
                    last = nc.tensor.matmul(PS[:, 6, h * AD:(h + 1) * AD], prob_t[s % 2][:, kb * P:(kb + 1) * P],
                                            v6[:, kb, h * AD:(h + 1) * AD], start=kb == 0, stop=kb == i)
                last.then_inc(pv_done, 1)

            def pooled(i):
                if i == 0:
                    pe.wait_ge(gain_in, G6 + 64)
                    pe.wait_ge(pool_ready, 4)
                after(pe, pool_left, i)
                for g in range(4):
                    last = nc.tensor.matmul(PS[:, 7, g * P:(g + 1) * P], pool_u[:, g, i * P:(i + 1) * P], w_pool[:, g, :],
                                            start=True, stop=True)
                last.then_inc(pool_done, 1)

            def mixed(i):
                pe.wait_ge(mix_done, i + 1)
                pe.wait_ge(prob_left, min((i + 1) * AH + TAIL_LAG, STEPS))
                turn_row(mix_row[i % 2], P, 4).then_inc(mix_turned, 1)

            for s in range(STEPS + 2):
                if s < STEPS:
                    scores(s)
                if 1 <= s < STEPS + 1:
                    turn(s - 1)
                if s >= 2:
                    values(s - 2)
                    if (s - 2) % AH == AH - 1:
                        pooled((s - 2) // AH)
                tails(s - 1, TAIL_LAG, mixed)
            mixed(NX - 1)

        def attn_scalar(act):
            def probs(s):
                i, h = divmod(s, AH)
                act.wait_ge(score_ready, s + 1)
                x = score[s % 2][:, 0:(i + 1) * P]
                nc.scalar.activation(x, x, ACT.Exp, scale=-1.0, bias=low_score(s), accum_out=row_sums(i)[:, h:h + 1])\
                    .then_inc(prob_ready, 1)

            def leave(s):
                i, h = divmod(s, AH)
                act.wait_ge(prob_turned, s + 1)
                after(act, pv_done, s - 1)
                nc.scalar.copy(prob_t[s % 2][:, 0:(i + 1) * P], banks(4, 2, (i + 1) * P)).then_inc(prob_left, 1)

            def squares(i):
                act.wait_ge(attn_left, i + 1)
                act.wait_ge(pool_left, i + 1)
                after(act, mix_n, 2 * i)
                for half in range(2):
                    act_own.step(act, nc.scalar.activation(mix_sq[:], mix_row[i % 2][:, half * HALF:(half + 1) * HALF], ACT.Square,
                                                           accum_out=stat[:, 78 + half:79 + half]))
                nc.scalar.activation(stat[:, 80:82], stat[:, 78:80], ACT.Sqrt, scale=1 / HALF, bias=RMS_EPS).then_inc(mix_std, 1)

            def mixed(i):
                act.wait_ge(mix_turned, i + 1)
                nc.scalar.copy(mix_t[:, :, i * P:(i + 1) * P], blocks(4)).then_inc(mix_ready, 1)

            for s in range(STEPS + 1):
                if s < STEPS:
                    probs(s)
                if s >= 1:
                    leave(s - 1)
                tails(s - 1, 1, squares)
                tails(s - 1, TAIL_LAG, mixed)
            squares(NX - 1)
            mixed(NX - 1)

        def attn_vector(dve):
            dve.wait_ge(cum_in, 16)
            dve.wait_ge(gain_in, G6 + 64)

            def leave(i):
                dve.wait_ge(pv_done, (i + 1) * AH)
                dve.wait_ge(prob_ready, (i + 1) * AH)
                after(dve, mix_turned, i - 1)
                dve_own.step(dve, nc.vector.reciprocal(row_sums(i), row_sums(i)))
                a = mix_row[i % 2][:, 0:HALF].rearrange("p (h d) -> p h d", h=AH)
                nc.vector.tensor_tensor(a, PS[:, 6, :].rearrange("p (h d) -> p h d", h=AH),
                                        row_sums(i).rearrange("p (h o) -> p h o", o=1).broadcast_to([P, AH, AD]), ALU.mult)\
                    .then_inc(attn_left, 1)
                dve.wait_ge(pool_done, i + 1)
                nc.vector.tensor_tensor(mix_row[i % 2][:, HALF:], PS[:, 7, :], pool_gain[:], ALU.mult).then_inc(pool_left, 1)

            def norm(i):
                dve.wait_ge(mix_std, i + 1)
                dve_own.step(dve, nc.vector.reciprocal(stat[:, 82:84], stat[:, 80:82]))
                for half in range(2):
                    x = mix_row[i % 2][:, half * HALF:(half + 1) * HALF]
                    nc.vector.tensor_scalar(x, x, stat[:, 82 + half:83 + half], None, ALU.mult).then_inc(mix_n, 1)

            for s in range(STEPS):
                i, h = divmod(s, AH)
                n = (i + 1) * P
                dve.wait_ge(score_done, s + 1)
                after(dve, prob_turned, s - 1)
                nc.vector.tensor_tensor_reduce(score[s % 2][:, 0:n], cum_bc[:, h, 0:n], banks(2 * (s % 2), 2, n), 1.0, BIG,
                                               ALU.add, ALU.min, low_score(s)).then_inc(score_ready, 1)
                tails(s, 2, leave)
                tails(s, 3, norm)
            leave(NX - 1)
            norm(NX - 1)

        def attn_pool(pool):
            own = pool_own
            pool.wait_ge(count_ready, 16)
            pool.wait_ge(in6_left, N_QK + 7)
            for g, w in enumerate((2, 4, 8, 16)):
                src, s = pool_u[:, g, :], 1
                for r in range(g + 1):
                    dst = pool_tmp[r % 2]
                    own.step(pool, nc.gpsimd.tensor_copy(dst[:, 0:s], src[:, 0:s]))
                    own.step(pool, nc.gpsimd.tensor_tensor(dst[:, s:], src[:, s:], src[:, 0:SEQ - s], ALU.add))
                    src, s = dst, 2 * s
                own.step(pool, nc.gpsimd.tensor_tensor(src[:, 0:w - 1], src[:, 0:w - 1], inv_count[:, 0:w - 1], ALU.mult))
                own.step(pool, nc.gpsimd.tensor_scalar(src[:, w - 1:], src[:, w - 1:], 1.0 / w, None, ALU.mult))
                nc.gpsimd.tensor_tensor(pool_u[:, g, :], src[:], pool_u[:, g, :], ALU.subtract).then_inc(pool_ready, 1)
                pool.wait_ge(pool_ready, g + 1)
            pool.wait_ge(gain_in, G6 + 64)
            for i in range(NX):
                pool.wait_ge(mix_n, 2 * i + 2)
                nc.gpsimd.tensor_tensor(mix_row[i % 2][:], mix_row[i % 2][:], mix_gain[:], ALU.mult).then_inc(mix_done, 1)

        (y7_std, h3_done, h3_std, n7_done) = (
            sem(s) for s in ("y7_std", "h3_done", "h3_std", "n7_done"))

        def mix_out_sync(sp):
            sp.wait_ge(in6_tile, N_QK + 5)
            sp.dma_start(w_mix_out[:], I["w_out_2"][0].rearrange("(k p) n -> p k n", p=P)).then_inc(matrix_in, 16)
            sp.wait_ge(score_done, STEPS)
            for s in range(2):
                sp.dma_start(rows7[s][:], row_tile(h2_rows, s)).then_inc(rows_in[s], 16)
            for s, name in enumerate(("g_mix_post_2", "g_ffn_pre_2")):
                sp.dma_start(gain7[s][:], bcast_row(I[name][0], D)).then_inc(gain_in, 16)
            sp.wait_ge(pool_done, NX)
            load_unit(sp, U_FFN)
            for j in range(NX):
                s = j % 2
                sp.wait_ge(h3_done, j + 1)
                sp.dma_start(row_tile(h3_rows, j), rows7[s][:]).then_inc(rows_out[s], 16)
                if j + 2 < NX:
                    sp.wait_ge(rows_out[s], H3_OUT + 16 * (j // 2 + 1))
                    sp.wait_ge(n7_done, j + 1)
                    sp.dma_start(rows7[s][:], row_tile(h2_rows, j + 2)).then_inc(rows_in[s], 16)
            for s in range(2):
                sp.wait_ge(rows_out[s], H3_OUT + 64)

        def mix_out_tensor(pe):
            pe.wait_ge(matrix_in, W7 + 16)

            def turn(j):
                pe.wait_ge(n7_done, j + 1)
                after(pe, part_lo, j - 1, N7)
                turn_row(normed7[j % 2], P, 4 + 2 * (j % 2)).then_inc(turned, 1)

            for j in range(NX):
                pe.wait_ge(mix_ready, j + 1)
                after(pe, dense_left, j - 1, Y7)
                if j == 0:
                    pe.wait_ge(score_ready, STEPS)
                dense_rows(lambda k: mix_t[:, k, j * P:(j + 1) * P], w_mix_out, P, 2 * (j % 2)).then_inc(dense_done, 1)
                if j == 0:
                    pe.wait_ge(mix_ready, NX)
                    pe.wait_ge(pool_left, NX)
                else:
                    turn(j - 1)
            turn(NX - 1)

        def mix_out_scalar(act):
            def high(j):
                act.wait_ge(turned, N7 + j + 1)
                nc.scalar.copy(xh7[:, :, j * P:(j + 1) * P], blocks(4 + 2 * (j % 2))).then_inc(part_hi, 1)

            for j in range(NX):
                act.wait_ge(dense_done, Y7 + j + 1)
                after(act, h3_done, j - 1)
                act_own.step(act, nc.scalar.activation(scaled7[j % 2][:], banks(2 * (j % 2), 2), ACT.Square, accum_out=stat[:, 0:1]))
                nc.scalar.activation(stat[:, 1:2], stat[:, 0:1], ACT.Sqrt, scale=1 / D, bias=RMS_EPS).then_inc(y7_std, 1)
                act.wait_ge(h3_done, j + 1)
                after(act, turned, j - 1, N7)
                act_own.step(act, nc.scalar.activation(normed7[j % 2][:], rows7[j % 2][:], ACT.Square, accum_out=stat[:, 16:17]))
                nc.scalar.activation(stat[:, 17:18], stat[:, 16:17], ACT.Sqrt, scale=1 / D, bias=RMS_EPS).then_inc(h3_std, 1)
                if j >= 1:
                    high(j - 1)
            high(NX - 1)

        def mix_out_vector(dve):
            dve.wait_ge(gain_in, G7 + 32)

            def low(j):
                cols = slice(j * P, (j + 1) * P)
                dve.wait_ge(part_hi, N7 + j + 1)
                nc.vector.tensor_tensor(xl7[:, :, cols], blocks(4 + 2 * (j % 2)), xh7[:, :, cols].bitcast(F32), ALU.subtract)\
                    .then_inc(part_lo, 1)

            for j in range(NX):
                dve.wait_ge(y7_std, j + 1)
                dve_own.step(dve, nc.vector.reciprocal(stat[:, 2:3], stat[:, 1:2]))
                nc.vector.scalar_tensor_tensor(out=scaled7[j % 2][:], in0=banks(2 * (j % 2), 2), scalar=stat[:, 2:3],
                                               in1=gain7[0][:], op0=ALU.mult, op1=ALU.mult).then_inc(dense_left, 1)
                if j >= 1:
                    low(j - 1)
                dve.wait_ge(h3_std, j + 1)
                dve_own.step(dve, nc.vector.reciprocal(stat[:, 18:19], stat[:, 17:18]))
                nc.vector.scalar_tensor_tensor(out=normed7[j % 2][:], in0=rows7[j % 2][:], scalar=stat[:, 18:19],
                                               in1=gain7[1][:], op0=ALU.mult, op1=ALU.mult).then_inc(n7_done, 1)
            low(NX - 1)

        def mix_out_pool(pool):
            for j in range(NX):
                x = rows7[j % 2]
                pool.wait_ge(rows_in[j % 2], ROWS7[j % 2] + 16 * (j // 2 + 1))
                pool.wait_ge(dense_left, Y7 + j + 1)
                nc.gpsimd.tensor_tensor(x[:], x[:], scaled7[j % 2][:], ALU.add).then_inc(h3_done, 1)

        (ff_tile, gate_left, up_left, ff_hi, ff_lo, dn_tile, dn_left, acc_zero) = (
            sem(s) for s in ("ff_tile", "gate_left", "up_left", "ff_hi", "ff_lo", "dn_tile", "dn_left", "acc_zero"))
        HALVES = 2 * NX

        def ffn_sync(sp):
            for u in range(U_FFN + 1, U_END):
                load_unit(sp, u)

        def ffn_pool(pool):
            pool.wait_ge(dense_done, Y7 + NX)
            split_unit(pool, u_gate(0), 0)
            split_unit(pool, u_gate(0) + 1, 1)
            pool.wait_ge(turned, N7 + NX)
            nc.gpsimd.memset(ff_acc[:], 0.0).then_inc(acc_zero, 1)
            for g in range(1, FGROUPS):
                pool.wait_ge(ff_tile, g * 4 - 2)
                split_unit(pool, u_gate(g), 0)
                pool.wait_ge(ff_tile, g * 4)
                split_unit(pool, u_gate(g) + 1, 1)
                after(pool, dn_tile, (g - 1) * HALVES)
                split_unit(pool, u_down(g - 1), 2)
            pool.wait_ge(dn_tile, (FGROUPS - 1) * HALVES)
            split_unit(pool, u_down(FGROUPS - 1), 2)

        def ffn_tensor(pe):
            def gate_up(g, gate_unit):
                x = (xh7, xl7)
                tile = lambda slot, t, bank: channel_tile(wh[slot], wl[slot], t, CHUNKS2, bank, x).then_inc(ff_tile, 1)
                first = isinstance(g, int)
                pe.wait_ge(unit_ready, gate_unit + 1)
                if not first:
                    pe.wait_ge(up_left, g * 2)
                tile(0, 0, 0)
                if not first:
                    pe.wait_ge(gate_left, g * 2)
                tile(0, 1, 2)
                pe.wait_ge(unit_ready, gate_unit + 2)
                if not first:
                    pe.wait_ge(up_left, g * 2 - 1)
                tile(1, 0, 4)
                pe.wait_ge(gate_left, g * 2 + 1)
                tile(1, 1, 0)

            def down(g, b, down_unit):
                pe.wait_ge(unit_ready, down_unit + 1)
                pe.wait_ge(ff_lo, g * 2 + 2)
                for j in range(NX):
                    cols = slice(j * P, (j + 1) * P)
                    for half in range(2):
                        pe.wait_ge(dn_left, g * HALVES + (2 * j + half + 1))
                        n = slice(half * HALF, (half + 1) * HALF)
                        products([(ffh[b][:, f, cols], ffl[b][:, f, cols], wh_down[:, f, n], wl_down[:, f, n]) for f in range(2)],
                                 [(0, HALF)], lambda c, cn: PS[:, 6 + half, :]).then_inc(dn_tile, 1)

            pe.wait_ge(part_lo, N7 + NX)
            pe.wait_ge(dense_left, Y7 + NX)
            gate_up(0, u_gate(0))
            with pe.Fori(0, FGROUPS // 2) as i:
                gate_up(i * 2 + 1, i * 6 + u_gate(1))
                down(i * 2, 0, i * 6 + u_down(0))
                gate_up(i * 2 + 2, i * 6 + u_gate(2))
                down(i * 2 + 1, 1, i * 6 + u_down(1))
            down(FGROUPS - 1, 0, u_down(FGROUPS - 1))

        def ffn_scalar(act):
            def group(g, b):
                for t in range(2):
                    act.wait_ge(ff_tile, g * 4 + t + 1)
                    nc.scalar.activation(ff_silu[:, t, :], banks(2 * t, 2), ACT.Silu).then_inc(gate_left, 1)
                for t in range(2):
                    act.wait_ge(up_left, g * 2 + t + 1)
                    nc.scalar.copy(ffh[b][:, t, :], ff_prod[t][:]).then_inc(ff_hi, 1)

            group(0, 0)
            with act.Fori(0, FGROUPS // 2) as i:
                group(i * 2 + 1, 1)
                group(i * 2 + 2, 0)

        def ffn_vector(dve):
            nc.vector.memset(stat[:, 88:89], 0.0).then_inc(dn_left, 2)

            def group(g, b):
                for t in range(2):
                    dve.wait_ge(ff_tile, g * 4 + t + 3)
                    dve.wait_ge(gate_left, g * 2 + t + 1)
                    if not isinstance(g, int):
                        dve.wait_ge(ff_lo, g * 2 + t - 1)
                    nc.vector.tensor_tensor(ff_prod[t][:], ff_silu[:, t, :], banks(4 * (1 - t), 2), ALU.mult).then_inc(up_left, 1)
                for t in range(2):
                    dve.wait_ge(ff_hi, g * 2 + t + 1)
                    nc.vector.tensor_tensor(ffl[b][:, t, :], ff_prod[t][:], ffh[b][:, t, :].bitcast(F32), ALU.subtract)\
                        .then_inc(ff_lo, 1)

            def add_down(g):
                for q in range(HALVES):
                    j, half = divmod(q, 2)
                    dve.wait_ge(dn_tile, g * HALVES + q + 1)
                    x = ff_acc[:, j, half * HALF:(half + 1) * HALF]
                    nc.vector.tensor_tensor(x, x, PS[:, 6 + half, :], ALU.add).then_inc(dn_left, 1)

            group(0, 0)
            dve.wait_ge(acc_zero, 1)
            with dve.Fori(0, FGROUPS // 2) as i:
                group(i * 2 + 1, 1)
                add_down(i * 2)
                group(i * 2 + 2, 0)
                add_down(i * 2 + 1)
            add_down(FGROUPS - 1)

        p_in = sem("p_in")
        (p_turned, p_ready, ff_std, ff_n, h4_done, h4_turned, act9_ready) = (
            sem(s) for s in ("p_turned", "p_ready", "ff_std", "ff_n", "h4_done", "h4_turned", "act9_ready"))
        (e_done, e_std, e_n, gated9, out_ready) = (
            sem(s) for s in ("e_done", "e_std", "e_n", "gated9", "out_ready"))

        def final_sync(sp):
            sp.wait_ge(ff_tile, 4 * FGROUPS)
            sp.dma_start(p_stage[:], I["p_2"][0, 0].rearrange("(j p) n -> p j n", p=P)).then_inc(p_in, 16)
            sp.dma_start(w_ple_proj[:], I["w_ple_proj_2"][0].rearrange("(k p) n -> p k n", p=P)).then_inc(matrix_in, 16)
            sp.dma_start(w_ple_gate[:], I["w_ple_gate_2"][0].rearrange("(k p) n -> p k n", p=P)).then_inc(matrix_in, 16)
            for s, name in enumerate(("g_ffn_post_2", "g_ple_2")):
                sp.dma_start(gain9[s][:], bcast_row(I[name][0], D)).then_inc(gain_in, 16)
            for s in range(2):
                sp.dma_start(rows9[s][:], row_tile(h3_rows, s)).then_inc(rows_in[s], 16)
            for j in range(NX):
                s = j % 2
                if j + 2 < NX:
                    sp.wait_ge(h4_done, j + 1)
                    sp.dma_start(rows9[s][:], row_tile(h3_rows, j + 2)).then_inc(rows_in[s], 16)
                sp.wait_ge(out_ready, j + 1)
                sp.dma_start(row_tile(out[0], j), out_row[s][:]).then_inc(rows_out[s], 16)
            for s in range(2):
                sp.wait_ge(rows_out[s], OUT + 64)

        def final_tensor(pe):
            pe.wait_ge(p_in, 16)
            pe.wait_ge(up_left, 2 * FGROUPS)
            pe.wait_ge(gate_left, 2 * FGROUPS)
            for k in range(2):
                for j in range(NX):
                    last = nc.tensor.transpose(PS[:, 2 * k + j // 4, (j % 4) * P:(j % 4 + 1) * P], p_stage[:, j, k * P:(k + 1) * P],
                                               ident[:])
            last.then_inc(p_turned, 1)
            pe.wait_ge(matrix_in, W9 + 32)
            pe.wait_ge(p_ready, 1)
            pe.wait_ge(dn_left, 2 + FGROUPS * HALVES)
            for j in range(NX):
                after(pe, e_n, j)
                for k in range(2):
                    for half in range(2):
                        last = nc.tensor.matmul(PS[:, 6 + half, :], p_t[:, k, j * P:(j + 1) * P],
                                                w_ple_proj[:, k, half * HALF:(half + 1) * HALF], start=k == 0, stop=k == 1)
                last.then_inc(e_done, 1)
                pe.wait_ge(h4_done, j + 1)
                after(pe, act9_ready, j)
                turn_row(ff_acc[:, j, :], P, 4).then_inc(h4_turned, 1)
                pe.wait_ge(act9_ready, j + 1)
                after(pe, dense_left, j - 1, Y9)
                dense_rows(lambda k: act9[j % 2][:, k, :], w_ple_gate, P, 2 * (j % 2)).then_inc(dense_done, 1)

        def final_scalar(act):
            act.wait_ge(p_turned, 1)
            nc.scalar.copy(p_t[:].rearrange("p k t -> p (k t)"), banks(0, 4, 2048)).then_inc(p_ready, 1)
            act.wait_ge(gain_in, G9 + 32)

            def ff_norm(j):
                act.wait_ge(dn_left, 2 + (FGROUPS - 1) * HALVES + 2 * j + 2)
                after(act, ff_n, j)
                act_own.step(act, nc.scalar.activation(sq9[:], ff_acc[:, j, :], ACT.Square, accum_out=stat[:, 0:1]))
                nc.scalar.activation(stat[:, 1:2], stat[:, 0:1], ACT.Sqrt, scale=1 / D, bias=RMS_EPS).then_inc(ff_std, 1)

            ff_norm(0)
            for j in range(NX):
                act.wait_ge(e_done, j + 1)
                act_own.step(act, nc.scalar.activation(sq9e[:], banks(6, 2), ACT.Square, accum_out=stat[:, 3:4]))
                after(act, e_n, j)
                nc.scalar.activation(stat[:, 4:5], stat[:, 3:4], ACT.Sqrt, scale=1 / D, bias=RMS_EPS).then_inc(e_std, 1)
                act.wait_ge(h4_turned, j + 1)
                after(act, dense_done, j - 1, Y9)
                nc.scalar.copy(act9[j % 2][:], blocks(4)).then_inc(act9_ready, 1)
                if j + 1 < NX:
                    ff_norm(j + 1)
                act.wait_ge(dense_done, Y9 + j + 1)
                after(act, rows_out[j % 2], 16 * (j // 2), OUT)
                nc.scalar.activation(out_row[j % 2][:], banks(2 * (j % 2), 2), ACT.Sigmoid).then_inc(dense_left, 1)

        def final_vector(dve):
            dve.wait_ge(gain_in, G9 + 32)

            def ff_norm(j):
                dve.wait_ge(ff_std, j + 1)
                dve_own.step(dve, nc.vector.reciprocal(stat[:, 2:3], stat[:, 1:2]))
                x = ff_acc[:, j, :]
                nc.vector.scalar_tensor_tensor(out=x, in0=x, scalar=stat[:, 2:3], in1=gain9[0][:], op0=ALU.mult, op1=ALU.mult)\
                    .then_inc(ff_n, 1)

            ff_norm(0)
            for j in range(NX):
                dve.wait_ge(e_std, j + 1)
                after(dve, gated9, j)
                dve_own.step(dve, nc.vector.reciprocal(stat[:, 5:6], stat[:, 4:5]))
                nc.vector.scalar_tensor_tensor(out=e_row[:], in0=banks(6, 2), scalar=stat[:, 5:6], in1=gain9[1][:],
                                               op0=ALU.mult, op1=ALU.mult).then_inc(e_n, 1)
                if j + 1 < NX:
                    ff_norm(j + 1)
                dve.wait_ge(e_n, j + 1)
                dve.wait_ge(dense_left, Y9 + j + 1)
                nc.vector.tensor_tensor(out_row[j % 2][:], out_row[j % 2][:], e_row[:], ALU.mult).then_inc(gated9, 1)

        def final_pool(pool):
            for j in range(NX):
                if j == 0:
                    pool.wait_ge(rows_in[0], ROWS9[0] + 16)
                    pool.wait_ge(ff_n, 1)
                    nc.gpsimd.tensor_tensor(ff_acc[:, 0, :], ff_acc[:, 0, :], rows9[0][:], ALU.add).then_inc(h4_done, 1)
                if j + 1 < NX:
                    n = j + 1
                    pool.wait_ge(rows_in[n % 2], ROWS9[n % 2] + 16 * (n // 2 + 1))
                    pool.wait_ge(ff_n, n + 1)
                    nc.gpsimd.tensor_tensor(ff_acc[:, n, :], ff_acc[:, n, :], rows9[n % 2][:], ALU.add).then_inc(h4_done, 1)
                pool.wait_ge(gated9, j + 1)
                pool.wait_ge(h4_done, j + 1)
                nc.gpsimd.tensor_tensor(out_row[j % 2][:], out_row[j % 2][:], ff_acc[:, j, :], ALU.add).then_inc(out_ready, 1)

        block = ctx.enter_context(nc.Block())

        @block.sync
        def _(sp):
            inputs_sync(sp)
            conv_in_sync(sp)
            conv_out_sync(sp)
            gla_in_sync(sp)
            gla_out_sync(sp)
            attn_in_sync(sp)
            mix_out_sync(sp)
            ffn_sync(sp)
            final_sync(sp)

        @block.tensor
        def _(pe):
            inputs_tensor(pe)
            conv_in_tensor(pe)
            conv_norm_tensor(pe)
            conv_out_tensor(pe)
            gla_in_tensor(pe)
            gla_tensor(pe)
            gla_gate_tensor(pe)
            gla_out_tensor(pe)
            attn_in_tensor(pe)
            attn_tensor(pe)
            mix_out_tensor(pe)
            ffn_tensor(pe)
            final_tensor(pe)

        @block.scalar
        def _(act):
            inputs_scalar(act)
            conv_in_scalar(act)
            conv_norm_scalar(act)
            conv_out_scalar(act)
            gla_in_scalar(act)
            gla_scalar(act)
            gla_gate_scalar(act)
            gla_out_scalar(act)
            attn_in_scalar(act)
            attn_scalar(act)
            mix_out_scalar(act)
            ffn_scalar(act)
            final_scalar(act)

        @block.vector
        def _(dve):
            inputs_vector(dve)
            conv_vector(dve)
            conv_norm_vector(dve)
            conv_out_vector(dve)
            gla_in_vector(dve)
            gla_vector(dve)
            gla_gate_vector(dve)
            gla_out_vector(dve)
            attn_in_vector(dve)
            attn_vector(dve)
            mix_out_vector(dve)
            ffn_vector(dve)
            final_vector(dve)

        @block.gpsimd
        def _(pool):
            consts_pool(pool)
            conv_in_pool(pool)
            conv_out_pool(pool)
            gla_in_pool(pool)
            gla_pool(pool)
            gla_gate_pool(pool)
            gla_out_pool(pool)
            attn_in_pool(pool)
            attn_pool(pool)
            mix_out_pool(pool)
            ffn_pool(pool)
            final_pool(pool)


_INS = ['x', 'meta', 'conv_w_in', 'conv_b_in', 'conv_w_dw', 'conv_b_dw', 'conv_norm_g', 'conv_norm_b', 'conv_w_out',
        'conv_b_out', 'gla_w_in', 'gla_w_a2', 'gla_b_a', 'gla_norm_g', 'gla_w_out', 'post_ln_g', 'post_ln_b', 'p_2',
        'g_mix_pre_2', 'w_in_2', 'b_forget_2', 'g_attn_grp_2', 'g_pool_grp_2', 'w_pool_2', 'pool_scale_2', 'w_out_2',
        'g_mix_post_2', 'g_ffn_pre_2', 'w_ffn_gate_2', 'w_ffn_up_2', 'w_ffn_down_2', 'g_ffn_post_2', 'w_ple_proj_2',
        'g_ple_2', 'w_ple_gate_2']


def kernel(**inputs):
    import numpy as _np
    import concourse.bacc as _bacc
    from concourse import mybir as _mybir
    from concourse.bass_utils import run_bass_kernel_spmd as _run

    nc = _bacc.Bacc("TRN2", target_bir_lowering=False, num_devices=1)
    arrays, aps = {}, {}
    for name in _INS:
        a = _np.ascontiguousarray(inputs[name])
        arrays[f"in_{name}_dram"] = a
        aps[name] = nc.dram_tensor(f"in_{name}_dram", a.shape, _mybir.dt.from_np(a.dtype), kind="ExternalInput").ap()
    out = nc.dram_tensor("out_0_dram", (1, SEQ, D), F32, kind="ExternalOutput").ap()
    hybrid_block(nc, aps, out)
    r = _run(nc, [arrays], core_ids=[0])
    return r.results[0]["out_0_dram"]
```

```python
from contextlib import ExitStack

import concourse.bass as bass
from concourse import mybir

ALU = mybir.AluOpType
ACT = mybir.ActivationFunctionType
F32 = mybir.dt.float32
F32R = mybir.dt.float32r
I32 = mybir.dt.int32

P = 128
D = 1024
SEQ = 1024
META = 16
T = META + SEQ
KT = D // P
NX = SEQ // P
HALF = 512
TAPS = 31
SIDE_TAPS = 7
PAD = TAPS - 1
ALPHA = 4 ** 0.25
LN_EPS = 1e-5
RMS_EPS = 1e-6
UNIT = 256
GH, GK, GV = 4, 128, 256
TAU = 16.0
RANK = 16
LEVELS = 7
AH, AD = 8, 64
FGROUPS = 11
MASKED = 1e30
BIG = 3e38

TILES = [(0, META)] + [(META + P * j, P) for j in range(NX)]
CHUNKS3 = [(0, 352), (352, 352), (704, 336)]
CHUNKS2 = [(0, 512), (512, 512)]

U_CONV, U_GQK, U_GV, U_GR, U_AQK, U_AV, U_AU, U_FFN, U_END = 0, 12, 16, 20, 24, 28, 30, 32, 65


def u_gate(g):
    return U_FFN if g == 0 else U_FFN + 2 + 3 * (g - 1)


def u_down(g):
    return U_FFN + 4 + 3 * g if g < FGROUPS - 1 else U_END - 1


class Chain:

    def __init__(self, sem):
        self.sem, self.n = sem, 0

    def step(self, eng, ins):
        self.n += 1
        ins.then_inc(self.sem, 1)
        eng.wait_ge(self.sem, self.n)


def after(eng, sem, value, base=0):
    if value > 0:
        eng.wait_ge(sem, base + value)


def hybrid_block(nc, I, out):
    ctx = ExitStack()
    with ctx:
        base = (nc.sbuf_base + 31) // 32 * 32

        def at(name, shape, off, dt=F32):
            return nc.alloc_sbuf_tensor_at(name, shape, dt, offset=base + off)

        def sem(name):
            return ctx.enter_context(nc.semaphore(name))

        C0 = 0
        A0 = 3200
        A1 = A0 + KT * T * 4
        S0 = A0 + 2 * KT * T * 4
        SLOT = 2 * KT * UNIT * 4
        W0 = S0 + 3 * SLOT
        O0 = W0 + 16384
        Z0 = O0 + KT * T * 4

        ident = at("ident", [P, P], C0)
        ones_mean = at("ones_mean", [P, P], C0 + 512)
        NV = TAPS + 6
        conv_vec = at("conv_vec", [P, KT, NV], C0 + 1024)
        causal = at("causal", [P, P], C0 + 1024)
        inv_count = at("inv_count", [P, 16], C0 + 2208)
        stat = at("stat", [P, 96], C0 + 2272)
        a1_raw = at("a1_raw", [P, KT, RANK], C0 + 2656)
        f_raw = at("f_raw", [P, KT, AH], C0 + 2656)

        xh = at("xh", [P, KT, T], A0, F32R)
        xl = at("xl", [P, KT, T], A0 + KT * T * 4, F32R)
        raw = at("raw", [P, KT, UNIT], W0)
        raw_down = raw[:].rearrange("p k n -> p (k n)").rearrange("p (f n) -> p f n", f=2)
        wh = [at(f"wh{s}", [P, KT, UNIT], S0 + s * SLOT, F32R) for s in range(3)]
        wl = [at(f"wl{s}", [P, KT, UNIT], S0 + s * SLOT + SLOT // 2, F32R) for s in range(3)]
        wh_down = wh[2][:].rearrange("p k n -> p (k n)").rearrange("p (f n) -> p f n", f=2)
        wl_down = wl[2][:].rearrange("p k n -> p (k n)").rearrange("p (f n) -> p f n", f=2)

        x_stage = at("x_stage", [P, 4, D], O0)
        vec_rows = at("vec_rows", [NV, D], Z0 + KT * (T + PAD) * 4)
        silu_z = at("silu_z", [P, KT, T], O0)
        glu = at("glu", [P, KT, T + PAD], Z0)
        gate_part = at("gate_part", [P, T], Z0 + KT * (T + PAD) * 4 + T * 4)
        tap_sum = [at(f"tap_sum{e}", [P, T], S0 + 2 * SLOT + e * T * 4) for e in range(2)]
        tap_part = [at("tap_part0", [P, T], W0 + 8192), at("tap_part1", [P, T], O0 + (KT - 1) * T * 4)]
        side_sum = [at("side_sum0", [P, T], S0 + 2 * SLOT + 2 * T * 4), at("side_sum1", [P, T], Z0 + KT * (T + PAD) * 4)]
        conv_sq = at("conv_sq", [P, KT, 352], S0 + 2 * SLOT)
        conv_std = at("conv_std", [P, T], Z0 + KT * (T + PAD) * 4)
        w_conv_out = at("w_conv_out", [P, KT, D], S0)
        rows3 = [at(f"rows3_{s}", [P, D], W0 + 8192 + s * 4096) for s in range(2)]
        gain3 = [at(f"gain3_{s}", [P, D], O0 + s * 4096) for s in range(3)]

        qk = at("qk", [P, 2 * GH, T], Z0)
        arg_a = at("arg_a", [P, 4, GH, P], Z0 + 33280)
        arg_b = at("arg_b", [P, LEVELS - 4, GH, P], W0)
        v_meta = at("v_meta", [META, D], Z0 + 33280)
        a1h = at("a1h", [P, KT, P], O0, F32R)
        a1l = at("a1l", [P, KT, P], O0 + 4096, F32R)
        a1_pad = at("a1_pad", [P, KT, P], O0 + 8192)
        decay = at("decay", [P, GH, P], Z0 + 41472)
        v_rows = at("v_rows", [P, NX, D], O0)
        k_decayed = at("k_decayed", [P, GH, P], S0 + 2 * SLOT)
        k_rows = at("k_rows", [P, GH, P], S0 + 2 * SLOT + 2048)
        att = at("att", [P, GH, P], S0 + 2 * SLOT + 4096)
        state = at("state", [P, GH, GV], S0 + 2 * SLOT + 6144)
        a1 = at("a1", [33, T], S0 + 2 * SLOT + 10240)
        pair_mask = at("pair_mask", [P, LEVELS, 64], S0 + 2 * SLOT + 14400, I32)
        pair_mask_f = at("pair_mask_f", [P, LEVELS, 64], Z0 + 33280)
        w_a2 = at("w_a2", [33, GH * GK], W0 + 8192)
        q_decayed = at("q_decayed", [P, GH, P], W0 + 8192 + 2048)
        soft = at("soft", [P, GH, P], W0 + 8192 + 4096)
        norm_bc = at("norm_bc", [P, GV], W0 + 8192 + 6144)
        o_junk = at("o_junk", [P, GV], W0 + 8192 + 7168)
        r_silu = [at(f"r_silu{s}", [P, GV], Z0 + 33280 + s * 1024) for s in range(2)]
        w_gla_out = at("w_gla_out", [P, KT, D], Z0)
        act5 = [at(f"act5_{s}", [P, KT, P], Z0 + 33280 + s * 4096) for s in range(2)]
        rows5 = [at(f"rows5_{s}", [P, D], S0 + 2 * SLOT + s * 4096) for s in range(2)]
        normed5 = at("normed5", [P, D], S0 + 2 * SLOT + 8192)
        gain5 = [at("gain5_0", [P, D], W0 + 8192), at("gain5_1", [P, D], W0 + 12288),
                 at("gain5_2", [P, D], S0 + 2 * SLOT + 12288)]

        aqk = at("aqk", [P, KT, SEQ], Z0)
        fh = at("fh", [P, KT, P], Z0 + 32768, F32R)
        fl = at("fl", [P, KT, P], Z0 + 32768 + 4096, F32R)
        f_pad = at("f_pad", [P, KT, P], O0 + 12288)
        f_logit = at("f_logit", [AH, SEQ], O0)
        f_soft = at("f_soft", [AH, SEQ], O0 + 4096)
        f_cum = at("f_cum", [AH, SEQ], O0 + 8192)
        v6 = at("v6", [P, NX, HALF], S0 + 2 * SLOT)
        pool_u = at("pool_u", [P, 4, SEQ], W0)
        cum_bc = at("cum_bc", [P, AH, SEQ], O0)
        score = [at(f"score{s}", [P, SEQ], A0 + 32768 + s * 4096) for s in range(3)]
        prob_t = [at(f"prob_t{s}", [P, SEQ], A0 + 45056 + s * 4096) for s in range(2)]
        mix_row = [at(f"mix_row{s}", [P, D], A0 + 53248 + s * 4096) for s in range(2)]
        pool_tmp = [at(f"pool_tmp{s}", [P, SEQ], A0 + s * 4096) for s in range(2)]
        mix_gain = at("mix_gain", [P, D], Z0 + 32768)
        pool_gain = at("pool_gain", [P, HALF], Z0 + 32768 + 4096)
        w_pool = at("w_pool", [P, 4, P], Z0 + 32768 + 6144)
        mix_t = at("mix_t", [P, KT, SEQ], A0)
        mix_sq = at("mix_sq", [P, HALF], Z0 + 40960)
        w_mix_out = at("w_mix_out", [P, KT, D], S0)
        rows7 = [at(f"rows7_{s}", [P, D], Z0 + s * 4096) for s in range(2)]
        scaled7 = [at(f"scaled7_{s}", [P, D], Z0 + 8192 + s * 4096) for s in range(2)]
        gain7 = [at(f"gain7_{s}", [P, D], Z0 + 16384 + s * 4096) for s in range(2)]
        normed7 = [at(f"normed7_{s}", [P, D], Z0 + 24576 + s * 4096) for s in range(2)]
        xh7 = at("xh7", [P, KT, T], O0, F32R)
        xl7 = at("xl7", [P, KT, T], A0 + KT * T * 4, F32R)

        ffh = [at(f"ffh{b}", [P, 2, SEQ], A0 + b * 16384, F32R) for b in range(2)]
        ffl = [at(f"ffl{b}", [P, 2, SEQ], A0 + b * 16384 + 8192, F32R) for b in range(2)]
        ff_acc = at("ff_acc", [P, NX, D], Z0)
        ff_silu = at("ff_silu", [P, 2, SEQ], Z0 + 32768)
        ff_prod = [at(f"ff_prod{t}", [P, SEQ], W0 + 8192 + t * 4096) for t in range(2)]

        rows9 = [at(f"rows9_{s}", [P, D], A1 + s * 4096) for s in range(2)]
        w_ple_gate = at("w_ple_gate", [P, KT, D], O0)
        w_ple_proj = at("w_ple_proj", [P, 2, D], A1 + 8192)
        p_t = at("p_t", [P, 2, SEQ], A1 + 16384)
        out_row = [at(f"out_row{s}", [P, D], A1 + 24576 + s * 4096) for s in range(2)]
        act9 = [at(f"act9_{s}", [P, KT, P], S0 + s * 4096) for s in range(2)]
        p_stage = at("p_stage", [P, NX, 2 * P], S0 + 8192)
        gain9 = [at(f"gain9_{s}", [P, D], S0 + SLOT + s * 4096) for s in range(2)]
        e_row = at("e_row", [P, D], S0 + SLOT + 8192)
        sq9 = at("sq9", [P, D], S0 + SLOT + 12288)
        sq9e = at("sq9e", [P, D], W0 + 8192)

        PS = ctx.enter_context(nc.psum_tensor("PS", [P, 8, 512], F32))

        def banks(b, n, cols=None):
            return PS[:, b:b + n, :].rearrange("p b n -> p (b n)")[:, 0:cols or n * 512]

        def blocks(b):
            return PS[:, b:b + 2, :].rearrange("p b (q n) -> p (b q) n", n=P)

        h1_rows = nc.dram_tensor("h1_rows", (SEQ, D), F32, kind="Internal").ap()
        h2_rows = nc.dram_tensor("h2_rows", (SEQ, D), F32, kind="Internal").ap()
        h3_rows = nc.dram_tensor("h3_rows", (SEQ, D), F32, kind="Internal").ap()
        cum_rows = nc.dram_tensor("cum_rows", (AH, SEQ), F32, kind="Internal").ap()
        x_rows = I["x"][0]
        meta_rows = I["meta"]

        def row_tile(dram, j):
            return dram[j * P:(j + 1) * P, :]

        def bcast_row(vec, n):
            return vec.rearrange("(o n) -> o n", o=1).broadcast_to([P, n])

        def unit_src(w, col):
            return w[:, col:col + UNIT].rearrange("(k p) n -> p k n", p=P)

        raw_ready, unit_hi, unit_ready = sem("raw_ready"), sem("unit_hi"), sem("unit_ready")

        turned, part_hi, part_lo = sem("turned"), sem("part_hi"), sem("part_lo")
        H1, N5, N7 = 9, 18, 26
        dense_done, dense_left = sem("dense_done"), sem("dense_left")
        row_var, row_std = sem("row_var"), sem("row_std")
        Y5, Y7, Y9 = 9, 17, 25
        matrix_in, gain_in = sem("matrix_in"), sem("gain_in")
        W5, W7, W9 = 16, 32, 48
        G5, G6, G7, G9 = 48, 96, 160, 192
        rows_in, rows_out = [sem("rows_in0"), sem("rows_in1")], [sem("rows_out0"), sem("rows_out1")]
        ROWS5, ROWS7, ROWS9 = [80, 64], [144, 128], [208, 192]
        H2_OUT, H3_OUT, OUT = 64, 128, 192
        dve_own, act_own, pool_own = Chain(sem("dve_own")), Chain(sem("act_own")), Chain(sem("pool_own"))

        def load_unit(sp, u):
            after(sp, unit_ready, u)
            if u < 8:
                for s in range(2):
                    sp.dma_start(raw[:, :, s * P:(s + 1) * P], I["conv_w_in"][0][:, u * P + s * D:u * P + s * D + P]
                                       .rearrange("(k p) n -> p k n", p=P)).then_inc(raw_ready, 16)
                return
            if u < U_GQK:
                src = unit_src(I["conv_w_in"][0], 2 * D + (u - 8) * UNIT)
            elif u < U_AQK:
                src = unit_src(I["gla_w_in"][0], (u - U_GQK) * UNIT)
            elif u < U_AU:
                src = unit_src(I["w_in_2"][0], (u - U_AQK) * UNIT)
            elif u < U_FFN:
                src = unit_src(I["w_in_2"][0], 3 * HALF + AH + (u - U_AU) * UNIT)
            else:
                n = u - U_FFN - 2
                if u == U_END - 1 or (n >= 0 and n % 3 == 2):
                    g = FGROUPS - 1 if u == U_END - 1 else n // 3
                    sp.dma_start(raw_down, I["w_ffn_down_2"][0][g * UNIT:(g + 1) * UNIT, :]
                                 .rearrange("(f p) n -> p f n", p=P)).then_inc(raw_ready, 16)
                    return
                g, up = (0, u - U_FFN) if n < 0 else (1 + n // 3, n % 3)
                src = unit_src(I["w_ffn_up_2" if up else "w_ffn_gate_2"][0], g * UNIT)
            sp.dma_start(raw[:], src).then_inc(raw_ready, 16)

        def raw_count(u):
            return 16 * (u + 1 + min(u + 1, 8))

        def unit_high(act, u, slot):
            act.wait_ge(raw_ready, raw_count(u))
            nc.scalar.copy(wh[slot][:], raw[:]).then_inc(unit_hi, 1)

        def unit_low(pool, u, slot):
            pool.wait_ge(unit_hi, u + 1)
            nc.gpsimd.tensor_tensor(wl[slot][:], raw[:], wh[slot][:].bitcast(F32), ALU.subtract).then_inc(unit_ready, 1)

        def split_unit(pool, u, slot):
            pool.wait_ge(raw_ready, raw_count(u))
            nc.gpsimd.tensor_copy(wh[slot][:], raw[:]).then_inc(unit_hi, 1)
            unit_low(pool, u, slot)

        def products(terms, chunks, out_of):
            for n, (sh, sl, mh, ml) in enumerate(terms):
                for m, (s, x) in enumerate(((sh, mh), (sh, ml), (sl, mh))):
                    for c, (c0, cn) in enumerate(chunks):
                        last = nc.tensor.matmul(out_of(c, cn), s, x[:, c0:c0 + cn], start=n == 0 and m == 0,
                                                stop=n == len(terms) - 1 and m == 2)
            return last

        def channel_tile(h, l, t, chunks, bank, x=(xh, xl)):
            return products([(h[:, k, t * P:(t + 1) * P], l[:, k, t * P:(t + 1) * P], x[0][:, k, :], x[1][:, k, :])
                             for k in range(KT)], chunks, lambda c, cn: PS[:, bank + c, 0:cn])

        def token_tile(slot, c0, bank):
            return products([(xh[:, k, c0:c0 + P], xl[:, k, c0:c0 + P], wh[slot][:, k, :], wl[slot][:, k, :])
                             for k in range(KT)], [(0, UNIT)], lambda c, cn: PS[:, bank, 0:cn])

        def dense_rows(act_of, w, rows, bank):
            for k in range(KT):
                for half in range(2):
                    last = nc.tensor.matmul(PS[0:rows, bank + half, :], act_of(k), w[:, k, half * HALF:(half + 1) * HALF],
                                            start=k == 0, stop=k == KT - 1)
            return last

        def turn_row(src, rows, bank):
            for k in range(KT):
                last = nc.tensor.transpose(blocks(bank)[:, k, 0:rows], src[0:rows, k * P:(k + 1) * P], ident[0:rows, 0:rows])
            return last

        const_ready, vec_in, vec_turned, vec_ready = sem("const_ready"), sem("vec_in"), sem("vec_turned"), sem("vec_ready")
        x_in = [sem(f"x_in{s}") for s in range(4)]

        def consts_pool(pool):
            own = Chain(const_ready)
            own.step(pool, nc.gpsimd.memset(ident[:], 0.0))
            own.step(pool, nc.gpsimd.affine_select(out=ident[:], in_=ident[:], compare_op=ALU.not_equal, fill=1.0, base=0,
                                             pattern=[[-1, P]], channel_multiplier=1))
            own.step(pool, nc.gpsimd.memset(ones_mean[:], 1.0 / D))

        def inputs_sync(sp):
            rows = [(0, TAPS, I["conv_w_dw"][0]), (TAPS, 1, I["conv_b_dw"]), (TAPS + 1, 1, I["conv_norm_g"]),
                    (TAPS + 2, 1, I["conv_norm_b"]), (TAPS + 3, 3, I["conv_b_in"][0].rearrange("(r n) -> r n", r=3))]
            for r0, n, src in rows:
                sp.dma_start(vec_rows[r0:r0 + n, :], src).then_inc(vec_in, 16)
            for t, (c0, n) in enumerate(TILES):
                after(sp, turned, t - 3)
                src = meta_rows if t == 0 else row_tile(x_rows, t - 1)
                sp.dma_start(x_stage[0:n, t % 4, :], src).then_inc(x_in[t % 4], 16)
                if t == 3:
                    load_unit(sp, 0)

        def inputs_tensor(pe):
            pe.wait_ge(const_ready, 3)
            pe.wait_ge(vec_in, 80)
            for k in range(KT):
                last = nc.tensor.transpose(PS[:, 0, k * NV:(k + 1) * NV], vec_rows[:, k * P:(k + 1) * P], ident[0:NV, 0:NV])
            last.then_inc(vec_turned, 1)
            for t, (c0, n) in enumerate(TILES):
                pe.wait_ge(x_in[t % 4], 16 * (t // 4 + 1))
                after(pe, part_lo, t - 1)
                turn_row(x_stage[:, t % 4, :], n, 4 + 2 * (t % 2)).then_inc(turned, 1)

        def inputs_scalar(act):
            for t, (c0, n) in enumerate(TILES):
                act.wait_ge(turned, t + 1)
                nc.scalar.copy(xh[:, :, c0:c0 + n], blocks(4 + 2 * (t % 2))[:, :, 0:n]).then_inc(part_hi, 1)

        def inputs_vector(dve):
            dve.wait_ge(vec_turned, 1)
            nc.vector.tensor_copy(conv_vec[:].rearrange("p k r -> p (k r)"), PS[:, 0, 0:KT * NV]).then_inc(vec_ready, 1)
            for t, (c0, n) in enumerate(TILES):
                dve.wait_ge(part_hi, t + 1)
                nc.vector.tensor_tensor(xl[:, :, c0:c0 + n], blocks(4 + 2 * (t % 2))[:, :, 0:n],
                                        xh[:, :, c0:c0 + n].bitcast(F32), ALU.subtract).then_inc(part_lo, 1)

        conv_tile, conv_left = sem("conv_tile"), sem("conv_left")
        pads_ready, glu_ready, tap_done, conv_ready = sem("pads_ready"), sem("glu_ready"), sem("tap_done"), sem("conv_ready")

        def conv_in_sync(sp):
            for u in range(1, U_GQK):
                load_unit(sp, u)

        def conv_in_tensor(pe):
            pe.wait_ge(part_lo, len(TILES))
            pe.wait_ge(vec_ready, 1)
            with pe.Fori(0, U_GQK // 2) as i:
                for slot in range(2):
                    pe.wait_ge(unit_ready, i * 2 + slot + 1)
                    for t in range(2):
                        pe.wait_ge(conv_left, i * 4 + 2 * slot + t + 1)
                        channel_tile(wh[slot], wl[slot], t, CHUNKS3, 3 * t).then_inc(conv_tile, 1)

        def out_of_banks(eng_op, dst, bank, width=352, cols=T):
            eng_op(dst[:, 0:2 * width].rearrange("p (c n) -> p c n", c=2), PS[:, bank:bank + 2, 0:width])
            return eng_op(dst[:, 2 * width:cols], PS[:, bank + 2, 0:cols - 2 * width])

        tap_scaled, tap_added = sem("tap_scaled"), sem("tap_added")
        VEC_TAPS = TAPS - SIDE_TAPS

        def conv_in_scalar(act):
            act.wait_ge(vec_ready, 1)
            bias = lambda r, k: conv_vec[:, k, TAPS + 3 + r:TAPS + 4 + r]

            def scale_taps(k, taps):
                for j in taps:
                    act.wait_ge(glu_ready, k + 1)
                    after(act, tap_added, k * SIDE_TAPS + j - 1)
                    w = conv_vec[:, k, VEC_TAPS + j:VEC_TAPS + j + 1]
                    nc.scalar.activation(tap_part[(k * SIDE_TAPS + j) % 2][:], glu[:, k, VEC_TAPS + j:VEC_TAPS + j + T], ACT.Copy,
                                         scale=w).then_inc(tap_scaled, 1)

            unit_high(act, 0, 0)
            unit_high(act, 1, 1)
            for u in range(8):
                act.wait_ge(conv_tile, 2 * u + 1)
                out_of_banks(lambda o, i: nc.scalar.activation(o, i, ACT.Identity, bias=bias(0, u)), glu[:, u, PAD:], 0)\
                    .then_inc(conv_left, 1)
                if u > 0:
                    scale_taps(u - 1, range(0, 4))
                act.wait_ge(conv_tile, 2 * u + 2)
                after(act, glu_ready, u)
                out_of_banks(lambda o, i: nc.scalar.activation(o, i, ACT.Sigmoid, bias=bias(1, u)), gate_part, 3)\
                    .then_inc(conv_left, 1)
                unit_high(act, u + 2, u % 2)
                if u > 0:
                    scale_taps(u - 1, range(4, SIDE_TAPS))
            for k in range(KT):
                act.wait_ge(conv_tile, 16 + k + 1)
                if k == KT - 1:
                    act.wait_ge(tap_added, KT * SIDE_TAPS)
                out_of_banks(lambda o, i: nc.scalar.activation(o, i, ACT.Silu, bias=bias(2, k)), silu_z[:, k, :], 3 * (k % 2))\
                    .then_inc(conv_left, 1)
                if k == 0:
                    scale_taps(KT - 1, range(0, 4))
                if k % 2 and 8 + k // 2 + 2 < U_GQK:
                    unit_high(act, 8 + k // 2 + 2, k // 2 % 2)
                if k == 1:
                    scale_taps(KT - 1, range(4, SIDE_TAPS))

        def conv_in_pool(pool):
            def add_taps(k, taps):
                acc = side_sum[k % 2]
                if 0 in taps:
                    after(pool, conv_ready, k - 1)
                for j in taps:
                    n = k * SIDE_TAPS + j
                    pool.wait_ge(tap_scaled, n + 1)
                    part = tap_part[n % 2][:]
                    if j == 0:
                        ins = nc.gpsimd.tensor_copy(acc[:], part)
                    else:
                        pool.wait_ge(tap_added, n)
                        ins = nc.gpsimd.tensor_tensor(acc[:], acc[:], part, ALU.add)
                    ins.then_inc(tap_added, 1)

            nc.gpsimd.memset(glu[:, :, 0:PAD], 0.0).then_inc(pads_ready, 1)
            unit_low(pool, 0, 0)
            unit_low(pool, 1, 1)
            for u in range(U_GQK):
                if 1 <= u <= 8:
                    add_taps(u - 1, range(0, 4))
                if u < 8:
                    pool.wait_ge(conv_left, 2 + 2 * u + 2)
                    x = glu[:, u, PAD:]
                    nc.gpsimd.tensor_tensor(x, x, gate_part[:], ALU.mult).then_inc(glu_ready, 1)
                if u + 2 < U_GQK:
                    unit_low(pool, u + 2, u % 2)
                if 1 <= u <= 8:
                    add_taps(u - 1, range(4, SIDE_TAPS))

        def conv_vector(dve):
            nc.vector.memset(stat[:, 95:96], 0.0).then_inc(conv_left, 2)
            dve.wait_ge(pads_ready, 1)
            n = VEC_TAPS + 1

            def tile(k, side):
                g = glu[:, bass.ds(k, 1), :].rearrange("p o t -> p (o t)")
                vec = conv_vec[:, bass.ds(k, 1), :].rearrange("p o r -> p (o r)")
                dve.wait_ge(glu_ready, k + 1)
                for j in range(VEC_TAPS):
                    if j >= 2:
                        dve.wait_ge(tap_done, k * n + (j - 1))
                    acc = tap_sum[j % 2]
                    if j == 0:
                        ins = nc.vector.tensor_scalar(acc[:], g[:, 0:T], vec[:, 0:1], vec[:, TAPS:TAPS + 1], ALU.mult, ALU.add)
                    elif j == 1:
                        ins = nc.vector.tensor_scalar(acc[:], g[:, 1:1 + T], vec[:, 1:2], None, ALU.mult)
                    else:
                        ins = nc.vector.scalar_tensor_tensor(out=acc[:], in0=g[:, j:j + T], scalar=vec[:, j:j + 1], in1=acc[:],
                                                             op0=ALU.mult, op1=ALU.add)
                    ins.then_inc(tap_done, 1)
                dve.wait_ge(tap_done, k * n + VEC_TAPS)
                nc.vector.tensor_tensor(tap_sum[0][:], tap_sum[0][:], tap_sum[1][:], ALU.add).then_inc(tap_done, 1)
                dve.wait_ge(tap_done, k * n + n)
                dve.wait_ge(tap_added, k * SIDE_TAPS + SIDE_TAPS)
                nc.vector.tensor_tensor(g[:, PAD:], tap_sum[0][:], side_sum[side][:], ALU.add).then_inc(conv_ready, 1)
                dve.wait_ge(conv_ready, k + 1)

            with dve.Fori(0, KT // 2) as i:
                for side in range(2):
                    tile(i * 2 + side, side)

        (mean_ready, centered, squared, var_ready, std_ready, conv_normed, conv_silu, conv_gated) = (
            sem(s) for s in ("mean_ready", "centered", "squared", "var_ready", "std_ready", "conv_normed", "conv_silu", "conv_gated"))

        def conv_chunk(c):
            c0, cn = CHUNKS3[c]
            return glu[:, :, PAD + c0:PAD + c0 + cn]

        def over_channels(ap, n):
            return ap.rearrange("p (o n) -> p o n", o=1).broadcast_to([P, KT, n])

        def conv_norm_tensor(pe):
            pe.wait_ge(conv_left, 2 + 24)
            for k in range(KT):
                pe.wait_ge(conv_ready, k + 1)
                for c, (c0, cn) in enumerate(CHUNKS3):
                    last = nc.tensor.matmul(PS[:, c, 0:cn], ones_mean[:], conv_chunk(c)[:, k, :], start=k == 0, stop=k == KT - 1)
                    if k == KT - 1:
                        last.then_inc(mean_ready, 1)
            for c, (c0, cn) in enumerate(CHUNKS3):
                pe.wait_ge(squared, c + 1)
                for k in range(KT):
                    last = nc.tensor.matmul(PS[:, 3 + c, 0:cn], ones_mean[:], conv_sq[:, k, 0:cn], start=k == 0, stop=k == KT - 1)
                last.then_inc(var_ready, 1)

        def conv_norm_vector(dve):
            for c, (c0, cn) in enumerate(CHUNKS3):
                dve.wait_ge(mean_ready, c + 1)
                nc.vector.tensor_tensor(conv_chunk(c), conv_chunk(c), over_channels(PS[:, c, 0:cn], cn), ALU.subtract)\
                    .then_inc(centered, 1)
            def normalise(c):
                c0, cn = CHUNKS3[c]
                dve.wait_ge(std_ready, c + 1)
                rstd = conv_std[:, c0:c0 + cn]
                dve_own.step(dve, nc.vector.reciprocal(rstd, rstd))
                nc.vector.tensor_tensor(conv_chunk(c), conv_chunk(c), over_channels(rstd, cn), ALU.mult).then_inc(conv_normed, 1)

            def gate(c):
                c0, cn = CHUNKS3[c]
                dve.wait_ge(conv_silu, KT * (c + 1))
                nc.vector.tensor_tensor(conv_chunk(c), conv_chunk(c), silu_z[:, :, c0:c0 + cn], ALU.mult).then_inc(conv_gated, 1)

            normalise(0)
            normalise(1)
            gate(0)
            normalise(2)
            gate(1)
            gate(2)

        def conv_norm_scalar(act):
            for c, (c0, cn) in enumerate(CHUNKS3):
                act.wait_ge(centered, c + 1)
                after(act, var_ready, c)
                nc.scalar.activation(conv_sq[:, :, 0:cn], conv_chunk(c), ACT.Square).then_inc(squared, 1)
            for c, (c0, cn) in enumerate(CHUNKS3):
                act.wait_ge(var_ready, c + 1)
                nc.scalar.activation(conv_std[:, c0:c0 + cn], PS[:, 3 + c, 0:cn], ACT.Sqrt, bias=LN_EPS).then_inc(std_ready, 1)
            for c, (c0, cn) in enumerate(CHUNKS3):
                act.wait_ge(conv_normed, c + 1)
                for k in range(KT):
                    x = conv_chunk(c)[:, k, :]
                    nc.scalar.activation(x, x, ACT.Silu, bias=conv_vec[:, k, TAPS + 2:TAPS + 3],
                                         scale=conv_vec[:, k, TAPS + 1:TAPS + 2]).then_inc(conv_silu, 1)

        a1_in = sem("a1_in")
        (xn3, h1_done) = (
            sem(s) for s in ("xn3", "h1_done"))
        STATS, MEAN, VAR, STD, RSTD = stat[:, 0:12], stat[:, 12:13], stat[:, 13:14], stat[:, 14:15], stat[:, 15:16]

        def conv_out_sync(sp):
            sp.wait_ge(conv_tile, 24)
            sp.dma_start(w_conv_out[:], I["conv_w_out"][0].rearrange("(k p) n -> p k n", p=P)).then_inc(matrix_in, 16)
            for t in range(2):
                src = meta_rows if t == 0 else row_tile(x_rows, t - 1)
                sp.dma_start(rows3[t][0:TILES[t][1], :], src).then_inc(rows_in[t], 16)
            load_unit(sp, U_GQK)
            sp.wait_ge(conv_gated, 3)
            for s, vec in enumerate((I["conv_b_out"][0], I["post_ln_g"][0], I["post_ln_b"][0])):
                sp.dma_start(gain3[s][:], bcast_row(vec, D)).then_inc(gain_in, 16)
            sp.dma_start(a1_raw[:], I["gla_w_in"][0][:, 3 * D:3 * D + RANK].rearrange("(k p) n -> p k n", p=P)).then_inc(a1_in, 16)
            for t, (c0, n) in enumerate(TILES):
                sp.wait_ge(h1_done, t + 1)
                if t > 0:
                    sp.dma_start(row_tile(h1_rows, t - 1), rows3[t % 2][:]).then_inc(rows_out[t % 2], 16)
                if t + 2 < len(TILES):
                    after(sp, rows_out[t % 2], 16 * (t // 2 + t % 2))
                    sp.wait_ge(turned, H1 + t + 1)
                    sp.dma_start(rows3[t % 2][:], row_tile(x_rows, t + 1)).then_inc(rows_in[t % 2], 16)

        def conv_out_tensor(pe):
            pe.wait_ge(matrix_in, 16)

            def turn(t):
                pe.wait_ge(h1_done, t + 1)
                after(pe, part_lo, t - 1, H1)
                turn_row(rows3[t % 2], TILES[t][1], 4 + 2 * (t % 2)).then_inc(turned, 1)

            for t, (c0, n) in enumerate(TILES):
                pe.wait_ge(conv_gated, (c0 + n - 1) // 352 + 1)
                after(pe, dense_left, t - 1)
                dense_rows(lambda k: glu[:, k, PAD + c0:PAD + c0 + n], w_conv_out, n, 2 * (t % 2)).then_inc(dense_done, 1)
                if t >= 1:
                    turn(t - 1)
            turn(len(TILES) - 1)

        def layer_norm_rows(dve, x, n, count):
            for h in range(2):
                last = nc.vector.bn_stats(STATS[0:n, h * 6:(h + 1) * 6], x[0:n, h * HALF:(h + 1) * HALF])
            dve_own.step(dve, last)
            nc.vector.bn_aggr(stat[0:n, 12:14], STATS[0:n, :]).then_inc(row_var, 1)
            dve.wait_ge(row_std, count)
            dve_own.step(dve, nc.vector.reciprocal(RSTD[0:n, :], STD[0:n, :]))
            return nc.vector.tensor_scalar(x[0:n, :], x[0:n, :], MEAN[0:n, :], RSTD[0:n, :], ALU.subtract, ALU.mult)

        def conv_out_vector(dve):
            dve.wait_ge(gain_in, 48)

            def low(t):
                c0, n = TILES[t]
                dve.wait_ge(part_hi, H1 + t + 1)
                nc.vector.tensor_tensor(xl[:, :, c0:c0 + n], blocks(4 + 2 * (t % 2))[:, :, 0:n],
                                        xh[:, :, c0:c0 + n].bitcast(F32), ALU.subtract).then_inc(part_lo, 1)

            for t, (c0, n) in enumerate(TILES):
                x = rows3[t % 2]
                dve.wait_ge(rows_in[t % 2], 16 * (t // 2 + 1))
                dve.wait_ge(dense_done, t + 1)
                nc.vector.scalar_tensor_tensor(out=x[0:n, :], in0=x[0:n, :], scalar=ALPHA, in1=banks(2 * (t % 2), 2, D)[0:n, :],
                                               op0=ALU.mult, op1=ALU.add).then_inc(dense_left, 1)
                dve.wait_ge(dense_left, t + 1)
                dve_own.step(dve, nc.vector.tensor_tensor(x[0:n, :], x[0:n, :], gain3[0][0:n, :], ALU.add))
                layer_norm_rows(dve, x, n, t + 1).then_inc(xn3, 1)
                if t >= 1:
                    low(t - 1)
            low(len(TILES) - 1)

        def conv_out_scalar(act):
            def high(t):
                c0, n = TILES[t]
                act.wait_ge(turned, H1 + t + 1)
                nc.scalar.copy(xh[:, :, c0:c0 + n], blocks(4 + 2 * (t % 2))[:, :, 0:n]).then_inc(part_hi, 1)

            for t, (c0, n) in enumerate(TILES):
                act.wait_ge(row_var, t + 1)
                nc.scalar.activation(STD[0:n, :], VAR[0:n, :], ACT.Sqrt, bias=LN_EPS).then_inc(row_std, 1)
                if t >= 1:
                    high(t - 1)
            high(len(TILES) - 1)

        def conv_out_pool(pool):
            for t, (c0, n) in enumerate(TILES):
                x = rows3[t % 2]
                pool.wait_ge(xn3, t + 1)
                pool_own.step(pool, nc.gpsimd.tensor_tensor(x[0:n, :], x[0:n, :], gain3[1][0:n, :], ALU.mult))
                nc.gpsimd.tensor_tensor(x[0:n, :], x[0:n, :], gain3[2][0:n, :], ALU.add).then_inc(h1_done, 1)

        (a1_split, a2_zero, a2_in, mask_ready) = (
            sem(s) for s in ("a1_split", "a2_zero", "a2_in", "mask_ready"))
        (gqk_tile, gqk_left, gv_tile, gv_left, a1_ready) = (
            sem(s) for s in ("gqk_tile", "gqk_left", "gv_tile", "gv_left", "a1_ready"))
        NV_TILES = len(TILES)

        def gla_in_sync(sp):
            load_unit(sp, U_GQK + 1)
            sp.wait_ge(a2_zero, 1)
            sp.dma_start(w_a2[0:RANK, :], I["gla_w_a2"][0]).then_inc(a2_in, 16)
            sp.dma_start(w_a2[32:33, :], I["gla_b_a"]).then_inc(a2_in, 16)
            sp.dma_start(norm_bc[:], bcast_row(I["gla_norm_g"][0], GV)).then_inc(a2_in, 16)
            for u in range(U_GQK + 2, U_GR + 2):
                load_unit(sp, u)

        def gla_in_pool(pool):
            own = Chain(a1_split)
            pool.wait_ge(dense_done, 9)
            split_unit(pool, U_GQK, 0)
            split_unit(pool, U_GQK + 1, 1)
            pool.wait_ge(h1_done, 9)
            own.step(pool, nc.gpsimd.memset(a1_pad[:], 0.0))
            pool.wait_ge(a1_in, 16)
            own.step(pool, nc.gpsimd.tensor_copy(a1_pad[:, :, 0:RANK], a1_raw[:]))
            own.step(pool, nc.gpsimd.tensor_copy(a1h[:], a1_pad[:]))
            own.step(pool, nc.gpsimd.tensor_tensor(a1l[:], a1_pad[:], a1h[:].bitcast(F32), ALU.subtract))
            for s in range(2):
                pool.wait_ge(rows_out[s], 64)
            pool.wait_ge(turned, H1 + 9)
            nc.gpsimd.memset(w_a2[:], 0.0).then_inc(a2_zero, 1)
            pool.wait_ge(a2_zero, 1)
            nc.gpsimd.memset(a1[32:33, :], 1.0).then_inc(a1_ready, 1)
            pool.wait_ge(a1_ready, 1)
            own = Chain(mask_ready)
            own.step(pool, nc.gpsimd.memset(pair_mask_f[:], 1.0))
            for l in range(LEVELS):
                b = 64 >> l
                view = pair_mask_f[:, l, :].rearrange("p (n b) -> p n b", b=b)
                own.step(pool, nc.gpsimd.affine_select(out=view, in_=view, compare_op=ALU.is_ge, fill=0.0, base=0,
                                                 pattern=[[-2 * b, 64 // b], [0, b]], channel_multiplier=1))
                own.step(pool, nc.gpsimd.affine_select(out=view, in_=view, compare_op=ALU.is_ge, fill=0.0, base=b - 1,
                                                 pattern=[[2 * b, 64 // b], [0, b]], channel_multiplier=-1))
            own.step(pool, nc.gpsimd.tensor_copy(pair_mask[:], pair_mask_f[:]))
            for u in range(U_GQK + 2, U_GR + 2):
                before = u - 2
                if before < U_GV:
                    pool.wait_ge(gqk_tile, 2 * (before - U_GQK + 1))
                else:
                    pool.wait_ge(gv_tile, NV_TILES * (before - U_GV + 1))
                split_unit(pool, u, u % 2)

        def gla_in_tensor(pe):
            pe.wait_ge(part_lo, H1 + 9)
            pe.wait_ge(dense_left, 9)
            with pe.Fori(0, 2) as i:
                for slot in range(2):
                    pe.wait_ge(unit_ready, i * 2 + U_GQK + slot + 1)
                    for t in range(2):
                        pe.wait_ge(gqk_left, i * 4 + 2 * slot + t + 1)
                        channel_tile(wh[slot], wl[slot], t, CHUNKS3, 3 * t).then_inc(gqk_tile, 1)
            pe.wait_ge(a1_split, 4)
            pe.wait_ge(gqk_left, 9)
            channel_tile(a1h, a1l, 0, CHUNKS3, 0).then_inc(gqk_tile, 1)
            pe.wait_ge(gqk_left, 10)
            with pe.Fori(0, 2) as i:
                for slot in range(2):
                    pe.wait_ge(unit_ready, i * 2 + U_GV + slot + 1)
                    for t, (c0, n) in enumerate(TILES):
                        q = slot * NV_TILES + t
                        pe.wait_ge(gv_left, i * (2 * NV_TILES) + q + 1)
                        token_tile(slot, c0, 3 + q % 3).then_inc(gv_tile, 1)

        def gla_in_vector(dve):
            nc.vector.memset(stat[:, 92:93], 0.0).then_inc(gqk_left, 2)
            nc.vector.memset(stat[:, 93:94], 0.0).then_inc(gv_left, 3)

        def gla_in_scalar(act):
            act.wait_ge(conv_gated, 3)
            act.wait_ge(dense_done, 9)
            for i in range(8):
                act.wait_ge(gqk_tile, i + 1)
                scale = GK ** -0.5 if i < GH else 1.0
                out_of_banks(lambda o, x: nc.scalar.activation(o, x, ACT.Copy, scale=scale), qk[:, i, :], 3 * (i % 2))\
                    .then_inc(gqk_left, 1)
            act.wait_ge(gqk_tile, 9)
            out_of_banks(lambda o, x: nc.scalar.copy(o, x[0:32]), a1[0:32, :], 0).then_inc(gqk_left, 1)
            act.wait_ge(mask_ready, 2 + 2 * LEVELS)
            for h in range(GH):
                for t, (c0, n) in enumerate(TILES):
                    q = h * NV_TILES + t
                    act.wait_ge(gv_tile, q + 1)
                    dst = v_meta[:, h * GV:(h + 1) * GV] if t == 0 else v_rows[:, t - 1, h * GV:(h + 1) * GV]
                    nc.scalar.copy(dst, PS[0:n, 3 + q % 3, 0:GV]).then_inc(gv_left, 1)

        (z_ready, z_abs, z_min, soft_ready, cum_done, bl_ready, kdec_exp, kdec_ready, ebl_ready, qdec_exp, qdec_ready,
         arg_ready, arg_exp, arg_mul, kt_done, k_rows_done, diag_done, diag_used, pair_done, att_ready, o_done, o_kept,
         s_done, state_ready) = (
            sem(s) for s in ("z_ready", "z_abs", "z_min", "soft_ready", "cum_done", "bl_ready", "kdec_exp", "kdec_ready",
                             "ebl_ready", "qdec_exp", "qdec_ready", "arg_ready", "arg_exp", "arg_mul", "kt_done", "k_rows_done",
                             "diag_done", "diag_used", "pair_done", "att_ready", "o_done", "o_kept", "s_done", "state_ready"))
        SS_O = stat[:, 20:52]
        GROUPS = [range(0, 4), range(4, LEVELS)]
        ARGS = [arg_a, arg_b]
        PAIR_BANK = [1, 4]

        def chunk_sum(c):
            return stat[:, 60 + 4 * (c % 2):64 + 4 * (c % 2)]

        def chunk_decay(c):
            return stat[:, 52 + 4 * (c % 2):56 + 4 * (c % 2)]

        def level_arg(l):
            return ARGS[l // 4][:, l % 4, :, :]

        def pair_scores(l):
            return banks(PAIR_BANK[l // 4], 2).rearrange("p (l h t) -> p l h t", l=4, h=GH)[:, l % 4, :, :]

        def halves(ap, l):
            return ap.rearrange("p h t -> p (h t)").rearrange("p (m e b) -> p m e b", e=2, b=64 >> l)

        def head_blocks(ap, l):
            return ap.rearrange("p h (m e b) -> p h m e b", e=2, b=64 >> l)

        def out_bank(b, h):
            return PS[:, b + h // 2, (h % 2) * GV:(h % 2 + 1) * GV]

        def logits(c):
            return PS[:, 0, :].rearrange("p (h t) -> p h t", h=GH)[:, :, 0:TILES[c][1]]

        def gla_tensor(pe):
            pe.wait_ge(a2_in, 48)
            pe.wait_ge(a1_ready, 1)
            pe.wait_ge(gqk_left, 2 + 9)
            pe.wait_ge(gv_left, 3 + 4 * NV_TILES)

            def gate_logits(c):
                c0, n = TILES[c]
                after(pe, k_rows_done, c)
                for h in range(GH):
                    last = nc.tensor.matmul(PS[:, 0, h * P:h * P + n], w_a2[:, h * GK:(h + 1) * GK], a1[:, c0:c0 + n],
                                            start=True, stop=True)
                last.then_inc(z_ready, 1)

            gate_logits(0)
            for c, (c0, n) in enumerate(TILES):
                if c < NX:
                    pe.wait_ge(kdec_ready, c + 1)
                    pe.wait_ge(z_min, c + 1)
                    for h in range(GH):
                        last = nc.tensor.transpose(PS[0:n, 0, h * P:(h + 1) * P], k_decayed[:, h, 0:n], ident[:])
                    last.then_inc(kt_done, 1)
                if c > 0:
                    after(pe, diag_used, c - 1)
                    for h in range(GH):
                        last = nc.tensor.matmul(PS[:, 3, h * P:(h + 1) * P], qk[:, GH + h, c0:c0 + n], qk[:, h, c0:c0 + n],
                                                start=True, stop=True)
                    last.then_inc(diag_done, 1)
                if c < NX:
                    gate_logits(c + 1)
                if c > 0:
                    after(pe, att_ready, c - 1)
                    for g, group in enumerate(GROUPS):
                        if g == 1:
                            after(pe, o_kept, c - 1)
                        pe.wait_ge(arg_mul, 2 * (c - 1) + g + 1)
                        for l in group:
                            for h in range(GH):
                                odd = halves(level_arg(l)[:, h:h + 1, :], l)[:, :, 1, :]
                                last = nc.tensor.matmul(pair_scores(l)[:, h, :], level_arg(l)[:, h, :], odd, start=True, stop=True)
                        last.then_inc(pair_done, 1)
                    pe.wait_ge(qdec_ready, c)
                    pe.wait_ge(att_ready, c)
                    pe.wait_ge(state_ready, c)
                    for h in range(GH):
                        nc.tensor.matmul(out_bank(4, h), att[:, h, :], v_rows[:, c - 1, h * GV:(h + 1) * GV], start=True, stop=False)
                        last = nc.tensor.matmul(out_bank(4, h), q_decayed[:, h, :], state[:, h, :], start=False, stop=True)
                    last.then_inc(o_done, 1)
                if c < NX:
                    pe.wait_ge(k_rows_done, c + 1)
                    after(pe, state_ready, c)
                    v = v_meta if c == 0 else v_rows[:, c - 1, :]
                    for h in range(GH):
                        last = nc.tensor.matmul(out_bank(6, h), k_rows[0:n, h, :], v[:, h * GV:(h + 1) * GV], start=True, stop=True)
                    last.then_inc(s_done, 1)

        def gla_scalar(act):
            def factors(c):
                n = TILES[c][1]
                x = soft[:, :, 0:n]
                act.wait_ge(z_ready, c + 1)
                after(act, cum_done, GH * c)
                nc.scalar.activation(x, logits(c), ACT.Abs).then_inc(z_abs, 1)
                act.wait_ge(z_abs, c + 1)
                act_own.step(act, nc.scalar.activation(x, x, ACT.Exp, scale=-1.0))
                nc.scalar.activation(x, x, ACT.Ln, bias=1.0).then_inc(soft_ready, 1)
                act.wait_ge(bl_ready, c + 1)
                if c < NX:
                    after(act, kt_done, c)
                    for h in range(GH):
                        last = nc.scalar.activation(k_decayed[:, h, 0:n], decay[:, h, 0:n], ACT.Exp,
                                                    bias=chunk_sum(c)[:, h:h + 1], scale=-1 / TAU)
                    last.then_inc(kdec_exp, 1)
                    after(act, state_ready, c - 1)
                    nc.scalar.activation(chunk_decay(c), chunk_sum(c), ACT.Exp).then_inc(ebl_ready, 1)
                if c > 0:
                    for g in range(2):
                        act.wait_ge(arg_ready, 2 * (c - 1) + g + 1)
                        nc.scalar.activation(ARGS[g][:], ARGS[g][:], ACT.Exp, scale=1 / TAU).then_inc(arg_exp, 1)

            factors(0)
            for c, (c0, n) in enumerate(TILES):
                if c < NX:
                    act.wait_ge(kt_done, c + 1)
                    after(act, s_done, c)
                    nc.scalar.copy(k_rows[0:n].rearrange("p h t -> p (h t)"), PS[0:n, 0, :]).then_inc(k_rows_done, 1)
                    factors(c + 1)
                if c > 0:
                    act.wait_ge(o_done, c)
                    for h in range(GH):
                        col = 4 * (c - 1) + h
                        act_own.step(act, nc.scalar.activation(o_junk[:], out_bank(4, h), ACT.Square, accum_out=SS_O[:, col:col + 1]))
                    if c < NX:
                        act.wait_ge(s_done, c + 1)
                    nc.scalar.copy(v_rows[:, c - 1, :], banks(4, 2)).then_inc(o_kept, 1)
                if c < NX:
                    nc.scalar.activation(q_decayed[:], decay[:], ACT.Exp, scale=1 / TAU).then_inc(qdec_exp, 1)

        def gla_vector(dve):
            dve.wait_ge(mask_ready, 2 + 2 * LEVELS)

            def sums(c):
                n = TILES[c][1]
                dve.wait_ge(z_abs, c + 1)
                after(dve, kdec_ready, min(c, NX))
                after(dve, qdec_ready, c - 1)
                after(dve, arg_ready, 2 * (c - 1))
                nc.vector.tensor_scalar(decay[:, :, 0:n], logits(c), 0.0, None, ALU.min).then_inc(z_min, 1)
                dve.wait_ge(z_min, c + 1)
                dve.wait_ge(soft_ready, c + 1)
                for h in range(GH):
                    x = decay[:, h, 0:n]
                    nc.vector.tensor_tensor_scan(x, x, soft[:, h, 0:n], 0.0, ALU.add, ALU.subtract).then_inc(cum_done, 1)
                dve.wait_ge(cum_done, GH * (c + 1))
                after(dve, ebl_ready, c - 1)
                nc.vector.tensor_scalar(chunk_sum(c), decay[:, :, n - 1:n].rearrange("p h o -> p (h o)"), 1 / TAU, None, ALU.mult)\
                    .then_inc(bl_ready, 1)

            def exponents(c, g):
                if c == 1 and g == 0:
                    dve.wait_ge(s_done, 1)
                after(dve, pair_done, 2 * (c - 2) + g + 1)
                for l in GROUPS[g]:
                    x, e = halves(decay[:], l), halves(level_arg(l), l)
                    b = 64 >> l
                    ref = x[:, :, 0, b - 1:b].broadcast_to([P, 4 * 64 // b, b])
                    nc.vector.tensor_tensor(e[:, :, 0, :], ref, x[:, :, 0, :], ALU.subtract)
                    last = nc.vector.tensor_tensor(e[:, :, 1, :], x[:, :, 1, :], ref, ALU.subtract)
                last.then_inc(arg_ready, 1)

            def weights(c, g):
                dve.wait_ge(pair_done, 2 * (c - 1) + g + 1)
                for l in GROUPS[g]:
                    b = 64 >> l
                    odd = head_blocks(att[:], l)[:, :, :, 1, :]
                    mask = pair_mask[:, l:l + 1, :].rearrange("p o (m b) -> p o m b", b=b).broadcast_to([P, GH, 64 // b, b])
                    ins = nc.vector.copy_predicated(odd, mask, pair_scores(l).rearrange("p h (m b) -> p h m b", b=b))
                    if l < LEVELS - 1:
                        dve_own.step(dve, ins)
                    else:
                        ins.then_inc(att_ready, 1)

            sums(0)
            for c in range(len(TILES)):
                if c > 0:
                    dve.wait_ge(diag_done, c)
                    after(dve, o_done, c - 1)
                    nc.vector.tensor_tensor(att[:], PS[:, 3, :].rearrange("p (h t) -> p h t", h=GH),
                                            ident[:].rearrange("p (o t) -> p o t", o=1).broadcast_to([P, GH, P]), ALU.mult)\
                        .then_inc(diag_used, 1)
                    dve.wait_ge(diag_used, c)
                if c < NX:
                    sums(c + 1)
                for g in range(2):
                    if c > 0:
                        weights(c, g)
                    if c < NX:
                        exponents(c + 1, g)
                if c < NX:
                    dve.wait_ge(s_done, c + 1)
                    dve.wait_ge(ebl_ready, c + 1)
                    if c == 0:
                        nc.vector.tensor_copy(state[:].rearrange("p h e -> p (h e)"), banks(6, 2)).then_inc(state_ready, 1)
                    else:
                        dve.wait_ge(o_done, c)
                        for h in range(GH):
                            last = nc.vector.scalar_tensor_tensor(out=state[:, h, :], in0=state[:, h, :],
                                                                  scalar=chunk_decay(c)[:, h:h + 1], in1=out_bank(6, h),
                                                                  op0=ALU.mult, op1=ALU.add)
                        last.then_inc(state_ready, 1)

        def gla_pool(pool):
            pool.wait_ge(gqk_left, 2 + 9)
            for c, (c0, n) in enumerate(TILES):
                q, k = qk[:, 0:GH, c0:c0 + n], qk[:, GH:, c0:c0 + n]
                if c < NX:
                    pool.wait_ge(kdec_exp, c + 1)
                    nc.gpsimd.tensor_tensor(k_decayed[:, :, 0:n], k_decayed[:, :, 0:n], k, ALU.mult).then_inc(kdec_ready, 1)
                if c == 0:
                    continue
                for g, group in enumerate(GROUPS):
                    pool.wait_ge(arg_exp, 2 * (c - 1) + g + 1)
                    for l in group:
                        e, ql, kl = head_blocks(level_arg(l), l), head_blocks(q, l), head_blocks(k, l)
                        nc.gpsimd.tensor_tensor(e[:, :, :, 0, :], e[:, :, :, 0, :], kl[:, :, :, 0, :], ALU.mult)
                        last = nc.gpsimd.tensor_tensor(e[:, :, :, 1, :], e[:, :, :, 1, :], ql[:, :, :, 1, :], ALU.mult)
                    last.then_inc(arg_mul, 1)
                pool.wait_ge(qdec_exp, c)
                nc.gpsimd.tensor_tensor(q_decayed[:], q_decayed[:], q, ALU.mult).then_inc(qdec_ready, 1)

        (r_tile, r_left, rstd_own, r_used, gla_ready) = (
            sem(s) for s in ("r_tile", "r_left", "rstd_own", "r_used", "gla_ready"))

        def gla_gate_tensor(pe):
            pe.wait_ge(att_ready, NX)
            pe.wait_ge(k_rows_done, NX)
            with pe.Fori(0, 2) as i:
                for slot in range(2):
                    pe.wait_ge(unit_ready, i * 2 + U_GR + slot + 1)
                    for j in range(NX):
                        pe.wait_ge(r_left, i * (2 * NX) + slot * NX + j + 1)
                        token_tile(slot, META + j * P, j % 4).then_inc(r_tile, 1)

        def gla_gate_scalar(act):
            act.wait_ge(o_kept, NX)
            nc.scalar.activation(SS_O, SS_O, ACT.Sqrt, scale=1 / GV, bias=RMS_EPS).then_inc(rstd_own, 1)
            act.wait_ge(pair_done, 2 * NX)
            for q in range(GH * NX):
                act.wait_ge(r_tile, q + 1)
                after(act, r_used, q - 1)
                nc.scalar.activation(r_silu[q % 2][:], PS[:, q % 4, 0:GV], ACT.Silu).then_inc(r_left, 1)

        def gla_gate_vector(dve):
            nc.vector.memset(stat[:, 94:95], 0.0).then_inc(r_left, 4)
            dve.wait_ge(rstd_own, 1)
            dve_own.step(dve, nc.vector.reciprocal(SS_O, SS_O))
            dve.wait_ge(o_kept, NX)
            for q in range(GH * NX):
                h, j = divmod(q, NX)
                col = 4 * j + h
                dve.wait_ge(r_left, 4 + q + 1)
                x = v_rows[:, j, h * GV:(h + 1) * GV]
                nc.vector.scalar_tensor_tensor(out=x, in0=x, scalar=SS_O[:, col:col + 1], in1=r_silu[q % 2][:],
                                               op0=ALU.mult, op1=ALU.mult).then_inc(r_used, 1)

        def gla_gate_pool(pool):
            pool.wait_ge(a2_in, 48)
            for q in range(GH * NX):
                h, j = divmod(q, NX)
                if j == 0 and h < 2:
                    pool.wait_ge(r_tile, NX * (h + 1))
                    split_unit(pool, U_GR + 2 + h, h)
            for q in range(GH * NX):
                h, j = divmod(q, NX)
                pool.wait_ge(r_used, q + 1)
                x = v_rows[:, j, h * GV:(h + 1) * GV]
                nc.gpsimd.tensor_tensor(x, x, norm_bc[:], ALU.mult).then_inc(gla_ready, 1)

        (gla_turned, act5_ready, xn5, h2_done, h2_std, h2_n, n5_done) = (
            sem(s) for s in ("gla_turned", "act5_ready", "xn5", "h2_done", "h2_std", "h2_n", "n5_done"))

        def gla_out_sync(sp):
            sp.wait_ge(pair_done, 2 * NX)
            for u in range(U_GR + 2, U_GR + 4):
                load_unit(sp, u)
            sp.wait_ge(qdec_ready, NX)
            sp.wait_ge(diag_done, NX)
            sp.dma_start(w_gla_out[:], I["gla_w_out"][0].rearrange("(k p) n -> p k n", p=P)).then_inc(matrix_in, 16)
            sp.wait_ge(state_ready, NX)
            sp.wait_ge(o_done, NX)
            for j in range(2):
                sp.dma_start(rows5[j][:], row_tile(h1_rows, j)).then_inc(rows_in[j], 16)
            sp.dma_start(gain5[2][:], bcast_row(I["g_mix_pre_2"][0], D)).then_inc(gain_in, 16)
            sp.wait_ge(gla_ready, GH * NX)
            for s, vec in enumerate((I["post_ln_g"][1], I["post_ln_b"][1])):
                sp.dma_start(gain5[s][:], bcast_row(vec, D)).then_inc(gain_in, 16)
            load_unit(sp, U_AQK)
            load_unit(sp, U_AQK + 1)
            for j in range(NX):
                s = j % 2
                sp.wait_ge(h2_done, j + 1)
                sp.dma_start(row_tile(h2_rows, j), rows5[s][:]).then_inc(rows_out[s], 16)
                if j + 2 < NX:
                    sp.wait_ge(rows_out[s], H2_OUT + 16 * (j // 2 + 1))
                    sp.wait_ge(h2_n, j + 1)
                    sp.dma_start(rows5[s][:], row_tile(h1_rows, j + 2)).then_inc(rows_in[s], 16)
            for s in range(2):
                sp.wait_ge(rows_out[s], H2_OUT + 64)

        def gla_out_tensor(pe):
            pe.wait_ge(matrix_in, W5 + 16)
            pe.wait_ge(r_left, 4 + GH * NX)

            def turn(j):
                pe.wait_ge(n5_done, j + 1)
                after(pe, part_lo, j, N5)
                turn_row(normed5, P, 6).then_inc(turned, 1)

            for j in range(NX):
                pe.wait_ge(gla_ready, (GH - 1) * NX + j + 1)
                after(pe, act5_ready, j)
                turn_row(v_rows[:, j, :], P, 4).then_inc(gla_turned, 1)
                pe.wait_ge(act5_ready, j + 1)
                after(pe, dense_left, j - 1, Y5)
                dense_rows(lambda k: act5[j % 2][:, k, :], w_gla_out, P, 2 * (j % 2)).then_inc(dense_done, 1)
                if j >= 1:
                    turn(j - 1)
            turn(NX - 1)

        def gla_out_scalar(act):
            def high(j):
                act.wait_ge(turned, N5 + j + 1)
                nc.scalar.copy(xh[:, :, j * P:(j + 1) * P], blocks(6)).then_inc(part_hi, 1)

            def gla_act(j):
                act.wait_ge(gla_turned, j + 1)
                after(act, dense_done, j - 1, Y5)
                nc.scalar.copy(act5[j % 2][:], blocks(4)).then_inc(act5_ready, 1)

            act.wait_ge(r_used, GH * NX)
            gla_act(0)
            for j in range(NX):
                if j + 1 < NX:
                    gla_act(j + 1)
                act.wait_ge(row_var, Y5 + j + 1)
                nc.scalar.activation(STD, VAR, ACT.Sqrt, bias=LN_EPS).then_inc(row_std, 1)
                act.wait_ge(h2_done, j + 1)
                after(act, turned, j, N5)
                act_own.step(act, nc.scalar.activation(normed5[:], rows5[j % 2][:], ACT.Square, accum_out=stat[:, 16:17]))
                nc.scalar.activation(stat[:, 17:18], stat[:, 16:17], ACT.Sqrt, scale=1 / D, bias=RMS_EPS).then_inc(h2_std, 1)
                if j >= 1:
                    high(j - 1)
            high(NX - 1)

        def gla_out_vector(dve):
            for j in range(NX):
                x = rows5[j % 2]
                dve.wait_ge(rows_in[j % 2], ROWS5[j % 2] + 16 * (j // 2 + 1))
                dve.wait_ge(dense_done, Y5 + j + 1)
                nc.vector.scalar_tensor_tensor(out=x[:], in0=x[:], scalar=ALPHA, in1=banks(2 * (j % 2), 2, D),
                                               op0=ALU.mult, op1=ALU.add).then_inc(dense_left, 1)
                dve.wait_ge(dense_left, Y5 + j + 1)
                layer_norm_rows(dve, x, P, Y5 + j + 1).then_inc(xn5, 1)
                if j >= 1:
                    low5(dve, j - 1)
                dve.wait_ge(h2_std, j + 1)
                dve_own.step(dve, nc.vector.reciprocal(stat[:, 18:19], stat[:, 17:18]))
                nc.vector.tensor_scalar(normed5[:], x[:], stat[:, 18:19], None, ALU.mult).then_inc(h2_n, 1)
            low5(dve, NX - 1)

        def low5(dve, j):
            cols = slice(j * P, (j + 1) * P)
            dve.wait_ge(part_hi, N5 + j + 1)
            nc.vector.tensor_tensor(xl[:, :, cols], blocks(6), xh[:, :, cols].bitcast(F32), ALU.subtract).then_inc(part_lo, 1)

        def gla_out_pool(pool):
            pool.wait_ge(r_tile, GH * NX)
            split_unit(pool, U_AQK, 0)
            split_unit(pool, U_AQK + 1, 1)
            pool.wait_ge(gain_in, G5 + 48)
            for j in range(NX):
                x = rows5[j % 2]
                pool.wait_ge(xn5, j + 1)
                pool_own.step(pool, nc.gpsimd.tensor_tensor(x[:], x[:], gain5[0][:], ALU.mult))
                nc.gpsimd.tensor_tensor(x[:], x[:], gain5[1][:], ALU.add).then_inc(h2_done, 1)
                pool.wait_ge(h2_n, j + 1)
                nc.gpsimd.tensor_tensor(normed5[:], normed5[:], gain5[2][:], ALU.mult).then_inc(n5_done, 1)

        (in6_tile, in6_left, v6_tile, v6_left) = (
            sem(s) for s in ("in6_tile", "in6_left", "v6_tile", "v6_left"))
        (f_in, f_split, f_abs, f_soft_ready, f_cum_ready, cum_out, cum_in, causal_ready) = (
            sem(s) for s in ("f_in", "f_split", "f_abs", "f_soft_ready", "f_cum_ready", "cum_out", "cum_in", "causal_ready"))
        count_ready = sem("count_ready")
        B_F = stat[0:AH, 76:77]
        N_QK = 8

        def attn_in_sync(sp):
            sp.dma_start(f_raw[:], I["w_in_2"][0][:, 3 * HALF:3 * HALF + AH].rearrange("(k p) n -> p k n", p=P)).then_inc(f_in, 16)
            sp.dma_start(B_F, I["b_forget_2"].rearrange("o h -> h o")).then_inc(f_in, 16)
            for u in range(U_AQK + 2, U_FFN):
                load_unit(sp, u)
                if u == U_AV:
                    sp.wait_ge(f_cum_ready, 1)
                    sp.dma_start(cum_rows, f_cum[:]).then_inc(cum_out, 16)
                    sp.wait_ge(cum_out, 16)
                    sp.dma_start(cum_bc[:].rearrange("p h t -> p (h t)"), bcast_row(cum_rows.rearrange("h t -> (h t)"), AH * SEQ))\
                        .then_inc(cum_in, 16)
                    sp.wait_ge(in6_tile, N_QK + 1)
                    for half, name in enumerate(("g_attn_grp_2", "g_pool_grp_2")):
                        sp.dma_start(mix_gain[:, half * HALF:(half + 1) * HALF], bcast_row(I[name][0], HALF)).then_inc(gain_in, 16)
                    sp.dma_start(pool_gain[:], bcast_row(I["pool_scale_2"][0], HALF)).then_inc(gain_in, 16)
                    sp.dma_start(w_pool[:], I["w_pool_2"][0].rearrange("g c d -> c g d")).then_inc(gain_in, 16)

        def attn_in_pool(pool):
            own = Chain(f_split)
            pool.wait_ge(dense_done, Y5 + NX)
            own.step(pool, nc.gpsimd.memset(f_pad[:], 0.0))
            pool.wait_ge(f_in, 32)
            own.step(pool, nc.gpsimd.tensor_copy(f_pad[:, :, 0:AH], f_raw[:]))
            own.step(pool, nc.gpsimd.tensor_copy(fh[:], f_pad[:]))
            own.step(pool, nc.gpsimd.tensor_tensor(fl[:], f_pad[:], fh[:].bitcast(F32), ALU.subtract))
            own = Chain(causal_ready)
            own.step(pool, nc.gpsimd.memset(causal[:], 0.0))
            own.step(pool, nc.gpsimd.affine_select(out=causal[:], in_=causal[:], compare_op=ALU.is_ge, fill=MASKED, base=0,
                                             pattern=[[-1, P]], channel_multiplier=1))
            for u in range(U_AQK + 2, U_FFN):
                before = u - 2
                if before < U_AV:
                    pool.wait_ge(in6_tile, 2 * (before - U_AQK + 1))
                else:
                    pool.wait_ge(v6_tile, NX * (before - U_AV + 1))
                split_unit(pool, u, u % 2)

        def attn_in_tensor(pe):
            pe.wait_ge(part_lo, N5 + NX)
            pe.wait_ge(dense_left, Y5 + NX)
            with pe.Fori(0, 2) as i:
                for slot in range(2):
                    pe.wait_ge(unit_ready, i * 2 + U_AQK + slot + 1)
                    for t in range(2):
                        pe.wait_ge(in6_left, i * 4 + 2 * slot + t + 1)
                        channel_tile(wh[slot], wl[slot], t, CHUNKS2, 2 * t).then_inc(in6_tile, 1)
            pe.wait_ge(f_split, 4)
            pe.wait_ge(in6_left, N_QK + 1)
            channel_tile(fh, fl, 0, CHUNKS2, 0).then_inc(in6_tile, 1)
            for slot in range(2):
                pe.wait_ge(unit_ready, U_AV + slot + 1)
                for j in range(NX):
                    q = slot * NX + j
                    pe.wait_ge(v6_left, q + 1)
                    token_tile(slot, j * P, 4 + j % 4).then_inc(v6_tile, 1)
            for slot in range(2):
                pe.wait_ge(unit_ready, U_AU + slot + 1)
                for t in range(2):
                    q = N_QK + 1 + 2 * slot + t
                    pe.wait_ge(in6_left, q + 1)
                    channel_tile(wh[slot], wl[slot], t, CHUNKS2, 2 * (q % 2)).then_inc(in6_tile, 1)

        def attn_in_scalar(act):
            act.wait_ge(dense_done, Y5 + NX)
            for i in range(N_QK):
                act.wait_ge(in6_tile, i + 1)
                nc.scalar.activation(aqk[:, i, :], banks(2 * (i % 2), 2), ACT.Copy, scale=-AD ** -0.5 if i < 4 else 1.0)\
                    .then_inc(in6_left, 1)
            act.wait_ge(f_in, 32)
            act.wait_ge(in6_tile, N_QK + 1)
            nc.scalar.activation(f_soft[:], banks(0, 2)[0:AH, :], ACT.Abs, bias=B_F).then_inc(f_abs, 1)
            act.wait_ge(f_abs, 1)
            act_own.step(act, nc.scalar.activation(f_soft[:], f_soft[:], ACT.Exp, scale=-1.0))
            nc.scalar.activation(f_soft[:], f_soft[:], ACT.Ln, bias=1.0).then_inc(f_soft_ready, 1)
            for q in range(2 * NX):
                half, j = divmod(q, NX)
                act.wait_ge(v6_tile, q + 1)
                nc.scalar.copy(v6[:, j, half * UNIT:(half + 1) * UNIT], PS[:, 4 + j % 4, 0:UNIT]).then_inc(v6_left, 1)
            act.wait_ge(unit_ready, U_FFN)
            for g in range(4):
                q = N_QK + 1 + g
                act.wait_ge(in6_tile, q + 1)
                nc.scalar.copy(pool_u[:, g, :], banks(2 * (q % 2), 2)).then_inc(in6_left, 1)

        def attn_in_vector(dve):
            nc.vector.memset(stat[:, 90:91], 0.0).then_inc(in6_left, 2)
            nc.vector.memset(stat[:, 91:92], 0.0).then_inc(v6_left, 4)
            for t in range(16):
                nc.vector.memset(inv_count[:, t:t + 1], 1.0 / (t + 1)).then_inc(count_ready, 1)
            dve.wait_ge(f_abs, 1)
            dve_own.step(dve, nc.vector.tensor_scalar(f_logit[:], banks(0, 2)[0:AH, :], B_F, 0.0, ALU.add, ALU.min))
            nc.vector.memset(stat[:, 89:90], 0.0).then_inc(in6_left, 1)
            dve.wait_ge(f_soft_ready, 1)
            nc.vector.tensor_tensor_scan(f_cum[:], f_logit[:], f_soft[:], 0.0, ALU.add, ALU.subtract).then_inc(f_cum_ready, 1)

        pool_ready = sem("pool_ready")
        (score_done, score_ready, prob_ready, prob_turned, prob_left, pv_done) = (
            sem(s) for s in ("score_done", "score_ready", "prob_ready", "prob_turned", "prob_left", "pv_done"))
        (attn_left, pool_done, pool_left, mix_std, mix_n, mix_done, mix_turned, mix_ready) = (
            sem(s) for s in ("attn_left", "pool_done", "pool_left", "mix_std", "mix_n", "mix_done", "mix_turned", "mix_ready"))
        STEPS = NX * AH

        def step(s):
            turn, h = divmod(s, AH)
            return NX - 1 - turn, turn, h

        def low_score(s):
            return stat[:, 56 + s % 3:57 + s % 3]

        def row_sums(turn):
            return stat[:, 60 + 8 * (turn % 2):68 + 8 * (turn % 2)]

        def tails(s, lag, work):
            turn, h = divmod(s - lag, AH)
            if h == AH - 1 and turn >= 0:
                work(turn)

        def attn_tensor(pe):
            pe.wait_ge(causal_ready, 2)
            pe.wait_ge(in6_left, N_QK + 7)
            pe.wait_ge(v6_left, 4 + 2 * NX)

            def scores(s):
                i, _, h = step(s)
                after(pe, score_ready, s - 1)
                rows = slice((h % 2) * AD, (h % 2 + 1) * AD)
                n, bank = (i + 1) * P, 2 * (s % 2)
                for c0 in range(0, n, 512):
                    cn = min(512, n - c0)
                    diag = c0 + cn == n
                    nc.tensor.matmul(PS[:, bank + c0 // 512, 0:cn], aqk[rows, h // 2, i * P:(i + 1) * P],
                                     aqk[rows, 4 + h // 2, c0:c0 + cn], start=True, stop=not diag)
                    if diag:
                        last = nc.tensor.matmul(PS[:, bank + c0 // 512, cn - P:cn], ident[:], causal[:], start=False, stop=True)
                last.then_inc(score_done, 1)

            def turn_probs(s):
                i, _, _ = step(s)
                pe.wait_ge(prob_ready, s + 1)
                after(pe, prob_left, s)
                after(pe, mix_ready, (s - 5) // AH)
                for kb in range(i + 1):
                    last = nc.tensor.transpose(blocks(4)[:, kb, :], score[s % 3][:, kb * P:(kb + 1) * P], ident[:])
                last.then_inc(prob_turned, 1)

            def values(s):
                i, turn, h = step(s)
                pe.wait_ge(prob_left, s + 1)
                if h == 0:
                    after(pe, attn_left, turn)
                for kb in range(i + 1):
                    last = nc.tensor.matmul(PS[:, 6, h * AD:(h + 1) * AD], prob_t[s % 2][:, kb * P:(kb + 1) * P],
                                            v6[:, kb, h * AD:(h + 1) * AD], start=kb == 0, stop=kb == i)
                last.then_inc(pv_done, 1)

            def pooled(turn):
                i = NX - 1 - turn
                if turn == 0:
                    pe.wait_ge(gain_in, G6 + 64)
                    pe.wait_ge(pool_ready, 4)
                after(pe, pool_left, turn)
                for g in range(4):
                    last = nc.tensor.matmul(PS[:, 7, g * P:(g + 1) * P], pool_u[:, g, i * P:(i + 1) * P], w_pool[:, g, :],
                                            start=True, stop=True)
                last.then_inc(pool_done, 1)

            def mixed(turn):
                pe.wait_ge(mix_done, turn + 1)
                pe.wait_ge(prob_left, min(turn * AH + 13, STEPS))
                turn_row(mix_row[turn % 2], P, 4).then_inc(mix_turned, 1)

            for s in range(STEPS + 3):
                if s < STEPS:
                    scores(s)
                if 2 <= s < STEPS + 2:
                    turn_probs(s - 2)
                if s >= 3:
                    values(s - 3)
                tails(s, 3, pooled)
                tails(s, 7, mixed)
            mixed(NX - 1)

        def attn_scalar(act):
            def probs(s):
                i, turn, h = step(s)
                act.wait_ge(score_ready, s + 1)
                x = score[s % 3][:, 0:(i + 1) * P]
                nc.scalar.activation(x, x, ACT.Exp, scale=-1.0, bias=low_score(s), accum_out=row_sums(turn)[:, h:h + 1])\
                    .then_inc(prob_ready, 1)

            def leave(s):
                i, _, _ = step(s)
                act.wait_ge(prob_turned, s + 1)
                after(act, pv_done, s - 1)
                nc.scalar.copy(prob_t[s % 2][:, 0:(i + 1) * P], banks(4, 2, (i + 1) * P)).then_inc(prob_left, 1)

            def squares(turn):
                act.wait_ge(attn_left, turn + 1)
                act.wait_ge(pool_left, turn + 1)
                after(act, mix_n, 2 * turn)
                for half in range(2):
                    act_own.step(act, nc.scalar.activation(mix_sq[:], mix_row[turn % 2][:, half * HALF:(half + 1) * HALF], ACT.Square,
                                                           accum_out=stat[:, 78 + half:79 + half]))
                nc.scalar.activation(stat[:, 80:82], stat[:, 78:80], ACT.Sqrt, scale=1 / HALF, bias=RMS_EPS).then_inc(mix_std, 1)

            def mixed(turn):
                i = NX - 1 - turn
                act.wait_ge(mix_turned, turn + 1)
                nc.scalar.copy(mix_t[:, :, i * P:(i + 1) * P], blocks(4)).then_inc(mix_ready, 1)

            for s in range(STEPS + 2):
                if s < STEPS:
                    probs(s)
                if s >= 2:
                    leave(s - 2)
                tails(s, 4, squares)
                tails(s, 7, mixed)
            squares(NX - 1)
            mixed(NX - 1)

        def attn_vector(dve):
            dve.wait_ge(cum_in, 16)
            dve.wait_ge(gain_in, G6 + 64)

            def leave(turn):
                dve.wait_ge(pv_done, (turn + 1) * AH)
                dve.wait_ge(prob_ready, (turn + 1) * AH)
                after(dve, mix_turned, turn - 1)
                dve_own.step(dve, nc.vector.reciprocal(row_sums(turn), row_sums(turn)))
                a = mix_row[turn % 2][:, 0:HALF].rearrange("p (h d) -> p h d", h=AH)
                nc.vector.tensor_tensor(a, PS[:, 6, :].rearrange("p (h d) -> p h d", h=AH),
                                        row_sums(turn).rearrange("p (h o) -> p h o", o=1).broadcast_to([P, AH, AD]), ALU.mult)\
                    .then_inc(attn_left, 1)
                dve.wait_ge(pool_done, turn + 1)
                nc.vector.tensor_tensor(mix_row[turn % 2][:, HALF:], PS[:, 7, :], pool_gain[:], ALU.mult).then_inc(pool_left, 1)

            def norm(turn):
                dve.wait_ge(mix_std, turn + 1)
                dve_own.step(dve, nc.vector.reciprocal(stat[:, 82:84], stat[:, 80:82]))
                for half in range(2):
                    x = mix_row[turn % 2][:, half * HALF:(half + 1) * HALF]
                    nc.vector.tensor_scalar(x, x, stat[:, 82 + half:83 + half], None, ALU.mult).then_inc(mix_n, 1)

            for s in range(STEPS):
                i, _, h = step(s)
                n = (i + 1) * P
                dve.wait_ge(score_done, s + 1)
                after(dve, prob_turned, s - 2)
                nc.vector.tensor_tensor_reduce(score[s % 3][:, 0:n], cum_bc[:, h, 0:n], banks(2 * (s % 2), 2, n), 1.0, BIG,
                                               ALU.add, ALU.min, low_score(s)).then_inc(score_ready, 1)
                tails(s, 4, leave)
                tails(s, 5, norm)
            leave(NX - 1)
            norm(NX - 1)

        def attn_pool(pool):
            own = pool_own
            pool.wait_ge(count_ready, 16)
            pool.wait_ge(in6_left, N_QK + 7)
            for g, w in enumerate((2, 4, 8, 16)):
                src, s = pool_u[:, g, :], 1
                for r in range(g + 1):
                    dst = pool_tmp[r % 2]
                    own.step(pool, nc.gpsimd.tensor_copy(dst[:, 0:s], src[:, 0:s]))
                    own.step(pool, nc.gpsimd.tensor_tensor(dst[:, s:], src[:, s:], src[:, 0:SEQ - s], ALU.add))
                    src, s = dst, 2 * s
                own.step(pool, nc.gpsimd.tensor_tensor(src[:, 0:w - 1], src[:, 0:w - 1], inv_count[:, 0:w - 1], ALU.mult))
                own.step(pool, nc.gpsimd.tensor_scalar(src[:, w - 1:], src[:, w - 1:], 1.0 / w, None, ALU.mult))
                nc.gpsimd.tensor_tensor(pool_u[:, g, :], src[:], pool_u[:, g, :], ALU.subtract).then_inc(pool_ready, 1)
                pool.wait_ge(pool_ready, g + 1)
            pool.wait_ge(gain_in, G6 + 64)
            for i in range(NX):
                pool.wait_ge(mix_n, 2 * i + 2)
                nc.gpsimd.tensor_tensor(mix_row[i % 2][:], mix_row[i % 2][:], mix_gain[:], ALU.mult).then_inc(mix_done, 1)

        (y7_std, h3_done, h3_std, n7_done) = (
            sem(s) for s in ("y7_std", "h3_done", "h3_std", "n7_done"))

        def mix_out_sync(sp):
            sp.wait_ge(in6_tile, N_QK + 5)
            sp.dma_start(w_mix_out[:], I["w_out_2"][0].rearrange("(k p) n -> p k n", p=P)).then_inc(matrix_in, 16)
            sp.wait_ge(score_done, STEPS)
            for s in range(2):
                sp.dma_start(rows7[s][:], row_tile(h2_rows, s)).then_inc(rows_in[s], 16)
            for s, name in enumerate(("g_mix_post_2", "g_ffn_pre_2")):
                sp.dma_start(gain7[s][:], bcast_row(I[name][0], D)).then_inc(gain_in, 16)
            sp.wait_ge(pool_done, NX)
            load_unit(sp, U_FFN)
            for j in range(NX):
                s = j % 2
                sp.wait_ge(h3_done, j + 1)
                sp.dma_start(row_tile(h3_rows, j), rows7[s][:]).then_inc(rows_out[s], 16)
                if j + 2 < NX:
                    sp.wait_ge(rows_out[s], H3_OUT + 16 * (j // 2 + 1))
                    sp.wait_ge(n7_done, j + 1)
                    sp.dma_start(rows7[s][:], row_tile(h2_rows, j + 2)).then_inc(rows_in[s], 16)
            for s in range(2):
                sp.wait_ge(rows_out[s], H3_OUT + 64)

        def mix_out_tensor(pe):
            pe.wait_ge(matrix_in, W7 + 16)

            def turn(j):
                pe.wait_ge(n7_done, j + 1)
                after(pe, part_lo, j - 1, N7)
                turn_row(normed7[j % 2], P, 4 + 2 * (j % 2)).then_inc(turned, 1)

            for j in range(NX):
                after(pe, dense_left, j - 1, Y7)
                if j == 0:
                    pe.wait_ge(mix_ready, NX)
                    pe.wait_ge(score_ready, STEPS)
                dense_rows(lambda k: mix_t[:, k, j * P:(j + 1) * P], w_mix_out, P, 2 * (j % 2)).then_inc(dense_done, 1)
                if j >= 1:
                    turn(j - 1)
            turn(NX - 1)

        def mix_out_scalar(act):
            def high(j):
                act.wait_ge(turned, N7 + j + 1)
                nc.scalar.copy(xh7[:, :, j * P:(j + 1) * P], blocks(4 + 2 * (j % 2))).then_inc(part_hi, 1)

            for j in range(NX):
                act.wait_ge(dense_done, Y7 + j + 1)
                after(act, h3_done, j - 1)
                act_own.step(act, nc.scalar.activation(scaled7[j % 2][:], banks(2 * (j % 2), 2), ACT.Square, accum_out=stat[:, 0:1]))
                nc.scalar.activation(stat[:, 1:2], stat[:, 0:1], ACT.Sqrt, scale=1 / D, bias=RMS_EPS).then_inc(y7_std, 1)
                act.wait_ge(h3_done, j + 1)
                after(act, turned, j - 1, N7)
                act_own.step(act, nc.scalar.activation(normed7[j % 2][:], rows7[j % 2][:], ACT.Square, accum_out=stat[:, 16:17]))
                nc.scalar.activation(stat[:, 17:18], stat[:, 16:17], ACT.Sqrt, scale=1 / D, bias=RMS_EPS).then_inc(h3_std, 1)
                if j >= 1:
                    high(j - 1)
            high(NX - 1)

        def mix_out_vector(dve):
            dve.wait_ge(gain_in, G7 + 32)

            def low(j):
                cols = slice(j * P, (j + 1) * P)
                dve.wait_ge(part_hi, N7 + j + 1)
                nc.vector.tensor_tensor(xl7[:, :, cols], blocks(4 + 2 * (j % 2)), xh7[:, :, cols].bitcast(F32), ALU.subtract)\
                    .then_inc(part_lo, 1)

            for j in range(NX):
                dve.wait_ge(y7_std, j + 1)
                dve_own.step(dve, nc.vector.reciprocal(stat[:, 2:3], stat[:, 1:2]))
                nc.vector.scalar_tensor_tensor(out=scaled7[j % 2][:], in0=banks(2 * (j % 2), 2), scalar=stat[:, 2:3],
                                               in1=gain7[0][:], op0=ALU.mult, op1=ALU.mult).then_inc(dense_left, 1)
                if j >= 1:
                    low(j - 1)
                dve.wait_ge(h3_std, j + 1)
                dve_own.step(dve, nc.vector.reciprocal(stat[:, 18:19], stat[:, 17:18]))
                nc.vector.scalar_tensor_tensor(out=normed7[j % 2][:], in0=rows7[j % 2][:], scalar=stat[:, 18:19],
                                               in1=gain7[1][:], op0=ALU.mult, op1=ALU.mult).then_inc(n7_done, 1)
            low(NX - 1)

        def mix_out_pool(pool):
            for j in range(NX):
                x = rows7[j % 2]
                pool.wait_ge(rows_in[j % 2], ROWS7[j % 2] + 16 * (j // 2 + 1))
                pool.wait_ge(dense_left, Y7 + j + 1)
                nc.gpsimd.tensor_tensor(x[:], x[:], scaled7[j % 2][:], ALU.add).then_inc(h3_done, 1)

        (ff_tile, gate_left, up_left, ff_hi, ff_lo, dn_tile, dn_left, acc_zero) = (
            sem(s) for s in ("ff_tile", "gate_left", "up_left", "ff_hi", "ff_lo", "dn_tile", "dn_left", "acc_zero"))
        HALVES = 2 * NX

        def ffn_sync(sp):
            for u in range(U_FFN + 1, U_END):
                load_unit(sp, u)

        def ffn_pool(pool):
            pool.wait_ge(dense_done, Y7 + NX)
            split_unit(pool, u_gate(0), 0)
            split_unit(pool, u_gate(0) + 1, 1)
            pool.wait_ge(turned, N7 + NX)
            nc.gpsimd.memset(ff_acc[:], 0.0).then_inc(acc_zero, 1)
            for g in range(1, FGROUPS):
                pool.wait_ge(ff_tile, g * 4 - 2)
                split_unit(pool, u_gate(g), 0)
                pool.wait_ge(ff_tile, g * 4)
                split_unit(pool, u_gate(g) + 1, 1)
                after(pool, dn_tile, (g - 1) * HALVES)
                split_unit(pool, u_down(g - 1), 2)
            pool.wait_ge(dn_tile, (FGROUPS - 1) * HALVES)
            split_unit(pool, u_down(FGROUPS - 1), 2)

        def ffn_tensor(pe):
            def gate_up(g, gate_unit):
                x = (xh7, xl7)
                tile = lambda slot, t, bank: channel_tile(wh[slot], wl[slot], t, CHUNKS2, bank, x).then_inc(ff_tile, 1)
                first = isinstance(g, int)
                pe.wait_ge(unit_ready, gate_unit + 1)
                if not first:
                    pe.wait_ge(up_left, g * 2)
                tile(0, 0, 0)
                if not first:
                    pe.wait_ge(gate_left, g * 2)
                tile(0, 1, 2)
                pe.wait_ge(unit_ready, gate_unit + 2)
                if not first:
                    pe.wait_ge(up_left, g * 2 - 1)
                tile(1, 0, 4)
                pe.wait_ge(gate_left, g * 2 + 1)
                tile(1, 1, 0)

            def down(g, b, down_unit):
                pe.wait_ge(unit_ready, down_unit + 1)
                pe.wait_ge(ff_lo, g * 2 + 2)
                for j in range(NX):
                    cols = slice(j * P, (j + 1) * P)
                    for half in range(2):
                        pe.wait_ge(dn_left, g * HALVES + (2 * j + half + 1))
                        n = slice(half * HALF, (half + 1) * HALF)
                        products([(ffh[b][:, f, cols], ffl[b][:, f, cols], wh_down[:, f, n], wl_down[:, f, n]) for f in range(2)],
                                 [(0, HALF)], lambda c, cn: PS[:, 6 + half, :]).then_inc(dn_tile, 1)

            pe.wait_ge(part_lo, N7 + NX)
            pe.wait_ge(dense_left, Y7 + NX)
            gate_up(0, u_gate(0))
            with pe.Fori(0, FGROUPS // 2) as i:
                gate_up(i * 2 + 1, i * 6 + u_gate(1))
                down(i * 2, 0, i * 6 + u_down(0))
                gate_up(i * 2 + 2, i * 6 + u_gate(2))
                down(i * 2 + 1, 1, i * 6 + u_down(1))
            down(FGROUPS - 1, 0, u_down(FGROUPS - 1))

        def ffn_scalar(act):
            def group(g, b):
                for t in range(2):
                    act.wait_ge(ff_tile, g * 4 + t + 1)
                    nc.scalar.activation(ff_silu[:, t, :], banks(2 * t, 2), ACT.Silu).then_inc(gate_left, 1)
                for t in range(2):
                    act.wait_ge(up_left, g * 2 + t + 1)
                    nc.scalar.copy(ffh[b][:, t, :], ff_prod[t][:]).then_inc(ff_hi, 1)

            group(0, 0)
            with act.Fori(0, FGROUPS // 2) as i:
                group(i * 2 + 1, 1)
                group(i * 2 + 2, 0)

        def ffn_vector(dve):
            nc.vector.memset(stat[:, 88:89], 0.0).then_inc(dn_left, 2)

            def group(g, b):
                for t in range(2):
                    dve.wait_ge(ff_tile, g * 4 + t + 3)
                    dve.wait_ge(gate_left, g * 2 + t + 1)
                    if not isinstance(g, int):
                        dve.wait_ge(ff_lo, g * 2 + t - 1)
                    nc.vector.tensor_tensor(ff_prod[t][:], ff_silu[:, t, :], banks(4 * (1 - t), 2), ALU.mult).then_inc(up_left, 1)
                for t in range(2):
                    dve.wait_ge(ff_hi, g * 2 + t + 1)
                    nc.vector.tensor_tensor(ffl[b][:, t, :], ff_prod[t][:], ffh[b][:, t, :].bitcast(F32), ALU.subtract)\
                        .then_inc(ff_lo, 1)

            def add_down(g):
                for q in range(HALVES):
                    j, half = divmod(q, 2)
                    dve.wait_ge(dn_tile, g * HALVES + q + 1)
                    x = ff_acc[:, j, half * HALF:(half + 1) * HALF]
                    nc.vector.tensor_tensor(x, x, PS[:, 6 + half, :], ALU.add).then_inc(dn_left, 1)

            group(0, 0)
            dve.wait_ge(acc_zero, 1)
            with dve.Fori(0, FGROUPS // 2) as i:
                group(i * 2 + 1, 1)
                add_down(i * 2)
                group(i * 2 + 2, 0)
                add_down(i * 2 + 1)
            add_down(FGROUPS - 1)

        p_in = sem("p_in")
        (p_turned, p_ready, ff_std, ff_n, h4_done, h4_turned, act9_ready) = (
            sem(s) for s in ("p_turned", "p_ready", "ff_std", "ff_n", "h4_done", "h4_turned", "act9_ready"))
        (e_done, e_std, e_n, gated9, out_ready) = (
            sem(s) for s in ("e_done", "e_std", "e_n", "gated9", "out_ready"))

        def final_sync(sp):
            sp.wait_ge(ff_tile, 4 * FGROUPS)
            sp.dma_start(p_stage[:], I["p_2"][0, 0].rearrange("(j p) n -> p j n", p=P)).then_inc(p_in, 16)
            sp.dma_start(w_ple_proj[:], I["w_ple_proj_2"][0].rearrange("(k p) n -> p k n", p=P)).then_inc(matrix_in, 16)
            sp.dma_start(w_ple_gate[:], I["w_ple_gate_2"][0].rearrange("(k p) n -> p k n", p=P)).then_inc(matrix_in, 16)
            for s, name in enumerate(("g_ffn_post_2", "g_ple_2")):
                sp.dma_start(gain9[s][:], bcast_row(I[name][0], D)).then_inc(gain_in, 16)
            for s in range(2):
                sp.dma_start(rows9[s][:], row_tile(h3_rows, s)).then_inc(rows_in[s], 16)
            for j in range(NX):
                s = j % 2
                if j + 2 < NX:
                    sp.wait_ge(h4_done, j + 1)
                    sp.dma_start(rows9[s][:], row_tile(h3_rows, j + 2)).then_inc(rows_in[s], 16)
                sp.wait_ge(out_ready, j + 1)
                sp.dma_start(row_tile(out[0], j), out_row[s][:]).then_inc(rows_out[s], 16)
            for s in range(2):
                sp.wait_ge(rows_out[s], OUT + 64)

        def final_tensor(pe):
            pe.wait_ge(p_in, 16)
            pe.wait_ge(up_left, 2 * FGROUPS)
            pe.wait_ge(gate_left, 2 * FGROUPS)
            for k in range(2):
                for j in range(NX):
                    last = nc.tensor.transpose(PS[:, 2 * k + j // 4, (j % 4) * P:(j % 4 + 1) * P], p_stage[:, j, k * P:(k + 1) * P],
                                               ident[:])
            last.then_inc(p_turned, 1)
            pe.wait_ge(matrix_in, W9 + 32)
            pe.wait_ge(p_ready, 1)
            pe.wait_ge(dn_left, 2 + FGROUPS * HALVES)
            for j in range(NX):
                after(pe, e_n, j)
                for k in range(2):
                    for half in range(2):
                        last = nc.tensor.matmul(PS[:, 6 + half, :], p_t[:, k, j * P:(j + 1) * P],
                                                w_ple_proj[:, k, half * HALF:(half + 1) * HALF], start=k == 0, stop=k == 1)
                last.then_inc(e_done, 1)
                pe.wait_ge(h4_done, j + 1)
                after(pe, act9_ready, j)
                turn_row(ff_acc[:, j, :], P, 4).then_inc(h4_turned, 1)
                pe.wait_ge(act9_ready, j + 1)
                after(pe, dense_left, j - 1, Y9)
                dense_rows(lambda k: act9[j % 2][:, k, :], w_ple_gate, P, 2 * (j % 2)).then_inc(dense_done, 1)

        def final_scalar(act):
            act.wait_ge(p_turned, 1)
            nc.scalar.copy(p_t[:].rearrange("p k t -> p (k t)"), banks(0, 4, 2048)).then_inc(p_ready, 1)
            act.wait_ge(gain_in, G9 + 32)

            def ff_norm(j):
                act.wait_ge(dn_left, 2 + (FGROUPS - 1) * HALVES + 2 * j + 2)
                after(act, ff_n, j)
                act_own.step(act, nc.scalar.activation(sq9[:], ff_acc[:, j, :], ACT.Square, accum_out=stat[:, 0:1]))
                nc.scalar.activation(stat[:, 1:2], stat[:, 0:1], ACT.Sqrt, scale=1 / D, bias=RMS_EPS).then_inc(ff_std, 1)

            ff_norm(0)
            for j in range(NX):
                act.wait_ge(e_done, j + 1)
                act_own.step(act, nc.scalar.activation(sq9e[:], banks(6, 2), ACT.Square, accum_out=stat[:, 3:4]))
                after(act, e_n, j)
                nc.scalar.activation(stat[:, 4:5], stat[:, 3:4], ACT.Sqrt, scale=1 / D, bias=RMS_EPS).then_inc(e_std, 1)
                act.wait_ge(h4_turned, j + 1)
                after(act, dense_done, j - 1, Y9)
                nc.scalar.copy(act9[j % 2][:], blocks(4)).then_inc(act9_ready, 1)
                if j + 1 < NX:
                    ff_norm(j + 1)
                act.wait_ge(dense_done, Y9 + j + 1)
                after(act, rows_out[j % 2], 16 * (j // 2), OUT)
                nc.scalar.activation(out_row[j % 2][:], banks(2 * (j % 2), 2), ACT.Sigmoid).then_inc(dense_left, 1)

        def final_vector(dve):
            dve.wait_ge(gain_in, G9 + 32)

            def ff_norm(j):
                dve.wait_ge(ff_std, j + 1)
                dve_own.step(dve, nc.vector.reciprocal(stat[:, 2:3], stat[:, 1:2]))
                x = ff_acc[:, j, :]
                nc.vector.scalar_tensor_tensor(out=x, in0=x, scalar=stat[:, 2:3], in1=gain9[0][:], op0=ALU.mult, op1=ALU.mult)\
                    .then_inc(ff_n, 1)

            ff_norm(0)
            for j in range(NX):
                dve.wait_ge(e_std, j + 1)
                after(dve, gated9, j)
                dve_own.step(dve, nc.vector.reciprocal(stat[:, 5:6], stat[:, 4:5]))
                nc.vector.scalar_tensor_tensor(out=e_row[:], in0=banks(6, 2), scalar=stat[:, 5:6], in1=gain9[1][:],
                                               op0=ALU.mult, op1=ALU.mult).then_inc(e_n, 1)
                if j + 1 < NX:
                    ff_norm(j + 1)
                dve.wait_ge(e_n, j + 1)
                dve.wait_ge(dense_left, Y9 + j + 1)
                nc.vector.tensor_tensor(out_row[j % 2][:], out_row[j % 2][:], e_row[:], ALU.mult).then_inc(gated9, 1)

        def final_pool(pool):
            for j in range(NX):
                if j == 0:
                    pool.wait_ge(rows_in[0], ROWS9[0] + 16)
                    pool.wait_ge(ff_n, 1)
                    nc.gpsimd.tensor_tensor(ff_acc[:, 0, :], ff_acc[:, 0, :], rows9[0][:], ALU.add).then_inc(h4_done, 1)
                if j + 1 < NX:
                    n = j + 1
                    pool.wait_ge(rows_in[n % 2], ROWS9[n % 2] + 16 * (n // 2 + 1))
                    pool.wait_ge(ff_n, n + 1)
                    nc.gpsimd.tensor_tensor(ff_acc[:, n, :], ff_acc[:, n, :], rows9[n % 2][:], ALU.add).then_inc(h4_done, 1)
                pool.wait_ge(gated9, j + 1)
                pool.wait_ge(h4_done, j + 1)
                nc.gpsimd.tensor_tensor(out_row[j % 2][:], out_row[j % 2][:], ff_acc[:, j, :], ALU.add).then_inc(out_ready, 1)

        block = ctx.enter_context(nc.Block())

        @block.sync
        def _(sp):
            inputs_sync(sp)
            conv_in_sync(sp)
            conv_out_sync(sp)
            gla_in_sync(sp)
            gla_out_sync(sp)
            attn_in_sync(sp)
            mix_out_sync(sp)
            ffn_sync(sp)
            final_sync(sp)

        @block.tensor
        def _(pe):
            inputs_tensor(pe)
            conv_in_tensor(pe)
            conv_norm_tensor(pe)
            conv_out_tensor(pe)
            gla_in_tensor(pe)
            gla_tensor(pe)
            gla_gate_tensor(pe)
            gla_out_tensor(pe)
            attn_in_tensor(pe)
            attn_tensor(pe)
            mix_out_tensor(pe)
            ffn_tensor(pe)
            final_tensor(pe)

        @block.scalar
        def _(act):
            inputs_scalar(act)
            conv_in_scalar(act)
            conv_norm_scalar(act)
            conv_out_scalar(act)
            gla_in_scalar(act)
            gla_scalar(act)
            gla_gate_scalar(act)
            gla_out_scalar(act)
            attn_in_scalar(act)
            attn_scalar(act)
            mix_out_scalar(act)
            ffn_scalar(act)
            final_scalar(act)

        @block.vector
        def _(dve):
            inputs_vector(dve)
            conv_vector(dve)
            conv_norm_vector(dve)
            conv_out_vector(dve)
            gla_in_vector(dve)
            gla_vector(dve)
            gla_gate_vector(dve)
            gla_out_vector(dve)
            attn_in_vector(dve)
            attn_vector(dve)
            mix_out_vector(dve)
            ffn_vector(dve)
            final_vector(dve)

        @block.gpsimd
        def _(pool):
            consts_pool(pool)
            conv_in_pool(pool)
            conv_out_pool(pool)
            gla_in_pool(pool)
            gla_pool(pool)
            gla_gate_pool(pool)
            gla_out_pool(pool)
            attn_in_pool(pool)
            attn_pool(pool)
            mix_out_pool(pool)
            ffn_pool(pool)
            final_pool(pool)


_INS = ['x', 'meta', 'conv_w_in', 'conv_b_in', 'conv_w_dw', 'conv_b_dw', 'conv_norm_g', 'conv_norm_b', 'conv_w_out',
        'conv_b_out', 'gla_w_in', 'gla_w_a2', 'gla_b_a', 'gla_norm_g', 'gla_w_out', 'post_ln_g', 'post_ln_b', 'p_2',
        'g_mix_pre_2', 'w_in_2', 'b_forget_2', 'g_attn_grp_2', 'g_pool_grp_2', 'w_pool_2', 'pool_scale_2', 'w_out_2',
        'g_mix_post_2', 'g_ffn_pre_2', 'w_ffn_gate_2', 'w_ffn_up_2', 'w_ffn_down_2', 'g_ffn_post_2', 'w_ple_proj_2',
        'g_ple_2', 'w_ple_gate_2']


def kernel(**inputs):
    import numpy as _np
    import concourse.bacc as _bacc
    from concourse import mybir as _mybir
    from concourse.bass_utils import run_bass_kernel_spmd as _run

    nc = _bacc.Bacc("TRN2", target_bir_lowering=False, num_devices=1)
    arrays, aps = {}, {}
    for name in _INS:
        a = _np.ascontiguousarray(inputs[name])
        arrays[f"in_{name}_dram"] = a
        aps[name] = nc.dram_tensor(f"in_{name}_dram", a.shape, _mybir.dt.from_np(a.dtype), kind="ExternalInput").ap()
    out = nc.dram_tensor("out_0_dram", (1, SEQ, D), F32, kind="ExternalOutput").ap()
    hybrid_block(nc, aps, out)
    r = _run(nc, [arrays], core_ids=[0])
    return r.results[0]["out_0_dram"]
```

```python
from contextlib import ExitStack

import concourse.bass as bass
from concourse import mybir

ALU = mybir.AluOpType
ACT = mybir.ActivationFunctionType
F32 = mybir.dt.float32
F32R = mybir.dt.float32r
I32 = mybir.dt.int32

P = 128
D = 1024
SEQ = 1024
META = 16
T = META + SEQ
KT = D // P
NX = SEQ // P
HALF = 512
TAPS = 31
SIDE_TAPS = 7
PAD = TAPS - 1
ALPHA = 4 ** 0.25
LN_EPS = 1e-5
RMS_EPS = 1e-6
UNIT = 256
GH, GK, GV = 4, 128, 256
TAU = 16.0
RANK = 16
LEVELS = 7
AH, AD = 8, 64
FGROUPS = 11
MASKED = 1e30
BIG = 3e38

TILES = [(0, META)] + [(META + P * j, P) for j in range(NX)]
CHUNKS3 = [(0, 352), (352, 352), (704, 336)]
CHUNKS4 = [(0, 176), (176, 176), (352, 352), (704, 336)]
CHUNKS2 = [(0, 512), (512, 512)]

U_CONV, U_CO, U_GQK, U_GV, U_GR, U_AQK, U_AU, U_AV, U_FFN, U_END = 0, 12, 16, 20, 24, 32, 36, 38, 40, 73
U_R, U_GO = (U_GR, U_GR + 1, U_GR + 2, U_GR + 4), (U_GR + 3, U_GR + 5, U_GR + 6, U_GR + 7)
U_Z = (U_CO + 1, U_CO + 3, U_GQK, U_GQK + 1, U_GO[0], U_GO[1], U_GO[3])
U_F = (U_FFN, U_FFN + 1)


def u_gate(g):
    return U_FFN if g == 0 else U_FFN + 2 + 3 * (g - 1)


def u_down(g):
    return U_FFN + 4 + 3 * g if g < FGROUPS - 1 else U_END - 1


class Chain:

    def __init__(self, sem):
        self.sem, self.n = sem, 0

    def step(self, eng, ins):
        self.n += 1
        ins.then_inc(self.sem, 1)
        eng.wait_ge(self.sem, self.n)


def after(eng, sem, value, base=0):
    if value > 0:
        eng.wait_ge(sem, base + value)


def hybrid_block(nc, I, out):
    ctx = ExitStack()
    with ctx:
        base = (nc.sbuf_base + 31) // 32 * 32

        def at(name, shape, off, dt=F32):
            return nc.alloc_sbuf_tensor_at(name, shape, dt, offset=base + off)

        def sem(name):
            return ctx.enter_context(nc.semaphore(name))

        C0 = 0
        A0 = 3200
        A1 = A0 + KT * T * 4
        S0 = A0 + 2 * KT * T * 4
        SLOT = 2 * KT * UNIT * 4
        W0 = S0 + 3 * SLOT
        O0 = W0 + 16384
        Z0 = O0 + KT * T * 4

        ident = at("ident", [P, P], C0)
        ones_mean = at("ones_mean", [P, P], C0 + 512)
        NV = TAPS + 6
        conv_vec = at("conv_vec", [P, KT, NV], C0 + 1024)
        causal = at("causal", [P, P], C0 + 1024)
        inv_count = at("inv_count", [P, 16], C0 + 2208)
        stat = at("stat", [P, 96], C0 + 2272)
        a1_raw = at("a1_raw", [P, KT, RANK], C0 + 2656)
        f_raw = at("f_raw", [P, KT, AH], C0 + 2656)

        xh = at("xh", [P, KT, T], A0, F32R)
        xl = at("xl", [P, KT, T], A0 + KT * T * 4, F32R)
        raw = at("raw", [P, KT, UNIT], W0)
        raw_z = at("raw_z", [P, KT, UNIT], Z0 + KT * (T + PAD) * 4)
        SLOTS = [S0, S0 + SLOT, S0 + 2 * SLOT, Z0, Z0 + SLOT, W0]
        wh = [at(f"wh{s}", [P, KT, UNIT], o, F32R) for s, o in enumerate(SLOTS)]
        wl = [at(f"wl{s}", [P, KT, UNIT], o + SLOT // 2, F32R) for s, o in enumerate(SLOTS)]
        wh_rows, wl_rows = [[w[:].rearrange("p k n -> p (k n)").rearrange("p (f n) -> p f n", f=2) for w in part] for part in (wh, wl)]

        x_stage = at("x_stage", [P, 4, D], O0)
        vec_rows = at("vec_rows", [NV, D], Z0 + KT * (T + PAD) * 4)
        silu_z = at("silu_z", [P, KT, T], O0)
        glu = at("glu", [P, KT, T + PAD], Z0)
        gate_part = at("gate_part", [P, T], Z0 + KT * (T + PAD) * 4 + T * 4)
        tap_sum = [at(f"tap_sum{e}", [P, T], S0 + 2 * SLOT + e * T * 4) for e in range(2)]
        tap_part = [at("tap_part0", [P, T], W0 + 8192), at("tap_part1", [P, T], O0 + (KT - 1) * T * 4)]
        side_sum = [at("side_sum0", [P, T], S0 + 2 * SLOT + 2 * T * 4), at("side_sum1", [P, T], Z0 + KT * (T + PAD) * 4)]
        conv_sq = at("conv_sq", [P, KT, T], A1)
        conv_std = at("conv_std", [P, T], A0)
        CO_SLOTS = (0, 1, 2, 5)
        rows3 = [at(f"rows3_{s}", [P, D], O0 + 12288 + s * 4096) for s in range(3)]
        gain3 = [at(f"gain3_{s}", [P, D], O0 + s * 4096) for s in range(3)]

        qk = at("qk", [P, 2 * GH, T], Z0)
        arg_a = at("arg_a", [P, 4, GH, P], Z0 + 33280)
        arg_b = at("arg_b", [P, LEVELS - 4, GH, P], W0)
        a1h = at("a1h", [P, KT, P], O0, F32R)
        a1l = at("a1l", [P, KT, P], O0 + 4096, F32R)
        a1_pad = at("a1_pad", [P, KT, P], O0 + 8192)
        decay = at("decay", [P, GH, P], Z0 + 41472)
        v_rows = at("v_rows", [P, NX, D], O0)
        k_decayed = at("k_decayed", [P, GH, P], S0 + 2 * SLOT)
        k_rows = at("k_rows", [P, GH, P], S0 + 2 * SLOT + 2048)
        att = at("att", [P, GH, P], S0 + 2 * SLOT + 4096)
        state = at("state", [P, GH, GV], S0 + 2 * SLOT + 6144)
        v_meta = at("v_meta", [META, D], S0 + 2 * SLOT + 6144)
        a1 = at("a1", [33, T], S0 + 2 * SLOT + 10240)
        pair_mask = at("pair_mask", [P, LEVELS, 64], S0 + 2 * SLOT + 14400, I32)
        pair_mask_f = at("pair_mask_f", [P, LEVELS, 64], Z0 + 33280)
        w_a2 = at("w_a2", [33, GH * GK], W0 + 8192)
        q_decayed = at("q_decayed", [P, GH, P], W0 + 8192 + 2048)
        soft = at("soft", [P, GH, P], W0 + 8192 + 4096)
        norm_bc = at("norm_bc", [P, GV], W0 + 8192 + 6144)
        o_junk = at("o_junk", [P, GV], W0 + 8192 + 4096)
        r_silu = [at("r_silu0", [P, GV], W0 + 8192 + 7168), at("r_silu1", [P, GV], C0 + 1024)]
        GO_SLOTS = (3, 4, 2, 0)
        rows5 = [at(f"rows5_{s}", [P, D], Z0 + 32768 + s * 4096) for s in range(2)]
        gain5 = [at("gain5_0", [P, D], W0 + 8192), at("gain5_1", [P, D], W0 + 12288), v_rows[:, 0, :]]

        aqk = at("aqk", [P, KT, SEQ], Z0)
        fh = at("fh", [P, KT, P], Z0 + 32768, F32R)
        fl = at("fl", [P, KT, P], Z0 + 32768 + 4096, F32R)
        f_pad = at("f_pad", [P, KT, P], O0 + 12288)
        f_logit = at("f_logit", [AH, SEQ], O0)
        f_soft = at("f_soft", [AH, SEQ], O0 + 4096)
        f_cum = at("f_cum", [AH, SEQ], O0 + 8192)
        v6 = at("v6", [P, NX, HALF], W0)
        pool_u = at("pool_u", [P, 4, SEQ], S0 + 2 * SLOT)
        cum_bc = at("cum_bc", [P, AH, SEQ], O0)
        score = [at(f"score{s}", [P, SEQ], A0 + 32768 + s * 4096) for s in range(3)]
        prob_t = [at(f"prob_t{s}", [P, SEQ], A0 + 45056 + s * 4096) for s in range(2)]
        mix_row = [at(f"mix_row{s}", [P, D], A0 + 53248 + s * 4096) for s in range(2)]
        pool_tmp = [at(f"pool_tmp{s}", [P, SEQ], Z0 + 32768 + s * 4096) for s in range(2)]
        mix_gain = at("mix_gain", [P, D], Z0 + 32768)
        pool_gain = at("pool_gain", [P, HALF], Z0 + 32768 + 4096)
        w_pool = at("w_pool", [P, 4, P], Z0 + 32768 + 6144)
        mix_t = at("mix_t", [P, KT, SEQ], A0)
        mix_sq = at("mix_sq", [P, HALF], Z0 + 40960)
        mo_raw = at("mo_raw", [P, KT, D], S0)
        mo_h, mo_l = at("mo_h", [P, KT, D], Z0, F32R), at("mo_l", [P, KT, D], S0 + 2 * SLOT, F32R)
        scaled7 = [at(f"scaled7_{s}", [P, D], A0 + s * 4096) for s in range(2)]
        normed7 = [at(f"normed7_{s}", [P, D], A0 + 8192 + s * 4096) for s in range(2)]
        rows7 = [at(f"rows7_{s}", [P, D], A0 + 16384 + s * 4096) for s in range(2)]
        raw_f = at("raw_f", [P, KT, UNIT], A0 + 24576)
        gain7 = [at(f"gain7_{s}", [P, D], Z0 + 32768 + s * 4096) for s in range(2)]
        xh7 = at("xh7", [P, KT, T], O0, F32R)
        xl7 = at("xl7", [P, KT, T], A0 + KT * T * 4, F32R)

        ffh = [at(f"ffh{b}", [P, 2, SEQ], A0 + b * 16384, F32R) for b in range(2)]
        ffl = [at(f"ffl{b}", [P, 2, SEQ], A0 + b * 16384 + 8192, F32R) for b in range(2)]
        ff_acc = at("ff_acc", [P, NX, D], Z0)
        ff_silu = at("ff_silu", [P, 2, SEQ], Z0 + 32768)
        ff_prod = [at(f"ff_prod{t}", [P, SEQ], W0 + 8192 + t * 4096) for t in range(2)]

        ple_raw = at("ple_raw", [P, KT, D], O0)
        ple_h, ple_l = at("ple_h", [P, KT, D], S0 + SLOT, F32R), at("ple_l", [P, KT, D], A1, F32R)
        p_stage = at("p_stage", [P, NX, 2 * P], Z0 + 32768)
        p_t = at("p_t", [P, 2, SEQ], W0 + 8192)
        w_ple_proj = at("w_ple_proj", [P, 2, D], W0)
        gain9 = [at(f"gain9_{s}", [P, D], A0 + 16384 + s * 4096) for s in range(2)]
        rows9 = [at(f"rows9_{s}", [P, D], A0 + 24576 + s * 4096) for s in range(2)]
        act9h = [at(f"act9h_{s}", [P, KT, P], S0 + s * 8192, F32R) for s in range(2)]
        act9l = [at(f"act9l_{s}", [P, KT, P], S0 + 4096 + s * 8192, F32R) for s in range(2)]
        out_row = [at(f"out_row{s}", [P, D], O0 + s * 4096) for s in range(2)]
        e_row = at("e_row", [P, D], O0 + 8192)
        sq9 = at("sq9", [P, D], O0 + 12288)
        sq9e = at("sq9e", [P, D], O0 + 16384)

        PS = ctx.enter_context(nc.psum_tensor("PS", [P, 8, 512], F32))

        def banks(b, n, cols=None):
            return PS[:, b:b + n, :].rearrange("p b n -> p (b n)")[:, 0:cols or n * 512]

        def blocks(b):
            return PS[:, b:b + 2, :].rearrange("p b (q n) -> p (b q) n", n=P)

        h1_rows = nc.dram_tensor("h1_rows", (SEQ, D), F32, kind="Internal").ap()
        h2_rows = nc.dram_tensor("h2_rows", (SEQ, D), F32, kind="Internal").ap()
        h3_rows = nc.dram_tensor("h3_rows", (SEQ, D), F32, kind="Internal").ap()
        cum_rows = nc.dram_tensor("cum_rows", (AH, SEQ), F32, kind="Internal").ap()
        x_rows = I["x"][0]
        meta_rows = I["meta"]

        def row_tile(dram, j):
            return dram[j * P:(j + 1) * P, :]

        def bcast_row(vec, n):
            return vec.rearrange("(o n) -> o n", o=1).broadcast_to([P, n])

        def unit_src(w, col):
            return w[:, col:col + UNIT].rearrange("(k p) n -> p k n", p=P)

        raw_ready, unit_hi, unit_ready = sem("raw_ready"), sem("unit_hi"), sem("unit_ready")

        turned, part_hi, part_lo = sem("turned"), sem("part_hi"), sem("part_lo")
        H1, N5, N7 = 9, 18, 26
        dense_done, dense_left = sem("dense_done"), sem("dense_left")
        row_var, row_std = sem("row_var"), sem("row_std")
        Y5, Y7, Y9 = 9, 17, 25
        matrix_in, gain_in = sem("matrix_in"), sem("gain_in")
        matrix_hi, matrix_lo = sem("matrix_hi"), sem("matrix_lo")
        M9 = 4
        W9 = 16
        G5, G6, G7, G9 = 48, 96, 160, 192
        rows_in, rows_out = [sem(f"rows_in{s}") for s in range(3)], [sem(f"rows_out{s}") for s in range(3)]
        ROWS5, ROWS7, ROWS9 = 48, 112, 176
        H1_OUT, H2_OUT, H3_OUT, OUT = [32, 48, 48], [32, 48], [96, 112], [160, 176]
        dve_own, act_own, pool_own = Chain(sem("dve_own")), Chain(sem("act_own")), Chain(sem("pool_own"))

        raw_z_ready, raw_f_ready = sem("raw_z_ready"), sem("raw_f_ready")

        def raw_of(u):
            if u in U_Z:
                return raw_z, raw_z_ready, U_Z
            if u in U_F:
                return raw_f, raw_f_ready, U_F
            return raw, raw_ready, [v for v in range(U_END) if v not in U_Z + U_F]

        def load_rows(sp, u, w, q):
            buf, ready, _ = raw_of(u)
            sp.dma_start(buf[:].rearrange("p k n -> p (k n)").rearrange("p (f n) -> p f n", f=2),
                         w[q * UNIT:(q + 1) * UNIT, :].rearrange("(f p) n -> p f n", p=P)).then_inc(ready, 16)

        def load_unit(sp, u):
            buf, ready, units = raw_of(u)
            if u != units[0]:
                sp.wait_ge(unit_ready, units[units.index(u) - 1] + 1)
            if u < 8:
                for s in range(2):
                    sp.dma_start(raw[:, :, s * P:(s + 1) * P], I["conv_w_in"][0][:, u * P + s * D:u * P + s * D + P]
                                       .rearrange("(k p) n -> p k n", p=P)).then_inc(raw_ready, 16)
                return
            if u < U_CO:
                src = unit_src(I["conv_w_in"][0], 2 * D + (u - 8) * UNIT)
            elif u < U_GQK:
                load_rows(sp, u, I["conv_w_out"][0], u - U_CO)
                return
            elif u in U_GO:
                load_rows(sp, u, I["gla_w_out"][0], U_GO.index(u))
                return
            elif u < U_AQK:
                src = unit_src(I["gla_w_in"][0], (u - U_GQK if u < U_GR else U_GR - U_GQK + U_R.index(u)) * UNIT)
            elif u < U_AU:
                src = unit_src(I["w_in_2"][0], (u - U_AQK) * UNIT)
            elif u < U_AV:
                src = unit_src(I["w_in_2"][0], 3 * HALF + AH + (u - U_AU) * UNIT)
            elif u < U_FFN:
                src = unit_src(I["w_in_2"][0], 2 * HALF + (u - U_AV) * UNIT)
            else:
                n = u - U_FFN - 2
                if u == U_END - 1 or (n >= 0 and n % 3 == 2):
                    g = FGROUPS - 1 if u == U_END - 1 else n // 3
                    load_rows(sp, u, I["w_ffn_down_2"][0], g)
                    return
                g, up = (0, u - U_FFN) if n < 0 else (1 + n // 3, n % 3)
                src = unit_src(I["w_ffn_up_2" if up else "w_ffn_gate_2"][0], g * UNIT)
            sp.dma_start(buf[:], src).then_inc(ready, 16)

        def raw_count(u):
            units = raw_of(u)[2]
            return 16 * (units.index(u) + 1 + (min(u + 1, 8) if u not in U_Z + U_F else 0))

        def unit_high(act, u, slot):
            buf, ready, _ = raw_of(u)
            act.wait_ge(ready, raw_count(u))
            nc.scalar.copy(wh[slot][:], buf[:]).then_inc(unit_hi, 1)

        def unit_low(pool, u, slot):
            pool.wait_ge(unit_hi, u + 1)
            nc.gpsimd.tensor_tensor(wl[slot][:], raw_of(u)[0][:], wh[slot][:].bitcast(F32), ALU.subtract).then_inc(unit_ready, 1)

        def split_unit(pool, u, slot):
            buf, ready, _ = raw_of(u)
            pool.wait_ge(ready, raw_count(u))
            nc.gpsimd.tensor_copy(wh[slot][:], buf[:]).then_inc(unit_hi, 1)
            unit_low(pool, u, slot)

        def split_unit_fast(dve, u, slot):
            buf, ready, _ = raw_of(u)
            dve.wait_ge(ready, raw_count(u))
            nc.vector.tensor_copy(wh[slot][:], buf[:]).then_inc(unit_hi, 1)
            dve.wait_ge(unit_hi, u + 1)
            nc.vector.tensor_tensor(wl[slot][:], buf[:], wh[slot][:].bitcast(F32), ALU.subtract).then_inc(unit_ready, 1)

        def products(terms, chunks, out_of):
            for n, (sh, sl, mh, ml) in enumerate(terms):
                for m, (s, x) in enumerate(((sh, mh), (sh, ml), (sl, mh))):
                    for c, (c0, cn) in enumerate(chunks):
                        last = nc.tensor.matmul(out_of(c, cn), s, x[:, c0:c0 + cn], start=n == 0 and m == 0,
                                                stop=n == len(terms) - 1 and m == 2)
            return last

        def channel_part(h, l, t, chunks, c, bank, x=(xh, xl)):
            c0, cn = chunks[c]
            cols = slice(t * P, (t + 1) * P)
            return products([(h[:, k, cols], l[:, k, cols], x[0][:, k, c0:c0 + cn], x[1][:, k, c0:c0 + cn]) for k in range(KT)],
                            [(0, cn)], lambda _, n: PS[:, bank + c, 0:n])

        def channel_tile(h, l, t, chunks, bank, x=(xh, xl)):
            return products([(h[:, k, t * P:(t + 1) * P], l[:, k, t * P:(t + 1) * P], x[0][:, k, :], x[1][:, k, :])
                             for k in range(KT)], chunks, lambda c, cn: PS[:, bank + c, 0:cn])

        def token_tile(slot, c0, bank):
            return products([(xh[:, k, c0:c0 + P], xl[:, k, c0:c0 + P], wh[slot][:, k, :], wl[slot][:, k, :])
                             for k in range(KT)], [(0, UNIT)], lambda c, cn: PS[:, bank, 0:cn])

        def dense_split(act_of, w_of, bank):
            return products([act_of(k) + w_of(k) for k in range(KT)], [(0, HALF), (HALF, HALF)], lambda c, cn: PS[:, bank + c, :])

        def dense_stage(act_of, w_of, bank, first=False, last=False):
            for k in range(KT):
                for half in range(2):
                    ins = nc.tensor.matmul(PS[:, bank + half, :], act_of(k), w_of(k)[:, half * HALF:(half + 1) * HALF],
                                           start=first and k == 0, stop=last and k == KT - 1)
            return ins

        def of_slots(slots, k):
            return wh_rows[slots[k // 2]][:, k % 2, :], wl_rows[slots[k // 2]][:, k % 2, :]

        def turn_row(src, rows, bank):
            for k in range(KT):
                last = nc.tensor.transpose(blocks(bank)[:, k, 0:rows], src[0:rows, k * P:(k + 1) * P], ident[0:rows, 0:rows])
            return last

        const_ready, vec_in, vec_turned, vec_ready = sem("const_ready"), sem("vec_in"), sem("vec_turned"), sem("vec_ready")
        x_in = [sem(f"x_in{s}") for s in range(4)]

        def consts_pool(pool):
            own = Chain(const_ready)
            own.step(pool, nc.gpsimd.memset(ident[:], 0.0))
            own.step(pool, nc.gpsimd.affine_select(out=ident[:], in_=ident[:], compare_op=ALU.not_equal, fill=1.0, base=0,
                                             pattern=[[-1, P]], channel_multiplier=1))
            own.step(pool, nc.gpsimd.memset(ones_mean[:], 1.0 / D))

        def inputs_sync(sp):
            rows = [(0, TAPS, I["conv_w_dw"][0]), (TAPS, 1, I["conv_b_dw"]), (TAPS + 1, 1, I["conv_norm_g"]),
                    (TAPS + 2, 1, I["conv_norm_b"]), (TAPS + 3, 3, I["conv_b_in"][0].rearrange("(r n) -> r n", r=3))]
            for r0, n, src in rows:
                sp.dma_start(vec_rows[r0:r0 + n, :], src).then_inc(vec_in, 16)
            for t, (c0, n) in enumerate(TILES):
                after(sp, turned, t - 3)
                src = meta_rows if t == 0 else row_tile(x_rows, t - 1)
                sp.dma_start(x_stage[0:n, t % 4, :], src).then_inc(x_in[t % 4], 16)
                if t == 1:
                    load_unit(sp, 0)

        def inputs_tensor(pe):
            pe.wait_ge(const_ready, 3)
            pe.wait_ge(vec_in, 80)
            for k in range(KT):
                last = nc.tensor.transpose(PS[:, 0, k * NV:(k + 1) * NV], vec_rows[:, k * P:(k + 1) * P], ident[0:NV, 0:NV])
            last.then_inc(vec_turned, 1)
            for t, (c0, n) in enumerate(TILES):
                pe.wait_ge(x_in[t % 4], 16 * (t // 4 + 1))
                after(pe, part_lo, t - 1)
                turn_row(x_stage[:, t % 4, :], n, 4 + 2 * (t % 2)).then_inc(turned, 1)

        def inputs_scalar(act):
            for t, (c0, n) in enumerate(TILES):
                act.wait_ge(turned, t + 1)
                nc.scalar.copy(xh[:, :, c0:c0 + n], blocks(4 + 2 * (t % 2))[:, :, 0:n]).then_inc(part_hi, 1)
                if t == 4:
                    unit_high(act, 0, 0)

        def inputs_vector(dve):
            dve.wait_ge(vec_turned, 1)
            nc.vector.tensor_copy(conv_vec[:].rearrange("p k r -> p (k r)"), PS[:, 0, 0:KT * NV]).then_inc(vec_ready, 1)
            for t, (c0, n) in enumerate(TILES):
                dve.wait_ge(part_hi, t + 1)
                nc.vector.tensor_tensor(xl[:, :, c0:c0 + n], blocks(4 + 2 * (t % 2))[:, :, 0:n],
                                        xh[:, :, c0:c0 + n].bitcast(F32), ALU.subtract).then_inc(part_lo, 1)

        conv_tile, conv_left = sem("conv_tile"), sem("conv_left")
        pads_ready, glu_ready, tap_done, conv_ready = sem("pads_ready"), sem("glu_ready"), sem("tap_done"), sem("conv_ready")

        def conv_in_sync(sp):
            for u in range(1, U_CO + 1):
                load_unit(sp, u)

        def conv_in_tensor(pe):
            pe.wait_ge(part_lo, len(TILES))
            pe.wait_ge(vec_ready, 1)
            with pe.Fori(0, U_CO // 2) as i:
                for slot in range(2):
                    pe.wait_ge(unit_ready, i * 2 + slot + 1)
                    for t in range(2):
                        pe.wait_ge(conv_left, i * 4 + 2 * slot + t + 1)
                        channel_tile(wh[slot], wl[slot], t, CHUNKS3, 3 * t).then_inc(conv_tile, 1)

        def out_of_banks(eng_op, dst, bank, width=352, cols=T):
            eng_op(dst[:, 0:2 * width].rearrange("p (c n) -> p c n", c=2), PS[:, bank:bank + 2, 0:width])
            return eng_op(dst[:, 2 * width:cols], PS[:, bank + 2, 0:cols - 2 * width])

        tap_scaled, tap_added = sem("tap_scaled"), sem("tap_added")
        VEC_TAPS = TAPS - SIDE_TAPS

        def conv_in_scalar(act):
            act.wait_ge(vec_ready, 1)
            bias = lambda r, k: conv_vec[:, k, TAPS + 3 + r:TAPS + 4 + r]

            def scale_taps(k, taps):
                for j in taps:
                    act.wait_ge(glu_ready, k + 1)
                    after(act, tap_added, k * SIDE_TAPS + j - 1)
                    w = conv_vec[:, k, VEC_TAPS + j:VEC_TAPS + j + 1]
                    nc.scalar.activation(tap_part[(k * SIDE_TAPS + j) % 2][:], glu[:, k, VEC_TAPS + j:VEC_TAPS + j + T], ACT.Copy,
                                         scale=w).then_inc(tap_scaled, 1)

            unit_high(act, 1, 1)
            for u in range(8):
                act.wait_ge(conv_tile, 2 * u + 1)
                out_of_banks(lambda o, i: nc.scalar.activation(o, i, ACT.Identity, bias=bias(0, u)), glu[:, u, PAD:], 0)\
                    .then_inc(conv_left, 1)
                if u > 0:
                    scale_taps(u - 1, range(0, 4))
                act.wait_ge(conv_tile, 2 * u + 2)
                after(act, glu_ready, u)
                out_of_banks(lambda o, i: nc.scalar.activation(o, i, ACT.Sigmoid, bias=bias(1, u)), gate_part, 3)\
                    .then_inc(conv_left, 1)
                unit_high(act, u + 2, u % 2)
                if u > 0:
                    scale_taps(u - 1, range(4, SIDE_TAPS))
            for k in range(KT):
                act.wait_ge(conv_tile, 16 + k + 1)
                if k == KT - 1:
                    act.wait_ge(tap_added, KT * SIDE_TAPS)
                out_of_banks(lambda o, i: nc.scalar.activation(o, i, ACT.Silu, bias=bias(2, k)), silu_z[:, k, :], 3 * (k % 2))\
                    .then_inc(conv_left, 1)
                if k == 0:
                    scale_taps(KT - 1, range(0, 4))
                if k % 2 and 8 + k // 2 + 2 < U_CO:
                    unit_high(act, 8 + k // 2 + 2, k // 2 % 2)
                if k == 1:
                    scale_taps(KT - 1, range(4, SIDE_TAPS))

        def conv_in_pool(pool):
            def add_taps(k, taps):
                acc = side_sum[k % 2]
                if 0 in taps:
                    after(pool, conv_ready, k - 1)
                for j in taps:
                    n = k * SIDE_TAPS + j
                    pool.wait_ge(tap_scaled, n + 1)
                    part = tap_part[n % 2][:]
                    if j == 0:
                        ins = nc.gpsimd.tensor_copy(acc[:], part)
                    else:
                        pool.wait_ge(tap_added, n)
                        ins = nc.gpsimd.tensor_tensor(acc[:], acc[:], part, ALU.add)
                    ins.then_inc(tap_added, 1)

            nc.gpsimd.memset(glu[:, :, 0:PAD], 0.0).then_inc(pads_ready, 1)
            unit_low(pool, 0, 0)
            unit_low(pool, 1, 1)
            for u in range(U_CO):
                if 1 <= u <= 8:
                    add_taps(u - 1, range(0, 4))
                if u < 8:
                    pool.wait_ge(conv_left, 2 + 2 * u + 2)
                    x = glu[:, u, PAD:]
                    nc.gpsimd.tensor_tensor(x, x, gate_part[:], ALU.mult).then_inc(glu_ready, 1)
                if u + 2 < U_CO:
                    unit_low(pool, u + 2, u % 2)
                if 1 <= u <= 8:
                    add_taps(u - 1, range(4, SIDE_TAPS))

        def conv_vector(dve):
            nc.vector.memset(stat[:, 95:96], 0.0).then_inc(conv_left, 2)
            dve.wait_ge(pads_ready, 1)
            n = VEC_TAPS + 1

            def tile(k, side):
                g = glu[:, bass.ds(k, 1), :].rearrange("p o t -> p (o t)")
                vec = conv_vec[:, bass.ds(k, 1), :].rearrange("p o r -> p (o r)")
                dve.wait_ge(glu_ready, k + 1)
                for j in range(VEC_TAPS):
                    if j >= 2:
                        dve.wait_ge(tap_done, k * n + (j - 1))
                    acc = tap_sum[j % 2]
                    if j == 0:
                        ins = nc.vector.tensor_scalar(acc[:], g[:, 0:T], vec[:, 0:1], vec[:, TAPS:TAPS + 1], ALU.mult, ALU.add)
                    elif j == 1:
                        ins = nc.vector.tensor_scalar(acc[:], g[:, 1:1 + T], vec[:, 1:2], None, ALU.mult)
                    else:
                        ins = nc.vector.scalar_tensor_tensor(out=acc[:], in0=g[:, j:j + T], scalar=vec[:, j:j + 1], in1=acc[:],
                                                             op0=ALU.mult, op1=ALU.add)
                    ins.then_inc(tap_done, 1)
                dve.wait_ge(tap_done, k * n + VEC_TAPS)
                nc.vector.tensor_tensor(tap_sum[0][:], tap_sum[0][:], tap_sum[1][:], ALU.add).then_inc(tap_done, 1)
                dve.wait_ge(tap_done, k * n + n)
                dve.wait_ge(tap_added, k * SIDE_TAPS + SIDE_TAPS)
                nc.vector.tensor_tensor(g[:, PAD:], tap_sum[0][:], side_sum[side][:], ALU.add).then_inc(conv_ready, 1)
                dve.wait_ge(conv_ready, k + 1)

            with dve.Fori(0, KT // 2) as i:
                for side in range(2):
                    tile(i * 2 + side, side)

        (mean_ready, centered, squared, var_ready, std_ready, conv_normed, conv_silu, conv_gated) = (
            sem(s) for s in ("mean_ready", "centered", "squared", "var_ready", "std_ready", "conv_normed", "conv_silu", "conv_gated"))

        gated_hi, gated_lo, summed = sem("gated_hi"), sem("gated_lo"), sem("summed")
        tile_sum = tap_part[0]

        def conv_chunk(c):
            c0, cn = CHUNKS3[c]
            return glu[:, :, PAD + c0:PAD + c0 + cn]

        def fine(c):
            c0, cn = CHUNKS4[c]
            return glu[:, :, PAD + c0:PAD + c0 + cn]

        def over_channels(ap, n):
            return ap.rearrange("p (o n) -> p o n", o=1).broadcast_to([P, KT, n])

        def conv_norm_tensor(pe):
            pe.wait_ge(conv_left, 2 + 24)
            pe.wait_ge(summed, KT - 1)
            for c, (c0, cn) in enumerate(CHUNKS3):
                nc.tensor.matmul(PS[:, c, 0:cn], ones_mean[:], tile_sum[:, c0:c0 + cn], start=True, stop=True).then_inc(mean_ready, 1)
            for c, (c0, cn) in enumerate(CHUNKS3):
                pe.wait_ge(squared, c + 1)
                for k in range(KT):
                    last = nc.tensor.matmul(PS[:, 3 + c, 0:cn], ones_mean[:], conv_sq[:, k, c0:c0 + cn], start=k == 0, stop=k == KT - 1)
                last.then_inc(var_ready, 1)

        def conv_norm_vector(dve):
            for c, (c0, cn) in enumerate(CHUNKS3):
                dve.wait_ge(mean_ready, c + 1)
                nc.vector.tensor_tensor(conv_chunk(c), conv_chunk(c), over_channels(PS[:, c, 0:cn], cn), ALU.subtract)\
                    .then_inc(centered, 1)
            def normalise(c):
                c0, cn = CHUNKS4[c]
                dve.wait_ge(std_ready, max(c, 1))
                rstd = conv_std[:, c0:c0 + cn]
                dve_own.step(dve, nc.vector.reciprocal(rstd, rstd))
                nc.vector.tensor_tensor(fine(c), fine(c), over_channels(rstd, cn), ALU.mult).then_inc(conv_normed, 1)

            def gate(c):
                c0, cn = CHUNKS4[c]
                dve.wait_ge(conv_silu, KT * (c + 1))
                nc.vector.tensor_tensor(fine(c), fine(c), silu_z[:, :, c0:c0 + cn], ALU.mult).then_inc(conv_gated, 1)

            def low(c):
                c0, cn = CHUNKS4[c]
                dve.wait_ge(gated_hi, c + 1)
                cols = slice(c0, c0 + cn)
                nc.vector.tensor_tensor(xl[:, :, cols], fine(c), xh[:, :, cols].bitcast(F32), ALU.subtract).then_inc(gated_lo, 1)

            def matrix_high(q):
                buf, ready, _ = raw_of(U_CO + q)
                dve.wait_ge(unit_hi, U_CO + q)
                dve.wait_ge(ready, raw_count(U_CO + q))
                nc.vector.tensor_copy(wh[CO_SLOTS[q]][:], buf[:]).then_inc(unit_hi, 1)

            matrix_high(1)
            matrix_high(2)
            normalise(0)
            normalise(1)
            dve.wait_ge(unit_ready, U_CO + 3)
            matrix_high(3)
            gate(0)
            gate(1)
            low(0)
            normalise(2)
            low(1)
            normalise(3)
            gate(2)
            low(2)
            gate(3)
            low(3)

        def conv_norm_scalar(act):
            def squares(c):
                c0, cn = CHUNKS3[c]
                act.wait_ge(centered, c + 1)
                nc.scalar.activation(conv_sq[:, :, c0:c0 + cn], conv_chunk(c), ACT.Square).then_inc(squared, 1)

            def deviation(c):
                c0, cn = CHUNKS3[c]
                act.wait_ge(var_ready, c + 1)
                nc.scalar.activation(conv_std[:, c0:c0 + cn], PS[:, 3 + c, 0:cn], ACT.Sqrt, bias=LN_EPS).then_inc(std_ready, 1)

            def silu(c):
                act.wait_ge(conv_normed, c + 1)
                for k in range(KT):
                    x = fine(c)[:, k, :]
                    nc.scalar.activation(x, x, ACT.Silu, bias=conv_vec[:, k, TAPS + 2:TAPS + 3],
                                         scale=conv_vec[:, k, TAPS + 1:TAPS + 2]).then_inc(conv_silu, 1)

            def high(c):
                c0, cn = CHUNKS4[c]
                act.wait_ge(conv_gated, c + 1)
                nc.scalar.copy(xh[:, :, c0:c0 + cn], fine(c)).then_inc(gated_hi, 1)

            unit_high(act, U_CO, CO_SLOTS[0])
            squares(0)
            squares(1)
            squares(2)
            deviation(0)
            silu(0)
            silu(1)
            high(0)
            deviation(1)
            high(1)
            deviation(2)
            silu(2)
            high(2)
            silu(3)
            high(3)

        def conv_norm_pool(pool):
            pool.wait_ge(tap_added, KT * SIDE_TAPS)
            for k in range(1, KT):
                pool.wait_ge(conv_ready, k + 1)
                after(pool, summed, k - 1)
                nc.gpsimd.tensor_tensor(tile_sum[:], (glu[:, 0, PAD:] if k == 1 else tile_sum[:]), glu[:, k, PAD:], ALU.add)\
                    .then_inc(summed, 1)
            for q in range(4):
                unit_low(pool, U_CO + q, CO_SLOTS[q])

        a1_in, gqk_tile = sem("a1_in"), sem("gqk_tile")
        QK_SLOTS = (4, 1, 0, 1)
        h1_done = sem("h1_done")
        STATS, MEAN, VAR, STD, RSTD = stat[:, 0:12], stat[:, 12:13], stat[:, 13:14], stat[:, 14:15], stat[:, 15:16]

        def conv_out_sync(sp):
            sp.dma_start(a1_raw[:], I["gla_w_in"][0][:, 3 * D:3 * D + RANK].rearrange("(k p) n -> p k n", p=P)).then_inc(a1_in, 16)
            sp.wait_ge(conv_ready, KT)
            for u in range(U_CO + 1, U_GQK + 1):
                load_unit(sp, u)
            sp.wait_ge(conv_gated, len(CHUNKS4))
            for t in range(3):
                src = meta_rows if t == 0 else row_tile(x_rows, t - 1)
                sp.dma_start(rows3[t][0:TILES[t][1], :], src).then_inc(rows_in[t], 16)
                if t == 0:
                    sp.dma_start(gain3[0][:], bcast_row(I["conv_b_out"][0], D)).then_inc(gain_in, 16)
            sp.wait_ge(gain_in, 16)
            for s, vec in enumerate((I["post_ln_g"][0], I["post_ln_b"][0])):
                sp.dma_start(gain3[s + 1][:], bcast_row(vec, D)).then_inc(gain_in, 16)
            load_unit(sp, U_GQK + 1)
            for t, (c0, n) in enumerate(TILES):
                s = t % 3
                sp.wait_ge(h1_done, t + 1)
                if t > 0:
                    sp.dma_start(row_tile(h1_rows, t - 1), rows3[s][:]).then_inc(rows_out[s], 16)
                if t + 3 < len(TILES):
                    after(sp, rows_out[s], 16 * ((t - 1) // 3 + 1))
                    sp.wait_ge(turned, H1 + t + 1)
                    sp.dma_start(rows3[s][:], row_tile(x_rows, t + 2)).then_inc(rows_in[s], 16)

        def conv_out_tensor(pe):
            def turn(t):
                pe.wait_ge(h1_done, t + 1)
                after(pe, part_lo, t, H1)
                turn_row(rows3[t % 3], TILES[t][1], 6).then_inc(turned, 1)

            pe.wait_ge(unit_hi, U_GQK)
            pe.wait_ge(gated_hi, 1)
            pe.wait_ge(std_ready, 1)
            dense_stage(lambda k: xh[:, k, 0:P], lambda k: of_slots(CO_SLOTS, k)[0], 0, first=True)
            pe.wait_ge(unit_ready, U_GQK)
            dense_stage(lambda k: xh[:, k, 0:P], lambda k: of_slots(CO_SLOTS, k)[1], 0)
            pe.wait_ge(gated_lo, 1)
            dense_stage(lambda k: xl[:, k, 0:P], lambda k: of_slots(CO_SLOTS, k)[0], 0, last=True).then_inc(dense_done, 1)
            for t, (c0, n) in enumerate(TILES):
                if t == 0:
                    continue
                pe.wait_ge(gated_lo, sum(c < c0 + P for c, _ in CHUNKS4))
                if t == 2:
                    pe.wait_ge(std_ready, 3)
                after(pe, dense_left, t - 2)
                cols = slice(c0, c0 + P)
                dense_split(lambda k: (xh[:, k, cols], xl[:, k, cols]), lambda k: of_slots(CO_SLOTS, k), 2 * (t % 3)).then_inc(dense_done, 1)
                for done in {1: (), 2: (), 3: (0,), 4: (1,), 5: (2, 3)}.get(t, (t - 2,)):
                    turn(done)

            part = lambda t, c: channel_part(wh[QK_SLOTS[0]], wl[QK_SLOTS[0]], t, CHUNKS3, c, 3 * t)
            pe.wait_ge(unit_ready, U_GQK + 1)
            pe.wait_ge(part_lo, H1 + 4)
            pe.wait_ge(dense_left, 7)
            part(0, 0)
            turn(7)
            pe.wait_ge(dense_left, 9)
            part(1, 0)
            pe.wait_ge(part_lo, H1 + 7)
            part(0, 1)
            turn(8)
            part(1, 1)
            pe.wait_ge(part_lo, H1 + 9)
            part(0, 2).then_inc(gqk_tile, 1)
            part(1, 2).then_inc(gqk_tile, 1)

        def layer_norm_rows(dve, x, n, count, gain, shift):
            for h in range(2):
                last = nc.vector.bn_stats(STATS[0:n, h * 6:(h + 1) * 6], x[0:n, h * HALF:(h + 1) * HALF])
            dve_own.step(dve, last)
            nc.vector.bn_aggr(stat[0:n, 12:14], STATS[0:n, :]).then_inc(row_var, 1)
            dve.wait_ge(row_var, count)
            dve_own.step(dve, nc.vector.scalar_tensor_tensor(out=x[0:n, :], in0=x[0:n, :], scalar=MEAN[0:n, :], in1=gain[0:n, :],
                                                             op0=ALU.subtract, op1=ALU.mult))
            dve.wait_ge(row_std, count)
            dve_own.step(dve, nc.vector.reciprocal(RSTD[0:n, :], STD[0:n, :]))
            return nc.vector.scalar_tensor_tensor(out=x[0:n, :], in0=x[0:n, :], scalar=RSTD[0:n, :], in1=shift[0:n, :],
                                                  op0=ALU.mult, op1=ALU.add)

        def conv_out_vector(dve):
            dve.wait_ge(gain_in, 16)

            def low(t):
                c0, n = TILES[t]
                dve.wait_ge(part_hi, H1 + t + 1)
                nc.vector.tensor_tensor(xl[:, :, c0:c0 + n], blocks(6)[:, :, 0:n],
                                        xh[:, :, c0:c0 + n].bitcast(F32), ALU.subtract).then_inc(part_lo, 1)

            for t, (c0, n) in enumerate(TILES):
                x = rows3[t % 3]
                dve.wait_ge(rows_in[t % 3], 16 * (t // 3 + 1))
                dve.wait_ge(dense_done, t + 1)
                nc.vector.scalar_tensor_tensor(out=x[0:n, :], in0=x[0:n, :], scalar=ALPHA, in1=banks(2 * (t % 3), 2, D)[0:n, :],
                                               op0=ALU.mult, op1=ALU.add).then_inc(dense_left, 1)
                dve.wait_ge(dense_left, t + 1)
                dve_own.step(dve, nc.vector.tensor_tensor(x[0:n, :], x[0:n, :], gain3[0][0:n, :], ALU.add))
                if t == 0:
                    dve.wait_ge(gain_in, 48)
                layer_norm_rows(dve, x, n, t + 1, gain3[1], gain3[2]).then_inc(h1_done, 1)
                if t >= 2:
                    low(t - 2)
            low(len(TILES) - 2)
            low(len(TILES) - 1)

        def conv_out_scalar(act):
            def high(t):
                c0, n = TILES[t]
                act.wait_ge(turned, H1 + t + 1)
                nc.scalar.copy(xh[:, :, c0:c0 + n], blocks(6)[:, :, 0:n]).then_inc(part_hi, 1)

            for t, (c0, n) in enumerate(TILES):
                act.wait_ge(row_var, t + 1)
                nc.scalar.activation(STD[0:n, :], VAR[0:n, :], ACT.Sqrt, bias=LN_EPS).then_inc(row_std, 1)
                if t >= 2:
                    high(t - 2)
            high(len(TILES) - 2)
            high(len(TILES) - 1)

        def conv_out_pool(pool):
            pool.wait_ge(gated_lo, len(CHUNKS4))
            split_unit(pool, U_GQK, QK_SLOTS[0])

        (a1_split, a2_zero, a2_in, mask_ready) = (
            sem(s) for s in ("a1_split", "a2_zero", "a2_in", "mask_ready"))
        (gqk_left, gv_tile, gv_left, a1_ready) = (
            sem(s) for s in ("gqk_left", "gv_tile", "gv_left", "a1_ready"))
        NV_TILES = len(TILES)

        def gla_in_sync(sp):
            sp.wait_ge(dense_done, 9)
            load_unit(sp, U_GQK + 2)
            sp.wait_ge(a2_zero, 1)
            sp.dma_start(w_a2[0:RANK, :], I["gla_w_a2"][0]).then_inc(a2_in, 16)
            sp.dma_start(w_a2[32:33, :], I["gla_b_a"]).then_inc(a2_in, 16)
            sp.dma_start(norm_bc[:], bcast_row(I["gla_norm_g"][0], GV)).then_inc(a2_in, 16)
            for u in range(U_GQK + 3, U_GR + 2):
                load_unit(sp, u)

        def gla_in_pool(pool):
            own = Chain(a1_split)
            pool.wait_ge(dense_done, 9)
            split_unit(pool, U_GQK + 1, QK_SLOTS[1])
            pool.wait_ge(h1_done, 9)
            own.step(pool, nc.gpsimd.memset(a1_pad[:], 0.0))
            pool.wait_ge(a1_in, 16)
            own.step(pool, nc.gpsimd.tensor_copy(a1_pad[:, :, 0:RANK], a1_raw[:]))
            own.step(pool, nc.gpsimd.tensor_copy(a1h[:], a1_pad[:]))
            own.step(pool, nc.gpsimd.tensor_tensor(a1l[:], a1_pad[:], a1h[:].bitcast(F32), ALU.subtract))
            for s in range(3):
                pool.wait_ge(rows_out[s], H1_OUT[s])
            pool.wait_ge(turned, H1 + 9)
            nc.gpsimd.memset(w_a2[:], 0.0).then_inc(a2_zero, 1)
            pool.wait_ge(a2_zero, 1)
            nc.gpsimd.memset(a1[32:33, :], 1.0).then_inc(a1_ready, 1)
            pool.wait_ge(a1_ready, 1)
            split_unit(pool, U_GQK + 2, QK_SLOTS[2])
            own = Chain(mask_ready)
            own.step(pool, nc.gpsimd.memset(pair_mask_f[:], 1.0))
            for l in range(LEVELS):
                b = 64 >> l
                view = pair_mask_f[:, l, :].rearrange("p (n b) -> p n b", b=b)
                own.step(pool, nc.gpsimd.affine_select(out=view, in_=view, compare_op=ALU.is_ge, fill=0.0, base=0,
                                                 pattern=[[-2 * b, 64 // b], [0, b]], channel_multiplier=1))
                own.step(pool, nc.gpsimd.affine_select(out=view, in_=view, compare_op=ALU.is_ge, fill=0.0, base=b - 1,
                                                 pattern=[[2 * b, 64 // b], [0, b]], channel_multiplier=-1))
            own.step(pool, nc.gpsimd.tensor_copy(pair_mask[:], pair_mask_f[:]))
            for u in range(U_GQK + 3, U_GR + 1):
                if u == U_GV + 2:
                    meta_keys(pool)
                before = u - 2
                if before < U_GV:
                    pool.wait_ge(gqk_tile, 2 * (before - U_GQK + 1))
                else:
                    pool.wait_ge(gv_tile, NV_TILES * (before - U_GV + 1))
                split_unit(pool, u, u % 2)

        def gla_in_tensor(pe):
            for n in range(1, 4):
                pe.wait_ge(unit_ready, U_GQK + n + 1)
                for t in range(2):
                    pe.wait_ge(gqk_left, 2 * n + t + 1)
                    channel_tile(wh[QK_SLOTS[n]], wl[QK_SLOTS[n]], t, CHUNKS3, 3 * t).then_inc(gqk_tile, 1)
            pe.wait_ge(a1_split, 4)
            pe.wait_ge(gqk_left, 9)
            channel_tile(a1h, a1l, 0, CHUNKS3, 0).then_inc(gqk_tile, 1)
            pe.wait_ge(gqk_left, 2 + 9)
            pe.wait_ge(a2_in, 48)
            pe.wait_ge(a1_ready, 1)
            gate_logits(pe, 0)
            for h in range(GH):
                pe.wait_ge(unit_ready, U_GV + h + 1)
                for t, (c0, n) in enumerate(TILES):
                    q = h * NV_TILES + t
                    if q == META_AT:
                        turn_keys(pe, 0)
                    if q == META_AT + 2:
                        gate_logits(pe, 1)
                    pe.wait_ge(gv_left, q + 1)
                    token_tile(h % 2, c0, 3 + q % 3).then_inc(gv_tile, 1)

        def gla_in_vector(dve):
            nc.vector.memset(stat[:, 92:93], 0.0).then_inc(gqk_left, 2)
            nc.vector.memset(stat[:, 93:94], 0.0).then_inc(gv_left, 3)

        def gla_in_scalar(act):
            act.wait_ge(conv_gated, len(CHUNKS4))
            act.wait_ge(dense_done, 9)
            for i in range(8):
                act.wait_ge(gqk_tile, i + 1)
                scale = GK ** -0.5 if i < GH else 1.0
                out_of_banks(lambda o, x: nc.scalar.activation(o, x, ACT.Copy, scale=scale), qk[:, i, :], 3 * (i % 2))\
                    .then_inc(gqk_left, 1)
            act.wait_ge(gqk_tile, 9)
            out_of_banks(lambda o, x: nc.scalar.copy(o, x[0:32]), a1[0:32, :], 0).then_inc(gqk_left, 1)
            soft_parts(act, 0)
            decays(act, 0)
            for h in range(GH):
                for t, (c0, n) in enumerate(TILES):
                    q = h * NV_TILES + t
                    act.wait_ge(gv_tile, q + 1)
                    dst = v_meta[:, h * GV:(h + 1) * GV] if t == 0 else v_rows[:, t - 1, h * GV:(h + 1) * GV]
                    nc.scalar.copy(dst, PS[0:n, 3 + q % 3, 0:GV]).then_inc(gv_left, 1)
                    if q == META_AT - 1:
                        copy_keys(act, 0)
                        soft_parts(act, 1)
                    if q == META_AT + 2:
                        decays(act, 1)
                    if q == META_AT + 5:
                        factors(act, 1, 0)

        (z_ready, z_abs, z_min, soft_ready, cum_done, bl_ready, kdec_exp, kdec_ready, ebl_ready, qdec_exp, qdec_ready,
         arg_ready, arg_exp, arg_mul, kt_done, k_rows_done, diag_done, diag_used, pair_done, att_ready, o_done, o_kept,
         s_done, state_ready) = (
            sem(s) for s in ("z_ready", "z_abs", "z_min", "soft_ready", "cum_done", "bl_ready", "kdec_exp", "kdec_ready",
                             "ebl_ready", "qdec_exp", "qdec_ready", "arg_ready", "arg_exp", "arg_mul", "kt_done", "k_rows_done",
                             "diag_done", "diag_used", "pair_done", "att_ready", "o_done", "o_kept", "s_done", "state_ready"))
        r_tile, r_left, r_used = sem("r_tile"), sem("r_left"), sem("r_used")
        EARLY = 2 * NX
        META_AT = 3 * NV_TILES
        SS_O = stat[:, 20:52]
        GROUPS = [range(0, 4), range(4, LEVELS)]
        ARGS = [arg_a, arg_b]
        PAIR_BANK = [1, 4]

        def chunk_sum(c):
            return stat[:, 60 + 4 * (c % 2):64 + 4 * (c % 2)]

        def chunk_decay(c):
            return stat[:, 52 + 4 * (c % 2):56 + 4 * (c % 2)]

        def level_arg(l):
            return ARGS[l // 4][:, l % 4, :, :]

        def pair_scores(l):
            return banks(PAIR_BANK[l // 4], 2).rearrange("p (l h t) -> p l h t", l=4, h=GH)[:, l % 4, :, :]

        def halves(ap, l):
            return ap.rearrange("p h t -> p (h t)").rearrange("p (m e b) -> p m e b", e=2, b=64 >> l)

        def head_blocks(ap, l):
            return ap.rearrange("p h (m e b) -> p h m e b", e=2, b=64 >> l)

        def out_bank(b, h):
            return PS[:, b + h // 2, (h % 2) * GV:(h % 2 + 1) * GV]

        def logits(c):
            return PS[:, 0, :].rearrange("p (h t) -> p h t", h=GH)[:, :, 0:TILES[c][1]]

        def gate_logits(pe, c):
            c0, n = TILES[c]
            after(pe, k_rows_done, c)
            for h in range(GH):
                last = nc.tensor.matmul(PS[:, 0, h * P:h * P + n], w_a2[:, h * GK:(h + 1) * GK], a1[:, c0:c0 + n],
                                        start=True, stop=True)
            last.then_inc(z_ready, 1)

        def turn_keys(pe, c):
            n = TILES[c][1]
            pe.wait_ge(kdec_ready, c + 1)
            pe.wait_ge(z_min, c + 1)
            for h in range(GH):
                last = nc.tensor.transpose(PS[0:n, 0, h * P:(h + 1) * P], k_decayed[:, h, 0:n], ident[:])
            last.then_inc(kt_done, 1)

        def gla_tensor(pe):
            pe.wait_ge(gv_left, 3 + 4 * NV_TILES)

            for c, (c0, n) in enumerate(TILES):
                if 0 < c < NX:
                    turn_keys(pe, c)
                if c > 0:
                    after(pe, diag_used, c - 1)
                    for h in range(GH):
                        last = nc.tensor.matmul(PS[:, 3, h * P:(h + 1) * P], qk[:, GH + h, c0:c0 + n], qk[:, h, c0:c0 + n],
                                                start=True, stop=True)
                    last.then_inc(diag_done, 1)
                if 0 < c < NX:
                    gate_logits(pe, c + 1)
                if c > 0:
                    after(pe, r_left, 2 * (c - 1))
                    for g, group in enumerate(GROUPS):
                        if g == 1:
                            after(pe, o_kept, c - 1)
                        pe.wait_ge(arg_mul, 2 * (c - 1) + g + 1)
                        for l in group:
                            for h in range(GH):
                                odd = halves(level_arg(l)[:, h:h + 1, :], l)[:, :, 1, :]
                                last = nc.tensor.matmul(pair_scores(l)[:, h, :], level_arg(l)[:, h, :], odd, start=True, stop=True)
                        last.then_inc(pair_done, 1)
                    if c == 1:
                        pe.wait_ge(unit_ready, U_GR + 2)
                    pe.wait_ge(att_ready, 2 * c - 1)
                    for h in range(2):
                        token_tile(h, c0, 1 + h).then_inc(r_tile, 1)
                    pe.wait_ge(qdec_ready, c)
                    pe.wait_ge(att_ready, 2 * c)
                    pe.wait_ge(state_ready, c)
                    for h in range(GH):
                        nc.tensor.matmul(out_bank(4, h), att[:, h, :], v_rows[:, c - 1, h * GV:(h + 1) * GV], start=True, stop=False)
                        last = nc.tensor.matmul(out_bank(4, h), q_decayed[:, h, :], state[:, h, :], start=False, stop=True)
                    last.then_inc(o_done, 1)
                if c < NX:
                    pe.wait_ge(k_rows_done, c + 1)
                    after(pe, state_ready, c)
                    v = v_meta if c == 0 else v_rows[:, c - 1, :]
                    for h in range(GH):
                        last = nc.tensor.matmul(out_bank(6, h), k_rows[0:n, h, :], v[:, h * GV:(h + 1) * GV], start=True, stop=True)
                    last.then_inc(s_done, 1)

        def copy_keys(act, c):
            n = TILES[c][1]
            act.wait_ge(kt_done, c + 1)
            after(act, s_done, c)
            nc.scalar.copy(k_rows[0:n].rearrange("p h t -> p (h t)"), PS[0:n, 0, :]).then_inc(k_rows_done, 1)

        def soft_parts(act, c):
            n = TILES[c][1]
            x = soft[:, :, 0:n]
            act.wait_ge(z_ready, c + 1)
            after(act, cum_done, GH * c)
            nc.scalar.activation(x, logits(c), ACT.Abs).then_inc(z_abs, 1)
            act.wait_ge(z_abs, c + 1)
            act_own.step(act, nc.scalar.activation(x, x, ACT.Exp, scale=-1.0))
            nc.scalar.activation(x, x, ACT.Ln, bias=1.0).then_inc(soft_ready, 1)

        def decays(act, c):
            n = TILES[c][1]
            act.wait_ge(bl_ready, c + 1)
            after(act, kt_done, c)
            for h in range(GH):
                last = nc.scalar.activation(k_decayed[:, h, 0:n], decay[:, h, 0:n], ACT.Exp,
                                            bias=chunk_sum(c)[:, h:h + 1], scale=-1 / TAU)
            last.then_inc(kdec_exp, 1)
            after(act, state_ready, c - 1)
            nc.scalar.activation(chunk_decay(c), chunk_sum(c), ACT.Exp).then_inc(ebl_ready, 1)

        def factors(act, c, g):
            act.wait_ge(arg_ready, 2 * (c - 1) + g + 1)
            nc.scalar.activation(ARGS[g][:], ARGS[g][:], ACT.Exp, scale=1 / TAU).then_inc(arg_exp, 1)

        def gla_scalar(act):
            for c, (c0, n) in enumerate(TILES):
                if 0 < c < NX:
                    copy_keys(act, c)
                    soft_parts(act, c + 1)
                    act.wait_ge(bl_ready, c + 2)
                    if c + 1 < NX:
                        decays(act, c + 1)
                if 0 < c < NX:
                    factors(act, c + 1, 0)
                if c < NX:
                    factors(act, c + 1, 1)
                if c > 0:
                    for h in range(2):
                        q = 2 * (c - 1) + h
                        act.wait_ge(r_tile, q + 1)
                        after(act, r_used, q - 1)
                        nc.scalar.activation(r_silu[h][:], PS[:, 1 + h, 0:GV], ACT.Silu).then_inc(r_left, 1)
                    act.wait_ge(o_done, c)
                    for h in range(GH):
                        col = 4 * (c - 1) + h
                        act_own.step(act, nc.scalar.activation(o_junk[:], out_bank(4, h), ACT.Square, accum_out=SS_O[:, col:col + 1]))
                    if c < NX:
                        act.wait_ge(s_done, c + 1)
                    nc.scalar.copy(v_rows[:, c - 1, :], banks(4, 2)).then_inc(o_kept, 1)
                if c < NX:
                    nc.scalar.activation(q_decayed[:], decay[:], ACT.Exp, scale=1 / TAU).then_inc(qdec_exp, 1)

        def gate_early(dve, c):
            dve.wait_ge(o_kept, c)
            dve.wait_ge(r_left, 2 * c)
            for h in range(2):
                x = v_rows[:, c - 1, h * GV:(h + 1) * GV]
                nc.vector.tensor_tensor(x, x, r_silu[h][:], ALU.mult).then_inc(r_used, 1)

        def gla_vector(dve):
            dve.wait_ge(mask_ready, 2 + 2 * LEVELS)

            def sums(c):
                n = TILES[c][1]
                dve.wait_ge(z_abs, c + 1)
                after(dve, kdec_ready, min(c, NX))
                after(dve, qdec_ready, c - 1)
                after(dve, arg_ready, 2 * (c - 1))
                nc.vector.tensor_scalar(decay[:, :, 0:n], logits(c), 0.0, None, ALU.min).then_inc(z_min, 1)
                dve.wait_ge(z_min, c + 1)
                dve.wait_ge(soft_ready, c + 1)
                for h in range(GH):
                    x = decay[:, h, 0:n]
                    nc.vector.tensor_tensor_scan(x, x, soft[:, h, 0:n], 0.0, ALU.add, ALU.subtract).then_inc(cum_done, 1)
                dve.wait_ge(cum_done, GH * (c + 1))
                after(dve, ebl_ready, c - 1)
                nc.vector.tensor_scalar(chunk_sum(c), decay[:, :, n - 1:n].rearrange("p h o -> p (h o)"), 1 / TAU, None, ALU.mult)\
                    .then_inc(bl_ready, 1)

            def exponents(c, g):
                if c == 1 and g == 1:
                    dve.wait_ge(unit_ready, U_GR + 2)
                after(dve, pair_done, 2 * (c - 2) + g + 1)
                for l in GROUPS[g]:
                    x, e = halves(decay[:], l), halves(level_arg(l), l)
                    b = 64 >> l
                    ref = x[:, :, 0, b - 1:b].broadcast_to([P, 4 * 64 // b, b])
                    nc.vector.tensor_tensor(e[:, :, 0, :], ref, x[:, :, 0, :], ALU.subtract)
                    last = nc.vector.tensor_tensor(e[:, :, 1, :], x[:, :, 1, :], ref, ALU.subtract)
                last.then_inc(arg_ready, 1)

            def weights(c, g):
                dve.wait_ge(pair_done, 2 * (c - 1) + g + 1)
                for l in GROUPS[g]:
                    b = 64 >> l
                    odd = head_blocks(att[:], l)[:, :, :, 1, :]
                    mask = pair_mask[:, l:l + 1, :].rearrange("p o (m b) -> p o m b", b=b).broadcast_to([P, GH, 64 // b, b])
                    ins = nc.vector.copy_predicated(odd, mask, pair_scores(l).rearrange("p h (m b) -> p h m b", b=b))
                    if l < LEVELS - 1 and l != 3:
                        dve_own.step(dve, ins)
                    else:
                        ins.then_inc(att_ready, 1)
                        dve.wait_ge(att_ready, 2 * (c - 1) + g + 1)

            sums(0)
            for c in range(len(TILES)):
                if c > 0:
                    dve.wait_ge(diag_done, c)
                    after(dve, o_done, c - 1)
                    nc.vector.tensor_tensor(att[:], PS[:, 3, :].rearrange("p (h t) -> p h t", h=GH),
                                            ident[:].rearrange("p (o t) -> p o t", o=1).broadcast_to([P, GH, P]), ALU.mult)\
                        .then_inc(diag_used, 1)
                    dve.wait_ge(diag_used, c)
                if c < NX:
                    sums(c + 1)
                for g in range(2):
                    if c > 0:
                        weights(c, g)
                    if c == 0 and g == 1:
                        dve.wait_ge(unit_ready, U_GR + 1)
                        dve.wait_ge(gv_tile, GH * NV_TILES)
                        split_unit_fast(dve, U_GR + 1, 1)
                    if c < NX:
                        exponents(c + 1, g)
                if c > 1:
                    gate_early(dve, c - 1)
                if c < NX:
                    dve.wait_ge(s_done, c + 1)
                    dve.wait_ge(ebl_ready, c + 1)
                    if c == 0:
                        nc.vector.tensor_copy(state[:].rearrange("p h e -> p (h e)"), banks(6, 2)).then_inc(state_ready, 1)
                    else:
                        dve.wait_ge(o_done, c)
                        for h in range(GH):
                            last = nc.vector.scalar_tensor_tensor(out=state[:, h, :], in0=state[:, h, :],
                                                                  scalar=chunk_decay(c)[:, h:h + 1], in1=out_bank(6, h),
                                                                  op0=ALU.mult, op1=ALU.add)
                        last.then_inc(state_ready, 1)

        def meta_keys(pool):
            pool.wait_ge(gqk_left, 2 + 8)
            pool.wait_ge(kdec_exp, 1)
            x = k_decayed[:, :, 0:META]
            nc.gpsimd.tensor_tensor(x, x, qk[:, GH:, 0:META], ALU.mult).then_inc(kdec_ready, 1)

        def gla_pool(pool):
            for c, (c0, n) in enumerate(TILES):
                q, k = qk[:, 0:GH, c0:c0 + n], qk[:, GH:, c0:c0 + n]
                if 0 < c < NX:
                    pool.wait_ge(kdec_exp, c + 1)
                    nc.gpsimd.tensor_tensor(k_decayed[:, :, 0:n], k_decayed[:, :, 0:n], k, ALU.mult).then_inc(kdec_ready, 1)
                if c == 0:
                    continue
                for g, group in enumerate(GROUPS):
                    pool.wait_ge(arg_exp, 2 * (c - 1) + g + 1)
                    for l in group:
                        e, ql, kl = head_blocks(level_arg(l), l), head_blocks(q, l), head_blocks(k, l)
                        nc.gpsimd.tensor_tensor(e[:, :, :, 0, :], e[:, :, :, 0, :], kl[:, :, :, 0, :], ALU.mult)
                        last = nc.gpsimd.tensor_tensor(e[:, :, :, 1, :], e[:, :, :, 1, :], ql[:, :, :, 1, :], ALU.mult)
                    last.then_inc(arg_mul, 1)
                pool.wait_ge(qdec_exp, c)
                nc.gpsimd.tensor_tensor(q_decayed[:], q_decayed[:], q, ALU.mult).then_inc(qdec_ready, 1)

        rstd_own, early_ready, gla_ready = sem("rstd_own"), sem("early_ready"), sem("gla_ready")
        BETWEEN = {0: [(U_GO[0], GO_SLOTS[0])], 2: [(U_R[3], 1)], 4: [(U_GO[1], GO_SLOTS[1])],
                   6: [(U_GO[2], GO_SLOTS[2])], 9: [(U_GO[3], GO_SLOTS[3])]}

        def gla_gate_tensor(pe):
            pe.wait_ge(att_ready, 2 * NX)
            pe.wait_ge(k_rows_done, NX)
            pe.wait_ge(r_left, EARLY)
            for q in range(EARLY):
                slot, j = divmod(q, NX)
                if j == 0:
                    pe.wait_ge(unit_ready, U_R[2 + slot] + 1)
                if q >= 4:
                    pe.wait_ge(r_left, EARLY + q - 3)
                token_tile(slot, META + j * P, q % 4).then_inc(r_tile, 1)

        def gla_gate_scalar(act):
            act.wait_ge(o_kept, NX)
            nc.scalar.activation(SS_O, SS_O, ACT.Sqrt, scale=1 / GV, bias=RMS_EPS).then_inc(rstd_own, 1)
            act.wait_ge(pair_done, 2 * NX)
            act.wait_ge(qdec_ready, NX)
            act.wait_ge(unit_ready, U_R[2] + 1)
            act.wait_ge(r_used, EARLY)
            for q in range(EARLY):
                for unit in BETWEEN.get(q, ()):
                    act.wait_ge(r_tile, EARLY + (q - 1 if q else 0))
                    unit_high(act, *unit)
                act.wait_ge(r_tile, EARLY + q + 1)
                if q >= 2:
                    act.wait_ge(r_used, EARLY + q - 1)
                nc.scalar.activation(r_silu[q % 2][:], PS[:, q % 4, 0:GV], ACT.Silu).then_inc(r_left, 1)

        def gla_gate_vector(dve):
            dve.wait_ge(r_tile, EARLY)
            split_unit_fast(dve, U_R[2], 0)
            gate_early(dve, NX)
            dve.wait_ge(rstd_own, 1)
            dve_own.step(dve, nc.vector.reciprocal(SS_O, SS_O))
            dve.wait_ge(a2_in, 48)
            dve.wait_ge(r_used, EARLY)

            def normed(h, j, other):
                x, col = v_rows[:, j, h * GV:(h + 1) * GV], 4 * j + h
                return nc.vector.scalar_tensor_tensor(out=x, in0=x, scalar=SS_O[:, col:col + 1], in1=other, op0=ALU.mult, op1=ALU.mult)

            for q in range(EARLY):
                h, j = divmod(q, NX)
                normed(h, j, norm_bc[:]).then_inc(early_ready, 1)
            for q in range(EARLY):
                h, j = divmod(q, NX)
                dve.wait_ge(r_left, EARLY + q + 1)
                normed(2 + h, j, r_silu[q % 2][:]).then_inc(r_used, 1)

        def gla_gate_pool(pool):
            pool.wait_ge(a2_in, 48)
            for q in range(EARLY):
                h, j = divmod(q, NX)
                for unit in BETWEEN.get(q, ()):
                    unit_low(pool, *unit)
                pool.wait_ge(r_used, EARLY + q + 1)
                x = v_rows[:, j, (2 + h) * GV:(3 + h) * GV]
                nc.gpsimd.tensor_tensor(x, x, norm_bc[:], ALU.mult).then_inc(gla_ready, 1)

        in6_tile = sem("in6_tile")
        gla_turned, gla_hi, gla_lo, h2_done, h2_std, n5_done = (
            sem(s) for s in ("gla_turned", "gla_hi", "gla_lo", "h2_done", "h2_std", "n5_done"))

        def normed5(j):
            return v_rows[:, 1 + j % 2, :]

        def gla_out_sync(sp):
            sp.wait_ge(pair_done, 2 * NX)
            load_unit(sp, U_GR + 2)
            sp.wait_ge(qdec_ready, NX)
            for u in range(U_GR + 3, U_AQK):
                load_unit(sp, u)
            sp.wait_ge(unit_ready, U_AQK)
            for j in range(2):
                sp.dma_start(rows5[j][:], row_tile(h1_rows, j)).then_inc(rows_in[j], 16)
            sp.wait_ge(gla_ready, EARLY)
            sp.wait_ge(early_ready, EARLY)
            for s, vec in enumerate((I["post_ln_g"][1], I["post_ln_b"][1])):
                sp.dma_start(gain5[s][:], bcast_row(vec, D)).then_inc(gain_in, 16)
            sp.wait_ge(gla_turned, 1)
            sp.dma_start(gain5[2], bcast_row(I["g_mix_pre_2"][0], D)).then_inc(gain_in, 16)
            load_unit(sp, U_AQK)
            load_unit(sp, U_AQK + 1)
            for j in range(NX):
                s = j % 2
                sp.wait_ge(h2_done, j + 1)
                sp.dma_start(row_tile(h2_rows, j), rows5[s][:]).then_inc(rows_out[s], 16)
                if j + 2 < NX:
                    sp.wait_ge(rows_out[s], H2_OUT[s] + 16 * (j // 2 + 1))
                    sp.wait_ge(n5_done, j + 1)
                    sp.dma_start(rows5[s][:], row_tile(h1_rows, j + 2)).then_inc(rows_in[s], 16)
            for s in range(2):
                sp.wait_ge(rows_out[s], H2_OUT[s] + 64)

        def gla_out_tensor(pe):
            def turn_gla(j):
                pe.wait_ge(gla_ready, NX + j + 1)
                after(pe, gla_lo, j)
                turn_row(v_rows[:, j, :], P, 4).then_inc(gla_turned, 1)

            def turn(j):
                pe.wait_ge(n5_done, j + 1)
                after(pe, part_lo, j, N5)
                turn_row(normed5(j), P, 6).then_inc(turned, 1)

            pe.wait_ge(early_ready, EARLY)
            pe.wait_ge(r_left, 2 * EARLY)
            turn_gla(0)
            pe.wait_ge(unit_ready, U_GO[3] + 1)
            pe.wait_ge(gla_hi, 1)
            dense_stage(lambda k: xh[:, k, 0:P], lambda k: of_slots(GO_SLOTS, k)[0], 0, first=True)
            dense_stage(lambda k: xh[:, k, 0:P], lambda k: of_slots(GO_SLOTS, k)[1], 0)
            turn_gla(1)
            pe.wait_ge(gla_lo, 1)
            dense_stage(lambda k: xl[:, k, 0:P], lambda k: of_slots(GO_SLOTS, k)[0], 0, last=True).then_inc(dense_done, 1)
            for j in range(1, NX):
                if j + 1 < NX:
                    turn_gla(j + 1)
                pe.wait_ge(gla_lo, j + 1)
                after(pe, dense_left, j - 1, Y5)
                cols = slice(j * P, (j + 1) * P)
                dense_split(lambda k: (xh[:, k, cols], xl[:, k, cols]), lambda k: of_slots(GO_SLOTS, k), 2 * (j % 2)).then_inc(dense_done, 1)
                if j >= 2:
                    turn(j - 2)

            part = lambda t, c: channel_part(wh[1], wl[1], t, CHUNKS2, c, 2 * t)
            pe.wait_ge(unit_ready, U_AQK + 1)
            pe.wait_ge(part_lo, N5 + 4)
            pe.wait_ge(dense_left, Y5 + 7)
            part(0, 0)
            turn(NX - 2)
            pe.wait_ge(dense_left, Y5 + 8)
            part(1, 0)
            turn(NX - 1)
            pe.wait_ge(part_lo, N5 + NX)
            part(0, 1).then_inc(in6_tile, 1)
            part(1, 1).then_inc(in6_tile, 1)

        def gla_out_scalar(act):
            def high(j):
                act.wait_ge(turned, N5 + j + 1)
                nc.scalar.copy(xh[:, :, j * P:(j + 1) * P], blocks(6)).then_inc(part_hi, 1)

            def gla_high(j):
                act.wait_ge(gla_turned, j + 1)
                nc.scalar.copy(xh[:, :, j * P:(j + 1) * P], blocks(4)).then_inc(gla_hi, 1)

            gla_high(0)
            for j in range(NX):
                if j + 1 < NX:
                    gla_high(j + 1)
                act.wait_ge(row_var, Y5 + j + 1)
                nc.scalar.activation(STD, VAR, ACT.Sqrt, bias=LN_EPS).then_inc(row_std, 1)
                act.wait_ge(h2_done, j + 1)
                act.wait_ge(gla_turned, 2 + j % 2)
                after(act, turned, j - 1, N5)
                act_own.step(act, nc.scalar.activation(normed5(j), rows5[j % 2][:], ACT.Square, accum_out=stat[:, 16:17]))
                nc.scalar.activation(stat[:, 17:18], stat[:, 16:17], ACT.Sqrt, scale=1 / D, bias=RMS_EPS).then_inc(h2_std, 1)
                if j >= 2:
                    high(j - 2)
            high(NX - 2)
            high(NX - 1)

        def gla_out_vector(dve):
            def low(j):
                cols = slice(j * P, (j + 1) * P)
                dve.wait_ge(part_hi, N5 + j + 1)
                nc.vector.tensor_tensor(xl[:, :, cols], blocks(6), xh[:, :, cols].bitcast(F32), ALU.subtract).then_inc(part_lo, 1)

            def gla_low(j):
                cols = slice(j * P, (j + 1) * P)
                dve.wait_ge(gla_hi, j + 1)
                nc.vector.tensor_tensor(xl[:, :, cols], blocks(4), xh[:, :, cols].bitcast(F32), ALU.subtract).then_inc(gla_lo, 1)

            gla_low(0)
            dve.wait_ge(gain_in, G5 + 48)
            for j in range(NX):
                x = rows5[j % 2]
                if j + 1 < NX:
                    gla_low(j + 1)
                dve.wait_ge(rows_in[j % 2], ROWS5 + 16 * (j // 2 + 1))
                dve.wait_ge(dense_done, Y5 + j + 1)
                nc.vector.scalar_tensor_tensor(out=x[:], in0=x[:], scalar=ALPHA, in1=banks(2 * (j % 2), 2),
                                               op0=ALU.mult, op1=ALU.add).then_inc(dense_left, 1)
                dve.wait_ge(dense_left, Y5 + j + 1)
                layer_norm_rows(dve, x, P, Y5 + j + 1, gain5[0], gain5[1]).then_inc(h2_done, 1)
                if j >= 2:
                    low(j - 2)
                dve.wait_ge(h2_std, j + 1)
                dve_own.step(dve, nc.vector.reciprocal(stat[:, 18:19], stat[:, 17:18]))
                nc.vector.scalar_tensor_tensor(out=normed5(j), in0=x[:], scalar=stat[:, 18:19], in1=gain5[2],
                                               op0=ALU.mult, op1=ALU.mult).then_inc(n5_done, 1)
            low(NX - 2)
            low(NX - 1)

        def gla_out_pool(pool):
            pool.wait_ge(r_tile, 2 * EARLY)
            split_unit(pool, U_AQK, 1)
            pool.wait_ge(dense_done, Y5 + NX)
            split_unit(pool, U_AQK + 1, 0)

        (in6_left, v6_tile, v6_left) = (
            sem(s) for s in ("in6_left", "v6_tile", "v6_left"))
        (f_in, f_split, f_abs, f_soft_ready, f_cum_ready, cum_out, cum_in) = (
            sem(s) for s in ("f_in", "f_split", "f_abs", "f_soft_ready", "f_cum_ready", "cum_out", "cum_in"))
        count_ready = sem("count_ready")
        B_F = stat[0:AH, 76:77]
        N_QK = 8

        def attn_in_sync(sp):
            sp.dma_start(f_raw[:], I["w_in_2"][0][:, 3 * HALF:3 * HALF + AH].rearrange("(k p) n -> p k n", p=P)).then_inc(f_in, 16)
            sp.dma_start(B_F, I["b_forget_2"].rearrange("o h -> h o")).then_inc(f_in, 16)
            for u in range(U_AQK + 2, U_FFN):
                load_unit(sp, u)
                if u == U_AU + 1:
                    sp.wait_ge(f_cum_ready, 1)
                    sp.dma_start(cum_rows, f_cum[:]).then_inc(cum_out, 16)
                    sp.wait_ge(cum_out, 16)
                    sp.dma_start(cum_bc[:].rearrange("p h t -> p (h t)"), bcast_row(cum_rows.rearrange("h t -> (h t)"), AH * SEQ))\
                        .then_inc(cum_in, 16)

        def attn_sync(sp):
            sp.wait_ge(pool_ready, 4)
            for half, name in enumerate(("g_attn_grp_2", "g_pool_grp_2")):
                sp.dma_start(mix_gain[:, half * HALF:(half + 1) * HALF], bcast_row(I[name][0], HALF)).then_inc(gain_in, 16)
            sp.dma_start(pool_gain[:], bcast_row(I["pool_scale_2"][0], HALF)).then_inc(gain_in, 16)
            sp.dma_start(w_pool[:], I["w_pool_2"][0].rearrange("g c d -> c g d")).then_inc(gain_in, 16)

        def attn_in_pool(pool):
            own = Chain(f_split)
            pool.wait_ge(dense_done, Y5 + NX)
            own.step(pool, nc.gpsimd.memset(f_pad[:], 0.0))
            pool.wait_ge(f_in, 32)
            own.step(pool, nc.gpsimd.tensor_copy(f_pad[:, :, 0:AH], f_raw[:]))
            pool.wait_ge(n5_done, NX)
            own.step(pool, nc.gpsimd.tensor_copy(fh[:], f_pad[:]))
            own.step(pool, nc.gpsimd.tensor_tensor(fl[:], f_pad[:], fh[:].bitcast(F32), ALU.subtract))
            own.step(pool, nc.gpsimd.memset(causal[:], 0.0))
            own.step(pool, nc.gpsimd.affine_select(out=causal[:], in_=causal[:], compare_op=ALU.is_ge, fill=MASKED, base=0,
                                             pattern=[[-1, P]], channel_multiplier=1))
            for u in range(U_AQK + 2, U_FFN):
                before = u - 2
                pool.wait_ge(in6_tile, 2 * (before - U_AQK + 1) + (before >= U_AU))
                split_unit(pool, u, (u + 1) % 2)

        def attn_in_tensor(pe):
            for n in range(1, 4):
                pe.wait_ge(unit_ready, U_AQK + n + 1)
                for t in range(2):
                    pe.wait_ge(in6_left, 2 * n + t + 1)
                    slot = (n + 1) % 2
                    channel_tile(wh[slot], wl[slot], t, CHUNKS2, 2 * t).then_inc(in6_tile, 1)
            pe.wait_ge(f_split, 4)
            pe.wait_ge(in6_left, N_QK + 1)
            channel_tile(fh, fl, 0, CHUNKS2, 0).then_inc(in6_tile, 1)
            for slot in range(2):
                pe.wait_ge(unit_ready, U_AU + slot + 1)
                for t in range(2):
                    q = N_QK + 1 + 2 * slot + t
                    pe.wait_ge(in6_left, q + 1)
                    channel_tile(wh[1 - slot], wl[1 - slot], t, CHUNKS2, 2 * (q % 2)).then_inc(in6_tile, 1)
            for slot in range(2):
                pe.wait_ge(unit_ready, U_AV + slot + 1)
                for j in range(NX):
                    q = slot * NX + j
                    pe.wait_ge(v6_left, q + 1)
                    token_tile(1 - slot, j * P, 4 + j % 4).then_inc(v6_tile, 1)

        def attn_in_scalar(act):
            act.wait_ge(dense_done, Y5 + NX)
            for i in range(N_QK):
                act.wait_ge(in6_tile, i + 1)
                nc.scalar.activation(aqk[:, i, :], banks(2 * (i % 2), 2), ACT.Copy, scale=-AD ** -0.5 if i < 4 else 1.0)\
                    .then_inc(in6_left, 1)
            act.wait_ge(f_in, 32)
            act.wait_ge(in6_tile, N_QK + 1)
            nc.scalar.activation(f_soft[:], banks(0, 2)[0:AH, :], ACT.Abs, bias=B_F).then_inc(f_abs, 1)
            act.wait_ge(f_abs, 1)
            act_own.step(act, nc.scalar.activation(f_soft[:], f_soft[:], ACT.Exp, scale=-1.0))
            nc.scalar.activation(f_soft[:], f_soft[:], ACT.Ln, bias=1.0).then_inc(f_soft_ready, 1)
            act.wait_ge(in6_left, 2 + N_QK + 1)
            for g in range(4):
                q = N_QK + 1 + g
                act.wait_ge(in6_tile, q + 1)
                nc.scalar.copy(pool_u[:, g, :], banks(2 * (q % 2), 2)).then_inc(in6_left, 1)
            act.wait_ge(unit_ready, U_FFN)
            for q in range(2 * NX):
                half, j = divmod(q, NX)
                act.wait_ge(v6_tile, q + 1)
                nc.scalar.copy(v6[:, j, half * UNIT:(half + 1) * UNIT], PS[:, 4 + j % 4, 0:UNIT]).then_inc(v6_left, 1)

        def attn_in_vector(dve):
            nc.vector.memset(stat[:, 90:91], 0.0).then_inc(in6_left, 2)
            nc.vector.memset(stat[:, 91:92], 0.0).then_inc(v6_left, 4)
            for t in range(16):
                nc.vector.memset(inv_count[:, t:t + 1], 1.0 / (t + 1)).then_inc(count_ready, 1)
            dve.wait_ge(f_abs, 1)
            dve_own.step(dve, nc.vector.tensor_scalar(f_logit[:], banks(0, 2)[0:AH, :], B_F, 0.0, ALU.add, ALU.min))
            nc.vector.memset(stat[:, 89:90], 0.0).then_inc(in6_left, 1)
            dve.wait_ge(f_soft_ready, 1)
            nc.vector.tensor_tensor_scan(f_cum[:], f_logit[:], f_soft[:], 0.0, ALU.add, ALU.subtract).then_inc(f_cum_ready, 1)

        pool_ready = sem("pool_ready")
        (score_done, score_ready, prob_ready, prob_turned, prob_left, pv_done) = (
            sem(s) for s in ("score_done", "score_ready", "prob_ready", "prob_turned", "prob_left", "pv_done"))
        (attn_left, pool_done, pool_left, mix_std, mix_done, mix_turned, mix_ready) = (
            sem(s) for s in ("attn_left", "pool_done", "pool_left", "mix_std", "mix_done", "mix_turned", "mix_ready"))
        STEPS = NX * AH

        def step(s):
            turn, h = divmod(s, AH)
            return NX - 1 - turn, turn, h

        def low_score(s):
            return stat[:, 56 + s % 3:57 + s % 3]

        def row_sums(turn):
            return stat[:, 60 + 8 * (turn % 2):68 + 8 * (turn % 2)]

        def tails(s, lag, work):
            turn, h = divmod(s - lag, AH)
            if h == AH - 1 and turn >= 0:
                work(turn)

        def attn_tensor(pe):
            pe.wait_ge(f_split, 4 + 2)
            pe.wait_ge(in6_left, N_QK + 7)
            pe.wait_ge(v6_left, 4 + 2 * NX)

            def scores(s):
                i, _, h = step(s)
                after(pe, score_ready, s - 1)
                rows = slice((h % 2) * AD, (h % 2 + 1) * AD)
                n, bank = (i + 1) * P, 2 * (s % 2)
                for c0 in range(0, n, 512):
                    cn = min(512, n - c0)
                    diag = c0 + cn == n
                    nc.tensor.matmul(PS[:, bank + c0 // 512, 0:cn], aqk[rows, h // 2, i * P:(i + 1) * P],
                                     aqk[rows, 4 + h // 2, c0:c0 + cn], start=True, stop=not diag)
                    if diag:
                        last = nc.tensor.matmul(PS[:, bank + c0 // 512, cn - P:cn], ident[:], causal[:], start=False, stop=True)
                last.then_inc(score_done, 1)

            def turn_probs(s):
                i, _, _ = step(s)
                pe.wait_ge(prob_ready, s + 1)
                after(pe, prob_left, s)
                after(pe, mix_ready, (s - 5) // AH)
                for kb in range(i + 1):
                    last = nc.tensor.transpose(blocks(4)[:, kb, :], score[s % 3][:, kb * P:(kb + 1) * P], ident[:])
                last.then_inc(prob_turned, 1)

            def values(s):
                i, turn, h = step(s)
                pe.wait_ge(prob_left, s + 1)
                if h == 0:
                    after(pe, attn_left, turn)
                for kb in range(i + 1):
                    last = nc.tensor.matmul(PS[:, 6, h * AD:(h + 1) * AD], prob_t[s % 2][:, kb * P:(kb + 1) * P],
                                            v6[:, kb, h * AD:(h + 1) * AD], start=kb == 0, stop=kb == i)
                last.then_inc(pv_done, 1)

            def pooled(turn):
                i = NX - 1 - turn
                if turn == 0:
                    pe.wait_ge(gain_in, G6 + 64)
                    pe.wait_ge(pool_ready, 4)
                after(pe, pool_left, turn)
                for g in range(4):
                    last = nc.tensor.matmul(PS[:, 7, g * P:(g + 1) * P], pool_u[:, g, i * P:(i + 1) * P], w_pool[:, g, :],
                                            start=True, stop=True)
                last.then_inc(pool_done, 1)

            def mixed(turn):
                pe.wait_ge(mix_done, turn + 1)
                pe.wait_ge(prob_left, min(turn * AH + 13, STEPS))
                turn_row(mix_row[turn % 2], P, 4).then_inc(mix_turned, 1)

            for s in range(STEPS + 3):
                if s < STEPS:
                    scores(s)
                if 2 <= s < STEPS + 2:
                    turn_probs(s - 2)
                if s >= 3:
                    values(s - 3)
                tails(s, 3, pooled)
                tails(s, 7, mixed)
            mixed(NX - 1)

        def attn_scalar(act):
            def probs(s):
                i, turn, h = step(s)
                act.wait_ge(score_ready, s + 1)
                x = score[s % 3][:, 0:(i + 1) * P]
                nc.scalar.activation(x, x, ACT.Exp, scale=-1.0, bias=low_score(s), accum_out=row_sums(turn)[:, h:h + 1])\
                    .then_inc(prob_ready, 1)

            def leave(s):
                i, _, _ = step(s)
                act.wait_ge(prob_turned, s + 1)
                after(act, pv_done, s - 1)
                nc.scalar.copy(prob_t[s % 2][:, 0:(i + 1) * P], banks(4, 2, (i + 1) * P)).then_inc(prob_left, 1)

            def squares(turn):
                act.wait_ge(attn_left, turn + 1)
                act.wait_ge(pool_left, turn + 1)
                after(act, mix_done, turn)
                for half in range(2):
                    act_own.step(act, nc.scalar.activation(mix_sq[:], mix_row[turn % 2][:, half * HALF:(half + 1) * HALF], ACT.Square,
                                                           accum_out=stat[:, 78 + half:79 + half]))
                nc.scalar.activation(stat[:, 80:82], stat[:, 78:80], ACT.Sqrt, scale=1 / HALF, bias=RMS_EPS).then_inc(mix_std, 1)

            def mixed(turn):
                i = NX - 1 - turn
                act.wait_ge(mix_turned, turn + 1)
                nc.scalar.copy(mix_t[:, :, i * P:(i + 1) * P], blocks(4)).then_inc(mix_ready, 1)

            for s in range(STEPS + 2):
                if s < STEPS:
                    probs(s)
                if s >= 2:
                    leave(s - 2)
                tails(s, 4, squares)
                tails(s, 7, mixed)
            squares(NX - 1)
            act.wait_ge(matrix_hi, 2)
            mo_high(act, nc.scalar.copy, 2)
            mo_high(act, nc.scalar.copy, 3)
            mixed(NX - 1)
            act.wait_ge(mix_ready, NX)
            act.wait_ge(score_ready, STEPS)
            for j in range(NX):
                mix_high(act, j)

        def attn_vector(dve):
            dve.wait_ge(cum_in, 16)

            def leave(turn):
                dve.wait_ge(pv_done, (turn + 1) * AH)
                dve.wait_ge(prob_ready, (turn + 1) * AH)
                after(dve, mix_turned, turn - 1)
                dve_own.step(dve, nc.vector.reciprocal(row_sums(turn), row_sums(turn)))
                a = mix_row[turn % 2][:, 0:HALF].rearrange("p (h d) -> p h d", h=AH)
                nc.vector.tensor_tensor(a, PS[:, 6, :].rearrange("p (h d) -> p h d", h=AH),
                                        row_sums(turn).rearrange("p (h o) -> p h o", o=1).broadcast_to([P, AH, AD]), ALU.mult)\
                    .then_inc(attn_left, 1)
                if turn == 0:
                    dve.wait_ge(gain_in, G6 + 64)
                dve.wait_ge(pool_done, turn + 1)
                nc.vector.tensor_tensor(mix_row[turn % 2][:, HALF:], PS[:, 7, :], pool_gain[:], ALU.mult).then_inc(pool_left, 1)

            def norm(turn):
                dve.wait_ge(mix_std, turn + 1)
                dve_own.step(dve, nc.vector.reciprocal(stat[:, 82:84], stat[:, 80:82]))
                for half in range(2):
                    x = mix_row[turn % 2][:, half * HALF:(half + 1) * HALF]
                    last = nc.vector.scalar_tensor_tensor(out=x, in0=x, scalar=stat[:, 82 + half:83 + half],
                                                          in1=mix_gain[:, half * HALF:(half + 1) * HALF], op0=ALU.mult, op1=ALU.mult)
                last.then_inc(mix_done, 1)

            for s in range(STEPS):
                i, _, h = step(s)
                n = (i + 1) * P
                dve.wait_ge(score_done, s + 1)
                after(dve, prob_turned, s - 2)
                nc.vector.tensor_tensor_reduce(score[s % 3][:, 0:n], cum_bc[:, h, 0:n], banks(2 * (s % 2), 2, n), 1.0, BIG,
                                               ALU.add, ALU.min, low_score(s)).then_inc(score_ready, 1)
                tails(s, 4, leave)
                tails(s, 5, norm)
            mo_high(dve, nc.vector.tensor_copy, 0)
            mo_high(dve, nc.vector.tensor_copy, 1)
            leave(NX - 1)
            norm(NX - 1)
            for q in range(4):
                mo_low(dve, q)

        def attn_pool(pool):
            own = pool_own
            pool.wait_ge(count_ready, 16)
            pool.wait_ge(in6_left, N_QK + 7)
            for g, w in enumerate((2, 4, 8, 16)):
                src, s = pool_u[:, g, :], 1
                for r in range(g + 1):
                    dst = pool_tmp[r % 2]
                    own.step(pool, nc.gpsimd.tensor_copy(dst[:, 0:s], src[:, 0:s]))
                    own.step(pool, nc.gpsimd.tensor_tensor(dst[:, s:], src[:, s:], src[:, 0:SEQ - s], ALU.add))
                    src, s = dst, 2 * s
                own.step(pool, nc.gpsimd.tensor_tensor(src[:, 0:w - 1], src[:, 0:w - 1], inv_count[:, 0:w - 1], ALU.mult))
                own.step(pool, nc.gpsimd.tensor_scalar(src[:, w - 1:], src[:, w - 1:], 1.0 / w, None, ALU.mult))
                nc.gpsimd.tensor_tensor(pool_u[:, g, :], src[:], pool_u[:, g, :], ALU.subtract).then_inc(pool_ready, 1)
                pool.wait_ge(pool_ready, g + 1)

        (mix_hi, mix_lo, ff_tile, y7_std, h3_done, h3_std, n7_done) = (
            sem(s) for s in ("mix_hi", "mix_lo", "ff_tile", "y7_std", "h3_done", "h3_std", "n7_done"))

        def mix_out_sync(sp):
            sp.wait_ge(v6_tile, 2 * NX)
            sp.dma_start(mo_raw[:], I["w_out_2"][0].rearrange("(k p) n -> p k n", p=P)).then_inc(matrix_in, 16)
            sp.wait_ge(mix_done, NX)
            for s, name in enumerate(("g_mix_post_2", "g_ffn_pre_2")):
                sp.dma_start(gain7[s][:], bcast_row(I[name][0], D)).then_inc(gain_in, 16)
            sp.wait_ge(mix_lo, NX)
            for s in range(2):
                sp.dma_start(rows7[s][:], row_tile(h2_rows, s)).then_inc(rows_in[s], 16)
            load_unit(sp, U_FFN)
            for j in range(NX):
                s = j % 2
                sp.wait_ge(h3_done, j + 1)
                sp.dma_start(row_tile(h3_rows, j), rows7[s][:]).then_inc(rows_out[s], 16)
                if j == 2:
                    load_unit(sp, U_FFN + 1)
                if j + 2 < NX:
                    sp.wait_ge(rows_out[s], H3_OUT[s] + 16 * (j // 2 + 1))
                    sp.wait_ge(n7_done, j + 1)
                    sp.dma_start(rows7[s][:], row_tile(h2_rows, j + 2)).then_inc(rows_in[s], 16)
            for s in range(2):
                sp.wait_ge(rows_out[s], H3_OUT[s] + 64)

        def mo_high(eng, copy, q):
            eng.wait_ge(matrix_in, 16)
            eng.wait_ge(score_done, STEPS)
            copy(mo_h[:, 2 * q:2 * q + 2, :], mo_raw[:, 2 * q:2 * q + 2, :]).then_inc(matrix_hi, 1)

        def mo_low(dve, q):
            dve.wait_ge(matrix_hi, q + 1)
            dve.wait_ge(pool_done, NX)
            dve.wait_ge(pv_done, STEPS)
            rows = slice(2 * q, 2 * q + 2)
            nc.vector.tensor_tensor(mo_l[:, rows, :], mo_raw[:, rows, :], mo_h[:, rows, :].bitcast(F32), ALU.subtract).then_inc(matrix_lo, 1)

        def mix_high(act, j):
            cols = slice(j * P, (j + 1) * P)
            nc.scalar.copy(xh7[:, :, cols], mix_t[:, :, cols]).then_inc(mix_hi, 1)

        def mix_out_tensor(pe):
            def turn(j):
                pe.wait_ge(n7_done, j + 1)
                after(pe, part_lo, j, N7)
                turn_row(normed7[j % 2], P, 6).then_inc(turned, 1)

            pe.wait_ge(score_ready, STEPS)
            pe.wait_ge(attn_left, NX)
            pe.wait_ge(pool_left, NX)
            pe.wait_ge(matrix_hi, 4)
            pe.wait_ge(mix_hi, 1)
            dense_stage(lambda k: xh7[:, k, 0:P], lambda k: mo_h[:, k, :], 0, first=True)
            pe.wait_ge(matrix_lo, 4)
            dense_stage(lambda k: xh7[:, k, 0:P], lambda k: mo_l[:, k, :], 0)
            pe.wait_ge(mix_lo, 1)
            dense_stage(lambda k: xl7[:, k, 0:P], lambda k: mo_h[:, k, :], 0, last=True).then_inc(dense_done, 1)
            for j in range(1, NX):
                pe.wait_ge(mix_lo, j + 1)
                after(pe, dense_left, j - 1, Y7)
                cols = slice(j * P, (j + 1) * P)
                dense_split(lambda k: (xh7[:, k, cols], xl7[:, k, cols]), lambda k: (mo_h[:, k, :], mo_l[:, k, :]), 2 * (j % 2))\
                    .then_inc(dense_done, 1)
                if j >= 2:
                    turn(j - 2)

            part = lambda t, c: channel_part(wh[0], wl[0], t, CHUNKS2, c, 2 * t, (xh7, xl7))
            pe.wait_ge(unit_ready, U_FFN + 1)
            pe.wait_ge(part_lo, N7 + 4)
            pe.wait_ge(dense_left, Y7 + 7)
            part(0, 0)
            turn(NX - 2)
            pe.wait_ge(dense_left, Y7 + 8)
            part(1, 0)
            turn(NX - 1)
            pe.wait_ge(part_lo, N7 + NX)
            part(0, 1).then_inc(ff_tile, 1)
            part(1, 1).then_inc(ff_tile, 1)

        def mix_out_scalar(act):
            def high(j):
                act.wait_ge(turned, N7 + j + 1)
                nc.scalar.copy(xh7[:, :, j * P:(j + 1) * P], blocks(6)).then_inc(part_hi, 1)

            for j in range(NX):
                act.wait_ge(dense_done, Y7 + j + 1)
                if j == 0:
                    act.wait_ge(mix_lo, NX)
                after(act, h3_done, j - 1)
                act_own.step(act, nc.scalar.activation(scaled7[j % 2][:], banks(2 * (j % 2), 2), ACT.Square, accum_out=stat[:, 0:1]))
                nc.scalar.activation(stat[:, 1:2], stat[:, 0:1], ACT.Sqrt, scale=1 / D, bias=RMS_EPS).then_inc(y7_std, 1)
                act.wait_ge(h3_done, j + 1)
                after(act, turned, j - 1, N7)
                act_own.step(act, nc.scalar.activation(normed7[j % 2][:], rows7[j % 2][:], ACT.Square, accum_out=stat[:, 16:17]))
                nc.scalar.activation(stat[:, 17:18], stat[:, 16:17], ACT.Sqrt, scale=1 / D, bias=RMS_EPS).then_inc(h3_std, 1)
                if j >= 2:
                    high(j - 2)
                if j in (1, 3):
                    act.wait_ge(matrix_lo, 4)
                    unit_high(act, U_FFN + j // 2, j // 2)
            high(NX - 2)
            high(NX - 1)

        def mix_out_vector(dve):
            dve.wait_ge(gain_in, G7 + 32)

            def low(j):
                cols = slice(j * P, (j + 1) * P)
                dve.wait_ge(part_hi, N7 + j + 1)
                nc.vector.tensor_tensor(xl7[:, :, cols], blocks(6), xh7[:, :, cols].bitcast(F32), ALU.subtract)\
                    .then_inc(part_lo, 1)

            for j in range(NX):
                dve.wait_ge(y7_std, j + 1)
                dve_own.step(dve, nc.vector.reciprocal(stat[:, 2:3], stat[:, 1:2]))
                nc.vector.scalar_tensor_tensor(out=scaled7[j % 2][:], in0=banks(2 * (j % 2), 2), scalar=stat[:, 2:3],
                                               in1=gain7[0][:], op0=ALU.mult, op1=ALU.mult).then_inc(dense_left, 1)
                dve.wait_ge(dense_left, Y7 + j + 1)
                x = rows7[j % 2]
                dve.wait_ge(rows_in[j % 2], ROWS7 + 16 * (j // 2 + 1))
                nc.vector.tensor_tensor(x[:], x[:], scaled7[j % 2][:], ALU.add).then_inc(h3_done, 1)
                if j >= 2:
                    low(j - 2)
                dve.wait_ge(h3_std, j + 1)
                dve_own.step(dve, nc.vector.reciprocal(stat[:, 18:19], stat[:, 17:18]))
                nc.vector.scalar_tensor_tensor(out=normed7[j % 2][:], in0=rows7[j % 2][:], scalar=stat[:, 18:19],
                                               in1=gain7[1][:], op0=ALU.mult, op1=ALU.mult).then_inc(n7_done, 1)
            low(NX - 2)
            low(NX - 1)

        def mix_out_pool(pool):
            pool.wait_ge(mix_turned, NX)
            for j in range(NX):
                cols = slice(j * P, (j + 1) * P)
                pool.wait_ge(mix_hi, j + 1)
                nc.gpsimd.tensor_tensor(xl7[:, :, cols], mix_t[:, :, cols], xh7[:, :, cols].bitcast(F32), ALU.subtract).then_inc(mix_lo, 1)
            for j in range(NX):
                if j in (1, 3):
                    unit_low(pool, U_FFN + j // 2, j // 2)

        (gate_left, up_left, ff_hi, ff_lo, dn_tile, dn_left, acc_zero) = (
            sem(s) for s in ("gate_left", "up_left", "ff_hi", "ff_lo", "dn_tile", "dn_left", "acc_zero"))
        HALVES = 2 * NX

        def ffn_sync(sp):
            sp.wait_ge(dense_done, Y7 + NX)
            for u in range(U_FFN + 2, U_END):
                load_unit(sp, u)

        def ffn_pool(pool):
            pool.wait_ge(dense_done, Y7 + NX)
            nc.gpsimd.memset(ff_acc[:], 0.0).then_inc(acc_zero, 1)
            for g in range(1, FGROUPS):
                pool.wait_ge(ff_tile, g * 4 - 2)
                split_unit(pool, u_gate(g), 0)
                pool.wait_ge(ff_tile, g * 4)
                split_unit(pool, u_gate(g) + 1, 1)
                after(pool, dn_tile, (g - 1) * HALVES)
                split_unit(pool, u_down(g - 1), 2)
            pool.wait_ge(ff_tile, 4 * FGROUPS)
            split_unit(pool, u_down(FGROUPS - 1), 0)
            for q in range(2, 4):
                ple_low(pool, nc.gpsimd, q).then_inc(matrix_lo, 1)

        def ffn_tensor(pe):
            def gate_up(g, gate_unit):
                x = (xh7, xl7)
                tile = lambda slot, t, bank: channel_tile(wh[slot], wl[slot], t, CHUNKS2, bank, x).then_inc(ff_tile, 1)
                first = isinstance(g, int)
                if not first:
                    pe.wait_ge(unit_ready, gate_unit + 1)
                    pe.wait_ge(up_left, g * 2)
                    tile(0, 0, 0)
                    pe.wait_ge(gate_left, g * 2)
                    tile(0, 1, 2)
                pe.wait_ge(unit_ready, gate_unit + 2)
                if not first:
                    pe.wait_ge(up_left, g * 2 - 1)
                tile(1, 0, 4)
                pe.wait_ge(gate_left, g * 2 + 1)
                tile(1, 1, 0)

            def down(g, b, down_unit, slot=2):
                pe.wait_ge(unit_ready, down_unit + 1)
                pe.wait_ge(ff_lo, g * 2 + 2)
                for j in range(NX):
                    cols = slice(j * P, (j + 1) * P)
                    for half in range(2):
                        pe.wait_ge(dn_left, g * HALVES + (2 * j + half + 1))
                        n = slice(half * HALF, (half + 1) * HALF)
                        products([(ffh[b][:, f, cols], ffl[b][:, f, cols], wh_rows[slot][:, f, n], wl_rows[slot][:, f, n]) for f in range(2)],
                                 [(0, HALF)], lambda c, cn: PS[:, 6 + half, :]).then_inc(dn_tile, 1)

            gate_up(0, u_gate(0))
            with pe.Fori(0, FGROUPS // 2) as i:
                gate_up(i * 2 + 1, i * 6 + u_gate(1))
                down(i * 2, 0, i * 6 + u_down(0))
                gate_up(i * 2 + 2, i * 6 + u_gate(2))
                down(i * 2 + 1, 1, i * 6 + u_down(1))
            turn_p(pe)
            down(FGROUPS - 1, 0, u_down(FGROUPS - 1), 0)

        def ffn_scalar(act):
            def group(g, b):
                for t in range(2):
                    act.wait_ge(ff_tile, g * 4 + t + 1)
                    nc.scalar.activation(ff_silu[:, t, :], banks(2 * t, 2), ACT.Silu).then_inc(gate_left, 1)
                for t in range(2):
                    act.wait_ge(up_left, g * 2 + t + 1)
                    nc.scalar.copy(ffh[b][:, t, :], ff_prod[t][:]).then_inc(ff_hi, 1)

            for s in range(2):
                act.wait_ge(rows_out[s], H3_OUT[s] + 64)
            group(0, 0)
            with act.Fori(0, FGROUPS // 2) as i:
                group(i * 2 + 1, 1)
                group(i * 2 + 2, 0)
            act.wait_ge(matrix_in, W9 + 16)
            for q in range(4):
                if q == 2:
                    act.wait_ge(dn_tile, (FGROUPS - 1) * HALVES)
                nc.scalar.copy(ple_h[:, 2 * q:2 * q + 2, :], ple_raw[:, 2 * q:2 * q + 2, :]).then_inc(matrix_hi, 1)

        def ple_low(eng, ops, q):
            eng.wait_ge(matrix_hi, M9 + q + 1)
            rows = slice(2 * q, 2 * q + 2)
            return ops.tensor_tensor(ple_l[:, rows, :], ple_raw[:, rows, :], ple_h[:, rows, :].bitcast(F32), ALU.subtract)

        def ffn_vector(dve):
            nc.vector.memset(stat[:, 88:89], 0.0).then_inc(dn_left, 2)

            def product(g, t):
                dve.wait_ge(ff_tile, g * 4 + t + 3)
                dve.wait_ge(gate_left, g * 2 + t + 1)
                if not isinstance(g, int):
                    dve.wait_ge(ff_lo, g * 2 + t - 1)
                nc.vector.tensor_tensor(ff_prod[t][:], ff_silu[:, t, :], banks(4 * (1 - t), 2), ALU.mult).then_inc(up_left, 1)

            def low(g, b, t):
                dve.wait_ge(ff_hi, g * 2 + t + 1)
                nc.vector.tensor_tensor(ffl[b][:, t, :], ff_prod[t][:], ffh[b][:, t, :].bitcast(F32), ALU.subtract).then_inc(ff_lo, 1)

            def add_down(g, first, last):
                for q in range(first, last):
                    j, half = divmod(q, 2)
                    dve.wait_ge(dn_tile, g * HALVES + q + 1)
                    x = ff_acc[:, j, half * HALF:(half + 1) * HALF]
                    nc.vector.tensor_tensor(x, x, PS[:, 6 + half, :], ALU.add).then_inc(dn_left, 1)

            def group(g, b, before):
                product(g, 0)
                low(g, b, 0)
                product(g, 1)
                add_down(before, 0, 3)
                low(g, b, 1)
                add_down(before, 3, HALVES)

            for t in range(2):
                product(0, t)
                low(0, 0, t)
            dve.wait_ge(acc_zero, 1)
            with dve.Fori(0, FGROUPS // 2) as i:
                group(i * 2 + 1, 1, i * 2)
                group(i * 2 + 2, 0, i * 2 + 1)
            for q in range(2):
                ple_low(dve, nc.vector, q).then_inc(matrix_lo, 1)
            add_down(FGROUPS - 1, 0, HALVES)

        p_in = sem("p_in")
        (p_turned, p_ready, ff_std, ff_n, h4_done, h4_turned, act9_hi, act9_lo) = (
            sem(s) for s in ("p_turned", "p_ready", "ff_std", "ff_n", "h4_done", "h4_turned", "act9_hi", "act9_lo"))
        (e_done, e_std, e_n, gated9, out_ready) = (
            sem(s) for s in ("e_done", "e_std", "e_n", "gated9", "out_ready"))

        def final_sync(sp):
            sp.wait_ge(ff_tile, 4 * FGROUPS)
            sp.wait_ge(up_left, 2 * FGROUPS)
            sp.dma_start(p_stage[:], I["p_2"][0, 0].rearrange("(j p) n -> p j n", p=P)).then_inc(p_in, 16)
            sp.dma_start(ple_raw[:], I["w_ple_gate_2"][0].rearrange("(k p) n -> p k n", p=P)).then_inc(matrix_in, 16)
            sp.wait_ge(unit_ready, U_END)
            sp.dma_start(w_ple_proj[:], I["w_ple_proj_2"][0].rearrange("(k p) n -> p k n", p=P)).then_inc(gain_in, 16)
            sp.wait_ge(dn_tile, (FGROUPS - 1) * HALVES)
            for s, name in enumerate(("g_ffn_post_2", "g_ple_2")):
                sp.dma_start(gain9[s][:], bcast_row(I[name][0], D)).then_inc(gain_in, 16)
            for s in range(2):
                sp.dma_start(rows9[s][:], row_tile(h3_rows, s)).then_inc(rows_in[s], 16)
            for j in range(NX):
                s = j % 2
                if j + 2 < NX:
                    sp.wait_ge(h4_done, j + 1)
                    sp.dma_start(rows9[s][:], row_tile(h3_rows, j + 2)).then_inc(rows_in[s], 16)
                sp.wait_ge(out_ready, j + 1)
                sp.dma_start(row_tile(out[0], j), out_row[s][:]).then_inc(rows_out[s], 16)
            for s in range(2):
                sp.wait_ge(rows_out[s], OUT[s] + 64)

        def turn_p(pe):
            pe.wait_ge(p_in, 16)
            pe.wait_ge(up_left, 2 * FGROUPS)
            pe.wait_ge(gate_left, 2 * FGROUPS)
            for k in range(2):
                for j in range(NX):
                    last = nc.tensor.transpose(PS[:, 2 * k + j // 4, (j % 4) * P:(j % 4 + 1) * P], p_stage[:, j, k * P:(k + 1) * P],
                                               ident[:])
            last.then_inc(p_turned, 1)

        def final_tensor(pe):
            def embed(j):
                after(pe, e_n, j)
                for k in range(2):
                    for half in range(2):
                        last = nc.tensor.matmul(PS[:, 6 + half, :], p_t[:, k, j * P:(j + 1) * P],
                                                w_ple_proj[:, k, half * HALF:(half + 1) * HALF], start=k == 0, stop=k == 1)
                last.then_inc(e_done, 1)

            def turn(j):
                pe.wait_ge(h4_done, j + 1)
                after(pe, act9_lo, j)
                turn_row(ff_acc[:, j, :], P, 4).then_inc(h4_turned, 1)

            pe.wait_ge(gain_in, G9 + 48)
            pe.wait_ge(p_ready, 1)
            pe.wait_ge(dn_left, 2 + FGROUPS * HALVES)
            embed(0)
            turn(0)
            pe.wait_ge(matrix_lo, M9 + 4)
            pe.wait_ge(act9_hi, 1)
            dense_stage(lambda k: act9h[0][:, k, :], lambda k: ple_h[:, k, :], 0, first=True)
            dense_stage(lambda k: act9h[0][:, k, :], lambda k: ple_l[:, k, :], 0)
            turn(1)
            pe.wait_ge(act9_lo, 1)
            dense_stage(lambda k: act9l[0][:, k, :], lambda k: ple_h[:, k, :], 0, last=True).then_inc(dense_done, 1)
            embed(1)
            for j in range(1, NX):
                if j + 1 < NX:
                    turn(j + 1)
                pe.wait_ge(act9_lo, j + 1)
                after(pe, dense_left, j - 1, Y9)
                s = j % 2
                dense_split(lambda k: (act9h[s][:, k, :], act9l[s][:, k, :]), lambda k: (ple_h[:, k, :], ple_l[:, k, :]), 2 * s)\
                    .then_inc(dense_done, 1)
                if j + 1 < NX:
                    embed(j + 1)

        def final_scalar(act):
            act.wait_ge(p_turned, 1)
            act.wait_ge(ff_lo, 2 * FGROUPS)
            nc.scalar.copy(p_t[:].rearrange("p k t -> p (k t)"), banks(0, 4)).then_inc(p_ready, 1)
            act.wait_ge(matrix_lo, M9 + 4)

            def ff_norm(j):
                act.wait_ge(dn_left, 2 + (FGROUPS - 1) * HALVES + 2 * j + 2)
                after(act, ff_n, j)
                act_own.step(act, nc.scalar.activation(sq9[:], ff_acc[:, j, :], ACT.Square, accum_out=stat[:, 0:1]))
                nc.scalar.activation(stat[:, 1:2], stat[:, 0:1], ACT.Sqrt, scale=1 / D, bias=RMS_EPS).then_inc(ff_std, 1)

            def high(j):
                act.wait_ge(h4_turned, j + 1)
                after(act, dense_done, j - 1, Y9)
                nc.scalar.copy(act9h[j % 2][:], blocks(4)).then_inc(act9_hi, 1)

            def embed_norm(j):
                act.wait_ge(e_done, j + 1)
                act_own.step(act, nc.scalar.activation(sq9e[:], banks(6, 2), ACT.Square, accum_out=stat[:, 3:4]))
                after(act, e_n, j)
                nc.scalar.activation(stat[:, 4:5], stat[:, 3:4], ACT.Sqrt, scale=1 / D, bias=RMS_EPS).then_inc(e_std, 1)

            ff_norm(0)
            embed_norm(0)
            ff_norm(1)
            high(0)
            for j in range(NX):
                if j + 2 < NX:
                    ff_norm(j + 2)
                if j + 1 < NX:
                    high(j + 1)
                act.wait_ge(dense_done, Y9 + j + 1)
                after(act, rows_out[j % 2], 16 * (j // 2), OUT[j % 2])
                nc.scalar.activation(out_row[j % 2][:], banks(2 * (j % 2), 2), ACT.Sigmoid).then_inc(dense_left, 1)
                if j + 1 < NX:
                    embed_norm(j + 1)

        def final_vector(dve):
            dve.wait_ge(gain_in, G9 + 48)

            def ff_norm(j):
                dve.wait_ge(ff_std, j + 1)
                dve_own.step(dve, nc.vector.reciprocal(stat[:, 2:3], stat[:, 1:2]))
                x = ff_acc[:, j, :]
                nc.vector.scalar_tensor_tensor(out=x, in0=x, scalar=stat[:, 2:3], in1=gain9[0][:], op0=ALU.mult, op1=ALU.mult)\
                    .then_inc(ff_n, 1)
                dve.wait_ge(ff_n, j + 1)
                dve.wait_ge(rows_in[j % 2], ROWS9 + 16 * (j // 2 + 1))
                nc.vector.tensor_tensor(x, x, rows9[j % 2][:], ALU.add).then_inc(h4_done, 1)

            def embed_norm(j):
                dve.wait_ge(e_std, j + 1)
                after(dve, gated9, j)
                dve_own.step(dve, nc.vector.reciprocal(stat[:, 5:6], stat[:, 4:5]))
                nc.vector.scalar_tensor_tensor(out=e_row[:], in0=banks(6, 2), scalar=stat[:, 5:6], in1=gain9[1][:],
                                               op0=ALU.mult, op1=ALU.mult).then_inc(e_n, 1)

            def low(j):
                dve.wait_ge(act9_hi, j + 1)
                nc.vector.tensor_tensor(act9l[j % 2][:], blocks(4), act9h[j % 2][:].bitcast(F32), ALU.subtract).then_inc(act9_lo, 1)

            ff_norm(0)
            embed_norm(0)
            ff_norm(1)
            low(0)
            for j in range(NX):
                if j + 2 < NX:
                    ff_norm(j + 2)
                if j + 1 < NX:
                    low(j + 1)
                dve.wait_ge(e_n, j + 1)
                dve.wait_ge(dense_left, Y9 + j + 1)
                nc.vector.tensor_tensor(out_row[j % 2][:], out_row[j % 2][:], e_row[:], ALU.mult).then_inc(gated9, 1)
                dve.wait_ge(gated9, j + 1)
                dve.wait_ge(h4_done, j + 1)
                nc.vector.tensor_tensor(out_row[j % 2][:], out_row[j % 2][:], ff_acc[:, j, :], ALU.add).then_inc(out_ready, 1)
                if j + 1 < NX:
                    embed_norm(j + 1)


        block = ctx.enter_context(nc.Block())

        @block.sync
        def _(sp):
            inputs_sync(sp)
            conv_in_sync(sp)
            conv_out_sync(sp)
            gla_in_sync(sp)
            gla_out_sync(sp)
            attn_in_sync(sp)
            attn_sync(sp)
            mix_out_sync(sp)
            ffn_sync(sp)
            final_sync(sp)

        @block.tensor
        def _(pe):
            inputs_tensor(pe)
            conv_in_tensor(pe)
            conv_norm_tensor(pe)
            conv_out_tensor(pe)
            gla_in_tensor(pe)
            gla_tensor(pe)
            gla_gate_tensor(pe)
            gla_out_tensor(pe)
            attn_in_tensor(pe)
            attn_tensor(pe)
            mix_out_tensor(pe)
            ffn_tensor(pe)
            final_tensor(pe)

        @block.scalar
        def _(act):
            inputs_scalar(act)
            conv_in_scalar(act)
            conv_norm_scalar(act)
            conv_out_scalar(act)
            gla_in_scalar(act)
            gla_scalar(act)
            gla_gate_scalar(act)
            gla_out_scalar(act)
            attn_in_scalar(act)
            attn_scalar(act)
            mix_out_scalar(act)
            ffn_scalar(act)
            final_scalar(act)

        @block.vector
        def _(dve):
            inputs_vector(dve)
            conv_vector(dve)
            conv_norm_vector(dve)
            conv_out_vector(dve)
            gla_in_vector(dve)
            gla_vector(dve)
            gla_gate_vector(dve)
            gla_out_vector(dve)
            attn_in_vector(dve)
            attn_vector(dve)
            mix_out_vector(dve)
            ffn_vector(dve)
            final_vector(dve)

        @block.gpsimd
        def _(pool):
            consts_pool(pool)
            conv_in_pool(pool)
            conv_norm_pool(pool)
            conv_out_pool(pool)
            gla_in_pool(pool)
            gla_pool(pool)
            gla_gate_pool(pool)
            gla_out_pool(pool)
            attn_in_pool(pool)
            attn_pool(pool)
            mix_out_pool(pool)
            ffn_pool(pool)


_INS = ['x', 'meta', 'conv_w_in', 'conv_b_in', 'conv_w_dw', 'conv_b_dw', 'conv_norm_g', 'conv_norm_b', 'conv_w_out',
        'conv_b_out', 'gla_w_in', 'gla_w_a2', 'gla_b_a', 'gla_norm_g', 'gla_w_out', 'post_ln_g', 'post_ln_b', 'p_2',
        'g_mix_pre_2', 'w_in_2', 'b_forget_2', 'g_attn_grp_2', 'g_pool_grp_2', 'w_pool_2', 'pool_scale_2', 'w_out_2',
        'g_mix_post_2', 'g_ffn_pre_2', 'w_ffn_gate_2', 'w_ffn_up_2', 'w_ffn_down_2', 'g_ffn_post_2', 'w_ple_proj_2',
        'g_ple_2', 'w_ple_gate_2']


def kernel(**inputs):
    import numpy as _np
    import concourse.bacc as _bacc
    from concourse import mybir as _mybir
    from concourse.bass_utils import run_bass_kernel_spmd as _run

    nc = _bacc.Bacc("TRN2", target_bir_lowering=False, num_devices=1)
    arrays, aps = {}, {}
    for name in _INS:
        a = _np.ascontiguousarray(inputs[name])
        arrays[f"in_{name}_dram"] = a
        aps[name] = nc.dram_tensor(f"in_{name}_dram", a.shape, _mybir.dt.from_np(a.dtype), kind="ExternalInput").ap()
    out = nc.dram_tensor("out_0_dram", (1, SEQ, D), F32, kind="ExternalOutput").ap()
    hybrid_block(nc, aps, out)
    r = _run(nc, [arrays], core_ids=[0])
    return r.results[0]["out_0_dram"]
```
